# Optimizing a Trainium2 kernel written in Bass

```python
import math
import jax, jax.numpy as jnp
from jax import lax
import numpy as np

D_MODEL = 1024
BATCH = 1
SEQ = 512
DEPTH = 1

HEAD_DIM = 64
NSA_HEADS = 8
NSA_KV_GROUPS = 2
NSA_REP = NSA_HEADS // NSA_KV_GROUPS
SB_HEADS = 8
CMP_BLOCK = 32
CMP_STRIDE = 16
CMP_HIDDEN = 2 * HEAD_DIM
SEL_BLOCK = 64
SEL_TOPK = 8
WINDOW = 512
Q_BLOCK = 128
SEL_Q_CHUNK = 64
D_FF = -(-8 * D_MODEL // (3 * 256)) * 256
RMS_EPS = 1e-6
NEG_INF = -1e30
FORCE_PRIORITY = 1e4
ATTN_SCALE = 1.0 / math.sqrt(HEAD_DIM)

NSA_Q_DIM = NSA_HEADS * HEAD_DIM
NSA_KV_DIM = 6 * NSA_KV_GROUPS * HEAD_DIM
NSA_GATE_DIM = 3 * NSA_HEADS
SB_QKV_DIM = 3 * SB_HEADS * HEAD_DIM
MERGE_DIM = 2 * D_MODEL
D_IN = NSA_Q_DIM + NSA_KV_DIM + NSA_GATE_DIM + SB_QKV_DIM + MERGE_DIM
IN_SPLITS = (NSA_Q_DIM, NSA_Q_DIM + NSA_KV_DIM, NSA_Q_DIM + NSA_KV_DIM + NSA_GATE_DIM,
             NSA_Q_DIM + NSA_KV_DIM + NSA_GATE_DIM + SB_QKV_DIM)


def rmsnorm(x, g):
    xf = x.astype(jnp.float32)
    y = xf * lax.rsqrt(jnp.mean(xf * xf, axis=-1, keepdims=True) + RMS_EPS)
    return (y * g.astype(jnp.float32)).astype(x.dtype)

def modulate(h, shift, scale):
    return h * (1.0 + scale) + shift

def alibi_slopes():
    i = jnp.arange(1, NSA_HEADS + 1, dtype=jnp.float32)
    return jnp.exp2(-8.0 * i / NSA_HEADS).reshape(NSA_KV_GROUPS, NSA_REP)

def compress(k, pos_emb, w1, w2):
    n_cmp = (k.shape[2] - CMP_BLOCK) // CMP_STRIDE + 1
    idx = jnp.arange(n_cmp)[:, None] * CMP_STRIDE + jnp.arange(CMP_BLOCK)[None, :]
    blocks = k[:, :, idx] + pos_emb
    flat = blocks.reshape(*blocks.shape[:3], CMP_BLOCK * HEAD_DIM)
    return jax.nn.gelu(flat @ w1) @ w2

def nsa_compressed(q, kc, vc, slopes):
    S = q.shape[3]
    n = kc.shape[2]
    t = jnp.arange(S)
    end = jnp.arange(n) * CMP_STRIDE + CMP_BLOCK - 1
    dist = (t[:, None] - end[None, :]).astype(jnp.float32)
    valid = dist >= 0
    s = jnp.einsum('bgrqd,bgnd->bgrqn', q.astype(jnp.float32), kc.astype(jnp.float32)) * ATTN_SCALE
    s = s - slopes[:, :, None, None] * dist
    s = jnp.where(valid, s, NEG_INF)
    p = jax.nn.softmax(s, axis=-1)
    p = jnp.where(valid.any(-1)[:, None], p, 0.0)
    o = jnp.einsum('bgrqn,bgnd->bgrqd', p.astype(vc.dtype), vc)
    return o, p.sum(axis=2)

def nsa_select_indices(p_cmp, S):
    n_cmp = p_cmp.shape[-1]
    n_sel = S // SEL_BLOCK
    c_start = jnp.arange(n_cmp) * CMP_STRIDE
    c_end = c_start + CMP_BLOCK - 1
    s_start = jnp.arange(n_sel) * SEL_BLOCK
    s_end = s_start + SEL_BLOCK - 1
    overlap = ((c_start[:, None] <= s_end[None, :]) & (c_end[:, None] >= s_start[None, :])).astype(jnp.float32)
    p_slc = jnp.einsum('bgqn,nj->bgqj', p_cmp, overlap)
    cur = (jnp.arange(S) // SEL_BLOCK)[:, None]
    j = jnp.arange(n_sel)[None, :]
    valid = j <= cur
    forced = (j == 0) | (j == cur) | (j == cur - 1)
    prio = jnp.where(valid, p_slc, NEG_INF)
    prio = jnp.where(forced & valid, FORCE_PRIORITY, prio)
    _, idx = lax.top_k(prio, min(SEL_TOPK, n_sel))
    return idx

def nsa_selected(q, k, v, idx, slopes):
    B, G, R, S, hd = q.shape
    n = idx.shape[-1]
    kb = k.reshape(B, G, S // SEL_BLOCK, SEL_BLOCK, hd)
    vb = v.reshape(B, G, S // SEL_BLOCK, SEL_BLOCK, hd)
    nc = S // SEL_Q_CHUNK
    q_c = q.reshape(B, G, R, nc, SEL_Q_CHUNK, hd).transpose(3, 0, 1, 2, 4, 5)
    idx_c = idx.reshape(B, G, nc, SEL_Q_CHUNK, n).transpose(2, 0, 1, 3, 4)
    t_c = jnp.arange(S).reshape(nc, SEL_Q_CHUNK)
    bi = jnp.arange(B)[:, None, None, None]
    gi = jnp.arange(G)[None, :, None, None]

    def chunk(args):
        qq, ii, tt = args
        ks = kb[bi, gi, ii]
        vs = vb[bi, gi, ii]
        pos = ii[..., None] * SEL_BLOCK + jnp.arange(SEL_BLOCK)
        dist = (tt[:, None, None] - pos).astype(jnp.float32)
        s = jnp.einsum('bgrqd,bgqnld->bgrqnl', qq.astype(jnp.float32), ks.astype(jnp.float32)) * ATTN_SCALE
        s = s - slopes[:, :, None, None, None] * dist[:, :, None]
        s = jnp.where((dist >= 0)[:, :, None], s, NEG_INF)
        p = jax.nn.softmax(s, axis=(-2, -1))
        return jnp.einsum('bgrqnl,bgqnld->bgrqd', p.astype(v.dtype), vs)

    o = lax.map(chunk, (q_c, idx_c, t_c))
    return o.transpose(1, 2, 3, 0, 4, 5).reshape(B, G, R, S, hd)

def nsa_window(q, k, v, slopes):
    B, G, R, S, hd = q.shape
    kp = jnp.pad(k, ((0, 0), (0, 0), (WINDOW, 0), (0, 0)))
    vp = jnp.pad(v, ((0, 0), (0, 0), (WINDOW, 0), (0, 0)))
    nq = S // Q_BLOCK
    q_c = q.reshape(B, G, R, nq, Q_BLOCK, hd).transpose(3, 0, 1, 2, 4, 5)
    starts = jnp.arange(nq) * Q_BLOCK
    span = WINDOW + Q_BLOCK

    def blk(args):
        qq, q0 = args
        kk = lax.dynamic_slice_in_dim(kp, q0, span, axis=2)
        vv = lax.dynamic_slice_in_dim(vp, q0, span, axis=2)
        t = q0 + jnp.arange(Q_BLOCK)
        s_pos = q0 - WINDOW + jnp.arange(span)
        dist = t[:, None] - s_pos[None, :]
        mask = (dist >= 0) & (dist < WINDOW) & (s_pos[None, :] >= 0)
        s = jnp.einsum('bgrqd,bgkd->bgrqk', qq.astype(jnp.float32), kk.astype(jnp.float32)) * ATTN_SCALE
        s = s - slopes[:, :, None, None] * dist.astype(jnp.float32)
        s = jnp.where(mask, s, NEG_INF)
        p = jax.nn.softmax(s, axis=-1)
        return jnp.einsum('bgrqk,bgkd->bgrqd', p.astype(v.dtype), vv)

    o = lax.map(blk, (q_c, starts))
    return o.transpose(1, 2, 3, 0, 4, 5).reshape(B, G, R, S, hd)

def stick_breaking(q, k, v):
    B, H, S, hd = q.shape
    nq = S // Q_BLOCK
    q_c = q.reshape(B, H, nq, Q_BLOCK, hd).transpose(2, 0, 1, 3, 4)
    starts = jnp.arange(nq) * Q_BLOCK
    kf = k.astype(jnp.float32)
    s_pos = jnp.arange(S)

    def blk(args):
        qq, q0 = args
        t = q0 + jnp.arange(Q_BLOCK)
        mask = s_pos[None, :] < t[:, None]
        z = jnp.einsum('bhqd,bhkd->bhqk', qq.astype(jnp.float32), kf) * ATTN_SCALE
        log_keep = jnp.where(mask, -jax.nn.softplus(z), 0.0)
        later = lax.cumsum(log_keep, axis=3, reverse=True) - log_keep
        a = jnp.where(mask, jnp.exp(jax.nn.log_sigmoid(z) + later), 0.0)
        return jnp.einsum('bhqk,bhkd->bhqd', a.astype(v.dtype), v)

    o = lax.map(blk, (q_c, starts))
    return o.transpose(1, 2, 0, 3, 4).reshape(B, H, S, hd)

def hybrid_mixer(h, w_in, cmp_pos_k, cmp_w1_k, cmp_w2_k, cmp_pos_v, cmp_w1_v, cmp_w2_v,
                 w_proj_a, w_proj_b, w_out):
    B, S, _ = h.shape
    G, R, hd = NSA_KV_GROUPS, NSA_REP, HEAD_DIM
    proj = h @ w_in
    q_a, kv_a, gate_a, qkv_b, merge = jnp.split(proj, IN_SPLITS, axis=-1)

    q_a = q_a.reshape(B, S, G, R, hd).transpose(0, 2, 3, 1, 4)
    kv_a = kv_a.reshape(B, S, 6, G, hd).transpose(2, 0, 3, 1, 4)
    k_cmp, v_cmp, k_sel, v_sel, k_win, v_win = (kv_a[i] for i in range(6))
    g_a = jax.nn.sigmoid(gate_a.reshape(B, S, G, R, 3).transpose(0, 2, 3, 1, 4))
    slopes = alibi_slopes()
    kc = compress(k_cmp, cmp_pos_k, cmp_w1_k, cmp_w2_k)
    vc = compress(v_cmp, cmp_pos_v, cmp_w1_v, cmp_w2_v)
    o_cmp, p_cmp = nsa_compressed(q_a, kc, vc, slopes)
    idx = nsa_select_indices(p_cmp, S)
    o_sel = nsa_selected(q_a, k_sel, v_sel, idx, slopes)
    o_win = nsa_window(q_a, k_win, v_win, slopes)
    o_a = g_a[..., 0:1] * o_cmp + g_a[..., 1:2] * o_sel + g_a[..., 2:3] * o_win
    y_a = o_a.transpose(0, 3, 1, 2, 4).reshape(B, S, NSA_Q_DIM) @ w_proj_a

    qkv_b = qkv_b.reshape(B, S, 3, SB_HEADS, hd).transpose(2, 0, 3, 1, 4)
    o_b = stick_breaking(qkv_b[0], qkv_b[1], qkv_b[2])
    y_b = o_b.transpose(0, 2, 1, 3).reshape(B, S, SB_HEADS * hd) @ w_proj_b

    merge = merge.reshape(B, S, 2, D_MODEL)
    y = jax.nn.sigmoid(merge[:, :, 0]) * y_a + jax.nn.sigmoid(merge[:, :, 1]) * y_b
    return y @ w_out

def swiglu(h, w_gate, w_up, w_down):
    return (jax.nn.silu(h @ w_gate) * (h @ w_up)) @ w_down

def first_inputs(seed: int = 0) -> dict:
    key = jax.random.key(seed)
    ks = jax.random.split(key, 20)

    def dense(k, shape, fan_in):
        return jax.random.normal(k, shape, jnp.float32) * (fan_in ** -0.5)

    def gain(k, shape):
        return 1.0 + 0.05 * jax.random.normal(k, shape, jnp.float32)

    L = DEPTH
    cmp_in = CMP_BLOCK * HEAD_DIM
    return {
        "x": jax.random.normal(ks[0], (BATCH, SEQ, D_MODEL), jnp.float32),
        "c": jax.random.normal(ks[1], (BATCH, D_MODEL), jnp.float32),
        "w_ada": dense(ks[2], (L, D_MODEL, 6 * D_MODEL), D_MODEL),
        "b_ada": 0.02 * jax.random.normal(ks[3], (L, 6 * D_MODEL), jnp.float32),
        "norm_mix_g": gain(ks[4], (L, D_MODEL)),
        "w_in": dense(ks[5], (L, D_MODEL, D_IN), D_MODEL),
        "cmp_pos_k": 0.02 * jax.random.normal(ks[6], (L, CMP_BLOCK, HEAD_DIM), jnp.float32),
        "cmp_w1_k": dense(ks[7], (L, cmp_in, CMP_HIDDEN), cmp_in),
        "cmp_w2_k": dense(ks[8], (L, CMP_HIDDEN, HEAD_DIM), CMP_HIDDEN),
        "cmp_pos_v": 0.02 * jax.random.normal(ks[9], (L, CMP_BLOCK, HEAD_DIM), jnp.float32),
        "cmp_w1_v": dense(ks[10], (L, cmp_in, CMP_HIDDEN), cmp_in),
        "cmp_w2_v": dense(ks[11], (L, CMP_HIDDEN, HEAD_DIM), CMP_HIDDEN),
        "w_proj_a": dense(ks[12], (L, NSA_Q_DIM, D_MODEL), NSA_Q_DIM),
        "w_proj_b": dense(ks[13], (L, SB_HEADS * HEAD_DIM, D_MODEL), SB_HEADS * HEAD_DIM),
        "w_out": dense(ks[14], (L, D_MODEL, D_MODEL), D_MODEL),
        "norm_ffn_g": gain(ks[15], (L, D_MODEL)),
        "w_ffn_gate": dense(ks[16], (L, D_MODEL, D_FF), D_MODEL),
        "w_ffn_up": dense(ks[17], (L, D_MODEL, D_FF), D_MODEL),
        "w_ffn_down": dense(ks[18], (L, D_FF, D_MODEL), D_FF),
        "norm_final_g": gain(ks[19], (D_MODEL,)),
    }

def first_block(x, c, w_ada, b_ada, norm_mix_g, w_in, cmp_pos_k, cmp_w1_k, cmp_w2_k,
              cmp_pos_v, cmp_w1_v, cmp_w2_v, w_proj_a, w_proj_b, w_out, norm_ffn_g,
              w_ffn_gate, w_ffn_up, w_ffn_down, norm_final_g):
    for l in range(DEPTH):
        mod = jax.nn.silu(c) @ w_ada[l] + b_ada[l]
        sh1, sc1, g1, sh2, sc2, g2 = jnp.split(mod[:, None, :], 6, axis=-1)
        h = modulate(rmsnorm(x, norm_mix_g[l]), sh1, sc1)
        x = x + g1 * hybrid_mixer(h, w_in[l], cmp_pos_k[l], cmp_w1_k[l], cmp_w2_k[l],
                                  cmp_pos_v[l], cmp_w1_v[l], cmp_w2_v[l],
                                  w_proj_a[l], w_proj_b[l], w_out[l])
        h = modulate(rmsnorm(x, norm_ffn_g[l]), sh2, sc2)
        x = x + g2 * swiglu(h, w_ffn_gate[l], w_ffn_up[l], w_ffn_down[l])
    return rmsnorm(x, norm_final_g)


PLE_DIM = 256
EPS = 1e-6
GM_WIDTH = 512
GM_GROUPS = 8
GM_CHUNK = 128
HG_HEADS = 4
HG_KEY = 128
HG_VAL = 128
HG_CHUNK = 64
HG_KW = HG_HEADS * HG_KEY
HG_VW = HG_HEADS * HG_VAL
IN_SPLITS_2 = [GM_WIDTH, GM_WIDTH, HG_KW, HG_KW, HG_VW, HG_VW, D_MODEL, D_MODEL]
IN_COLS = sum(IN_SPLITS_2)
N_GROUPS = 4
EXP_PER_GROUP = 8
N_EXPERTS = N_GROUPS * EXP_PER_GROUP
TOP_K = 2
D_EXPERT = 512
MOE_BLOCK = 128


def rmsnorm_2(x, g):
    xf = x.astype(jnp.float32)
    y = xf * lax.rsqrt(jnp.mean(xf * xf, axis=-1, keepdims=True) + EPS)
    return y.astype(x.dtype) * g

def layernorm(x, g, b):
    xf = x.astype(jnp.float32)
    mu = jnp.mean(xf, axis=-1, keepdims=True)
    var = jnp.mean(jnp.square(xf - mu), axis=-1, keepdims=True)
    y = (xf - mu) * lax.rsqrt(var + EPS)
    return y.astype(x.dtype) * g + b

def gmlp_branch(u, v, ln_g, ln_b, w_sp, b_sp):
    B, S, _ = u.shape
    n_c = S // GM_CHUNK
    dg = GM_WIDTH // GM_GROUPS
    v = layernorm(v, ln_g, ln_b).reshape(B, n_c, GM_CHUNK, GM_GROUPS, dg)
    mask = jnp.tril(jnp.ones((GM_CHUNK, GM_CHUNK), dtype=bool))
    w = jnp.where(mask[None], w_sp, jnp.zeros_like(w_sp))
    s = jnp.einsum('gts,bcsgd->bctgd', w, v) + b_sp.T[:, :, None]
    return u * s.reshape(B, S, GM_WIDTH)

def hgrn2_branch(q, f_raw, i_in, og, lb, norm_g):
    B, S, _ = q.shape
    C = HG_CHUNK
    n_c = S // C
    dt = q.dtype
    qf = jax.nn.silu(q.astype(jnp.float32)).reshape(B, n_c, C, HG_HEADS, HG_KEY)
    f = lb + (1.0 - lb) * jax.nn.sigmoid(f_raw.astype(jnp.float32))
    log_f = jnp.log(f).reshape(B, n_c, C, HG_HEADS, HG_KEY)
    k = (1.0 - f).reshape(B, n_c, C, HG_HEADS, HG_KEY)
    v = i_in.astype(jnp.float32).reshape(B, n_c, C, HG_HEADS, HG_VAL)
    b = jnp.cumsum(log_f, axis=2)
    b_last = b[:, :, -1:]
    q_dec = qf * jnp.exp(b)
    k_inv = k * jnp.exp(-b)
    k_end = k * jnp.exp(b_last - b)
    mask = jnp.tril(jnp.ones((C, C), dtype=bool))
    att = jnp.einsum('bcthk,bcshk->bchts', q_dec, k_inv)
    att = jnp.where(mask, att, jnp.zeros_like(att))
    o_intra = jnp.einsum('bchts,bcshv->bcthv', att, v)
    dS = jnp.einsum('bcshk,bcshv->bchkv', k_end, v)
    decay = jnp.exp(b_last[:, :, 0])

    def step(s_prev, inp):
        dec, ds = inp
        return dec[..., None] * s_prev + ds, s_prev

    s0 = jnp.zeros((B, HG_HEADS, HG_KEY, HG_VAL), jnp.float32)
    _, s_starts = lax.scan(step, s0, (jnp.moveaxis(decay, 1, 0), jnp.moveaxis(dS, 1, 0)))
    o_inter = jnp.einsum('bcthk,cbhkv->bcthv', q_dec, s_starts)
    o = (o_intra + o_inter).reshape(B, S, HG_HEADS, HG_VAL)
    o = o * lax.rsqrt(jnp.mean(o * o, axis=-1, keepdims=True) + EPS)
    o = o * norm_g.astype(jnp.float32).reshape(HG_HEADS, HG_VAL)
    return o.reshape(B, S, HG_VW).astype(dt) * jax.nn.sigmoid(og)

def hier_moe(h, w_grp, w_exp, w1, w3, w2):
    B, S, D = h.shape
    T = B * S
    xt = h.reshape(T, D)
    grp_logits = (xt @ w_grp).astype(jnp.float32)
    grp_prob = jax.nn.softmax(grp_logits, axis=-1)
    p_g, g_sel = lax.top_k(grp_prob, 1)
    exp_logits = (xt @ w_exp).astype(jnp.float32).reshape(T, N_GROUPS, EXP_PER_GROUP)
    sel_logits = jnp.take_along_axis(exp_logits, g_sel[:, :, None], axis=1)[:, 0]
    top_l, top_e = lax.top_k(sel_logits, TOP_K)
    gate = jax.nn.softmax(top_l, axis=-1) * p_g

    A = T * TOP_K
    eid = (g_sel * EXP_PER_GROUP + top_e).reshape(A)
    tok = jnp.repeat(jnp.arange(T, dtype=jnp.int32), TOP_K)
    wa = gate.reshape(A)
    order = jnp.argsort(eid)
    eid_s, tok_s, w_s = eid[order], tok[order], wa[order]
    counts = jnp.bincount(eid, length=N_EXPERTS)
    padded = ((counts + MOE_BLOCK - 1) // MOE_BLOCK) * MOE_BLOCK
    pad_end = jnp.cumsum(padded)
    pad_start = pad_end - padded
    start = jnp.cumsum(counts) - counts
    rank = jnp.arange(A, dtype=jnp.int32) - start[eid_s]
    dest = pad_start[eid_s] + rank
    n_blk = -(-A // MOE_BLOCK) + N_EXPERTS
    P = n_blk * MOE_BLOCK
    buf = jnp.zeros((P, D), xt.dtype).at[dest].set(xt[tok_s])
    blk_start = jnp.arange(n_blk, dtype=jnp.int32) * MOE_BLOCK
    blk_e = jnp.minimum(jnp.searchsorted(pad_end, blk_start, side='right'), N_EXPERTS - 1)

    def expert_block(args):
        xb, e = args
        return (jax.nn.silu(xb @ w1[e]) * (xb @ w3[e])) @ w2[e]

    ybuf = lax.map(expert_block, (buf.reshape(n_blk, MOE_BLOCK, D), blk_e)).reshape(P, D)
    contrib = ybuf[dest] * w_s[:, None].astype(xt.dtype)
    out = jax.ops.segment_sum(contrib, tok_s, num_segments=T)
    return out.reshape(B, S, D)

def second_inputs(seed: int = 0) -> dict:
    key = jax.random.key(seed)
    ks = jax.random.split(key, 24)

    def nrm(k, shape, scale):
        return jax.random.normal(k, shape, jnp.float32) * scale

    def gain(k, shape):
        return 1.0 + 0.05 * jax.random.normal(k, shape, jnp.float32)

    L = DEPTH
    return {
        "x": nrm(ks[0], (BATCH, SEQ, D_MODEL), 1.0),
        "p": nrm(ks[1], (DEPTH, BATCH, SEQ, PLE_DIM), 1.0),
        "g_mix": gain(ks[2], (L, D_MODEL)),
        "w_in": nrm(ks[3], (L, D_MODEL, IN_COLS), D_MODEL ** -0.5),
        "gm_ln_g": gain(ks[4], (L, GM_WIDTH)),
        "gm_ln_b": nrm(ks[5], (L, GM_WIDTH), 0.02),
        "gm_w_sp": nrm(ks[6], (L, GM_GROUPS, GM_CHUNK, GM_CHUNK), 0.1 * GM_CHUNK ** -0.5),
        "gm_b_sp": gain(ks[7], (L, GM_GROUPS, GM_CHUNK)),
        "w_up_a": nrm(ks[8], (L, GM_WIDTH, D_MODEL), GM_WIDTH ** -0.5),
        "hg_lb_param": gain(ks[9], (L + 1, HG_KW)),
        "hg_norm_g": gain(ks[10], (L, HG_VW)),
        "w_up_b": nrm(ks[11], (L, HG_VW, D_MODEL), HG_VW ** -0.5),
        "w_out": nrm(ks[12], (L, D_MODEL, D_MODEL), D_MODEL ** -0.5),
        "g_ffn": gain(ks[13], (L, D_MODEL)),
        "w_grp": nrm(ks[14], (L, D_MODEL, N_GROUPS), D_MODEL ** -0.5),
        "w_exp": nrm(ks[15], (L, D_MODEL, N_EXPERTS), D_MODEL ** -0.5),
        "w1": nrm(ks[16], (L, N_EXPERTS, D_MODEL, D_EXPERT), D_MODEL ** -0.5),
        "w3": nrm(ks[17], (L, N_EXPERTS, D_MODEL, D_EXPERT), D_MODEL ** -0.5),
        "w2": nrm(ks[18], (L, N_EXPERTS, D_EXPERT, D_MODEL), D_EXPERT ** -0.5),
        "g_ple": gain(ks[19], (L, D_MODEL)),
        "w_pg": nrm(ks[20], (L, D_MODEL, D_MODEL), D_MODEL ** -0.5),
        "w_ple": nrm(ks[21], (L, PLE_DIM, D_MODEL), PLE_DIM ** -0.5),
        "g_final": gain(ks[22], (D_MODEL,)),
    }

def second_block(x, p, g_mix, w_in, gm_ln_g, gm_ln_b, gm_w_sp, gm_b_sp, w_up_a,
              hg_lb_param, hg_norm_g, w_up_b, w_out, g_ffn, w_grp, w_exp,
              w1, w3, w2, g_ple, w_pg, w_ple, g_final):
    lb_all = jnp.cumsum(jax.nn.softmax(hg_lb_param.astype(jnp.float32), axis=0), axis=0)
    split_idx = [int(s) for s in np.cumsum(IN_SPLITS_2)[:-1]]
    for i in range(DEPTH):
        h = rmsnorm_2(x, g_mix[i])
        z = h @ w_in[i]
        u, v, hq, hf, hi, hog, gate_a, gate_b = jnp.split(z, split_idx, axis=-1)
        y_a = gmlp_branch(jax.nn.gelu(u), jax.nn.gelu(v), gm_ln_g[i], gm_ln_b[i], gm_w_sp[i], gm_b_sp[i])
        y_b = hgrn2_branch(hq, hf, hi, hog, lb_all[i], hg_norm_g[i])
        merged = jax.nn.sigmoid(gate_a) * (y_a @ w_up_a[i]) + jax.nn.sigmoid(gate_b) * (y_b @ w_up_b[i])
        x = x + merged @ w_out[i]
        h = rmsnorm_2(x, g_ffn[i])
        x = x + hier_moe(h, w_grp[i], w_exp[i], w1[i], w3[i], w2[i])
        h = rmsnorm_2(x, g_ple[i])
        x = x + jax.nn.sigmoid(h @ w_pg[i]) * (p[i] @ w_ple[i])
    return rmsnorm_2(x, g_final)


def setup_inputs(seed=0):
    out = dict(first_inputs(seed))
    for name, value in second_inputs(seed + 1).items():
        if name != "x":
            out[name + "_2"] = value
    return out


def reference(
    x, c, w_ada, b_ada, norm_mix_g, w_in, cmp_pos_k, cmp_w1_k, cmp_w2_k, cmp_pos_v, cmp_w1_v,
    cmp_w2_v, w_proj_a, w_proj_b, w_out, norm_ffn_g, w_ffn_gate, w_ffn_up, w_ffn_down,
    norm_final_g, p_2, g_mix_2, w_in_2, gm_ln_g_2, gm_ln_b_2, gm_w_sp_2, gm_b_sp_2, w_up_a_2,
    hg_lb_param_2, hg_norm_g_2, w_up_b_2, w_out_2, g_ffn_2, w_grp_2, w_exp_2, w1_2, w3_2, w2_2,
    g_ple_2, w_pg_2, w_ple_2, g_final_2,
):
    x = first_block(
        x, c, w_ada, b_ada, norm_mix_g, w_in, cmp_pos_k, cmp_w1_k, cmp_w2_k, cmp_pos_v,
        cmp_w1_v, cmp_w2_v, w_proj_a, w_proj_b, w_out, norm_ffn_g, w_ffn_gate, w_ffn_up,
        w_ffn_down, norm_final_g,
    )
    return second_block(
        x, p_2, g_mix_2, w_in_2, gm_ln_g_2, gm_ln_b_2, gm_w_sp_2, gm_b_sp_2, w_up_a_2,
        hg_lb_param_2, hg_norm_g_2, w_up_b_2, w_out_2, g_ffn_2, w_grp_2, w_exp_2, w1_2, w3_2,
        w2_2, g_ple_2, w_pg_2, w_ple_2, g_final_2,
    )


_drawn_inputs = setup_inputs


def setup_inputs(seed=0):
    import zlib

    import numpy as np

    out = dict(_drawn_inputs(seed))
    spreads = {}
    factors = {'cmp_pos_k': 53.061,
     'cmp_pos_v': 7.907,
     'gm_ln_g_2': 23.106,
     'gm_ln_b_2': 41.564,
     'hg_lb_param_2': 21.746,
     'g_ple_2': 6.163}
    for name, (base, spread) in spreads.items():
        noise = np.random.default_rng([zlib.crc32(name.encode()), seed]).standard_normal(out[name].shape)
        drawn = base * np.exp(spread * noise) if base else spread * noise
        out[name] = __import__('jax').numpy.asarray(drawn.astype(out[name].dtype))
    for name, factor in factors.items():
        out[name] = (out[name] * factor).astype(out[name].dtype)
    return out
```

```python
from contextlib import ExitStack

import numpy as np

import concourse.bass as bass
from concourse import mybir

ALU = mybir.AluOpType
ACT = mybir.ActivationFunctionType
AX = mybir.AxisListType
F32 = mybir.dt.float32
I32 = mybir.dt.int32
U32 = mybir.dt.uint32

P = 128
D = 1024
KD = D // P
T = 512
NT = T // P
CH = 512
HEADS = 8
HD = 64
GROUPS = 2
REP = HEADS // GROUPS
SCALE = HD ** -0.5
CMP_BLOCK, CMP_STRIDE = 32, 16
NCMP = (T - CMP_BLOCK) // CMP_STRIDE + 1
NC = 32
FF = 2816
KF = FF // P
EPS = 1e-6
EXPERTS, EGROUPS = 32, 4
EPG = EXPERTS // EGROUPS
DE = 512
KE = DE // P
CAP = 64
SPILL = 16
PAIRS = EXPERTS // 2
SLOTS = (PAIRS + SPILL) * P
RING = 4
U = CH
HG_HEADS, HG_CHUNK = 4, 64
GM_GROUPS = 8
NEG = -1e30
MASKED = -1e33
SP_CAP = 60.0


class Chunks:

    def __init__(self):
        self.items = []
        self.landed = []

    def add(self, *parts):
        i = len(self.items)
        before = self.landed[i - RING] if i >= RING else 0
        self.items.append(parts)
        self.landed.append(before + 16 * len(parts))
        return i


def feature_tiles(w, c0, c1):
    return w[:, c0:c1].rearrange("(k p) n -> p k n", p=P)


class Build:

    def __init__(self, nc, ctx, a, out):
        self.nc, self.ctx, self.a, self.out = nc, ctx, a, out
        self.of_block = []
        self.ring = self.sb("ring", [P, RING, 8 * CH])
        self.reg_a = self.sb("reg_a", [P, 8 * U])
        self.reg_b = self.sb("reg_b", [P, 8 * U])
        self.w1flat = self.sb("w1flat", [P, 8 * U])
        self.s_ab = self.sb("s_ab", [P, 24 * U])
        self.s_a, self.s_b = self.s_ab[:, 0:16 * U], self.s_ab[:, 16 * U:24 * U]
        self.u_big = self.sb("u_big", [P, 13 * U])
        self.scr = self.sb("scr", [P, 4 * U])
        self.small = self.sb("small", [P, 64])
        self.rows2 = self.sb("rows2", [P, 2, HEADS, 2])
        self.take_x(self.reg_a)
        self.take_h(self.reg_b)
        self.h_dram = nc.dram_tensor("h_saved", (P, 8 * U), F32).ap()
        self.ring_full = [self.lasting_sem(f"ring_full{i}") for i in range(RING)]
        self.ring_used = self.lasting_sem("ring_used")
        self.ch = Chunks()
        self.loaded = 0

    def sb(self, name, shape, dt=F32):
        return self.ctx.enter_context(self.nc.sbuf_tensor(name, shape, dt))

    def sem(self, name):
        s = self.nc.alloc_semaphore(name=name)
        self.of_block.append(s)
        return s

    def lasting_sem(self, name):
        return self.nc.alloc_semaphore(name=name)

    def next_block(self):
        self.nc.clear_and_free_semaphores(self.of_block)
        self.of_block = []
        self.nc.all_engine_barrier()

    def take_x(self, reg):
        self.x = reg[:].rearrange("p (t d) -> p t d", t=NT)

    def take_h(self, reg):
        self.hT = reg[:].rearrange("p (k t) -> p k t", k=KD)
        self.hTflat = reg

    def chunk(self, i, part=0):
        at = 0
        for p in self.ch.items[i][:part]:
            at += p.shape[1] * p.shape[2]
        _, k, n = self.ch.items[i][part].shape
        return self.ring[:, i % RING, at:at + k * n].rearrange("p (k n) -> p k n", k=k)

    def wait_chunk(self, eng, i):
        eng.wait_ge(self.ring_full[i % RING], self.ch.landed[i])

    def load_until(self, sp, end):
        for i in range(self.loaded, min(end, len(self.ch.items))):
            if i >= RING:
                sp.wait_ge(self.ring_used, i - RING + 1)
            for part, dram in enumerate(self.ch.items[i]):
                sp.dma_start(self.chunk(i, part), dram).then_inc(self.ring_full[i % RING], 16)
        self.loaded = max(self.loaded, min(end, len(self.ch.items)))


def plan_weights(b):
    a, add = b.a, b.ch.add

    def halves(w):
        return [(h, 0, KD, add(feature_tiles(w, h * CH, h * CH + CH))) for h in range(2)]

    b.c_ada = [add(feature_tiles(a["w_ada"][0], j * CH, j * CH + CH)) for j in range(12)]
    w = a["w_in"][0]
    ends = [0, 512, 1024, 1304, 1816, 2328, 2840]
    b.c_in = [add(feature_tiles(w, c0, c1)) for c0, c1 in zip(ends, ends[1:])]
    b.c_merge1 = plan_merge(add, w, ends[-1], a["w_proj_a"][0], a["w_proj_b"][0])
    b.c_out1 = halves(a["w_out"][0])
    b.c_ffn = [add(feature_tiles(a["w_ffn_gate"][0], j, j + 256), feature_tiles(a["w_ffn_up"][0], j, j + 256))
               for j in range(0, FF, 256)]
    w = a["w_ffn_down"][0]
    b.c_down = [(h, k, min(k + 8, KF), add(feature_tiles(w[k * P:min(k + 8, KF) * P, :], h * CH, h * CH + CH)))
                for h in range(2) for k in range(0, KF, 8)]
    w = a["w_in_2"][0]
    b.c_in2 = [add(feature_tiles(w, j * CH, j * CH + CH)) for j in range(6)]
    b.c_merge2 = plan_merge(add, w, 6 * CH, a["w_up_a_2"][0], a["w_up_b_2"][0])
    b.c_out2 = halves(a["w_out_2"][0])


def plan_merge(add, w, c0, wa, wb):
    out = []
    for n in range(0, D, 256):
        out.append((add(feature_tiles(w, c0 + n, c0 + n + 256), feature_tiles(w, c0 + D + n, c0 + D + n + 256)),
                    add(feature_tiles(wa, n, n + 256), feature_tiles(wb, n, n + 256))))
    return out


VROWS = [("c", 8), ("norm_mix_g", 8), ("norm_ffn_g", 8), ("g_mix_2", 8), ("g_ffn_2", 8),
         ("g_ple_2", 8), ("hg_norm_g_2", 4), ("hg_lb_param_2", 8), ("gm_b_sp_2", 8)]
VAT = {}
_n = 0
for _name, _k in VROWS:
    VAT[_name] = _n
    _n += _k
NV = _n


def stage_constants(b):
    nc, a = b.nc, b.a
    b.ident = b.sb("ident", [P, P])
    b.ones = b.sb("ones", [P, P])
    b.vcol = b.sb("vcol", [P, NV])
    b.sc = b.sb("silu_c", [P, KD])
    vrow = b.scr[0:NV, 0:P]
    loads, pool_done, cols, cols_out = (b.sem(n) for n in ("k_loads", "k_pool", "k_cols", "k_out"))
    b.x_in = b.sem("x_in")
    with nc.psum_tensor("k_ps", [P, CH], F32) as ps, nc.Block() as block:
        @block.sync
        def _(sp):
            for name, k in VROWS:
                n = "a b c -> (a b) c" if len(a[name].shape) == 3 else None
                v = a[name].rearrange(n) if n else a[name].rearrange("a (k p) -> (a k) p", p=P)
                sp.dma_start(vrow[VAT[name]:VAT[name] + k, :], v).then_inc(loads, 16)
            sp.dma_start(b.x[:], a["x"][0].rearrange("(t p) d -> p t d", p=P)).then_inc(b.x_in, 16)
            b.load_until(sp, RING)

        @block.gpsimd
        def _(pool):
            nc.gpsimd.memset(b.ident[:], 0.0).then_inc(pool_done, 1)
            nc.gpsimd.memset(b.ones[:], 1.0).then_inc(pool_done, 1)
            pool.wait_ge(pool_done, 2)
            nc.gpsimd.affine_select(out=b.ident[:], in_=b.ident[:], compare_op=ALU.not_equal, fill=1.0,
                                    base=0, pattern=[[-1, P]], channel_multiplier=1).then_inc(pool_done, 1)

        @block.tensor
        def _(pe):
            pe.wait_ge(pool_done, 3)
            pe.wait_ge(loads, 16 * len(VROWS))
            nc.tensor.transpose(ps[:, 0:NV], vrow, b.ident[0:NV, 0:NV]).then_inc(cols, 1)

        @block.vector
        def _(dve):
            dve.wait_ge(cols, 1)
            nc.vector.tensor_copy(b.vcol[:], ps[:, 0:NV]).then_inc(cols_out, 1)

        @block.scalar
        def _(act):
            act.wait_ge(cols_out, 1)
            nc.scalar.activation(b.sc[:], b.vcol[:, 0:KD], ACT.Silu)


def stage_modulation(b):
    nc, a = b.nc, b.a
    acc = b.u_big[:, 0:6 * D]
    b.modcol = b.sb("modcol", [P, 4 * KD])
    b.mulcol = b.sb("mulcol", [P, 2 * KD])
    b.g1row = b.sb("g1row", [P, D])
    b.g2row = b.sb("g2row", [P, D])
    bias_in, step, summed, cols, rows, moved = (
        b.sem(n) for n in ("ada_bias", "ada_step", "ada_summed", "ada_cols", "ada_rows", "ada_moved"))
    COLS = [0, 1, 3, 4]
    with ExitStack() as ps_ctx:
        psc = ps_ctx.enter_context(nc.psum_tensor("ada_psc", [P, CH], F32))
        psr = [ps_ctx.enter_context(nc.psum_tensor(f"ada_psr{i}", [P, CH], F32)) for i in range(4)]
        block = ps_ctx.enter_context(nc.Block())

        @block.sync
        def _(sp):
            sp.wait_ge(step, 1)
            sp.dma_start(acc[0:1, :], a["b_ada"]).then_inc(bias_in, 16)
            b.load_until(sp, b.c_ada[-1] + 1 + RING)

        @block.vector
        def _(dve):
            nc.vector.memset(acc, 0.0).then_inc(step, 1)
            dve.wait_ge(bias_in, 16)
            n = 1
            for j, c in enumerate(b.c_ada):
                b.wait_chunk(dve, c)
                w, s = b.chunk(c), acc[:, j * CH:j * CH + CH]
                for k in range(KD):
                    dve.wait_ge(step, n)
                    last = nc.vector.scalar_tensor_tensor(out=s, in0=w[:, k, :], scalar=b.sc[:, k:k + 1], in1=s,
                                                          op0=ALU.mult, op1=ALU.add).then_inc(step, 1)
                    n += 1
                dve.wait_ge(step, n)
                nc.vector.sem_inc(b.ring_used, 1)
            nc.vector.sem_inc(summed, 1)
            dve.wait_ge(cols, 1)
            nc.vector.tensor_copy(b.modcol[:], psc[:, 0:4 * KD]).then_inc(step, 1)
            n += 1
            dve.wait_ge(step, n)
            for i, g in enumerate(("norm_mix_g", "norm_ffn_g")):
                nc.vector.scalar_tensor_tensor(
                    out=b.mulcol[:, i * KD:i * KD + KD], in0=b.modcol[:, (2 * i + 1) * KD:(2 * i + 2) * KD],
                    scalar=1.0, in1=b.vcol[:, VAT[g]:VAT[g] + KD], op0=ALU.add, op1=ALU.mult)
            dve.wait_ge(rows, 4)
            for i in range(4):
                dst = (b.g1row, b.g2row)[i // 2]
                nc.vector.tensor_copy(dst[:, i % 2 * CH:i % 2 * CH + CH], psr[i][:])

        @block.tensor
        def _(pe):
            pe.wait_ge(summed, 1)
            for i, part in enumerate(COLS):
                for k in range(KD):
                    mm = nc.tensor.matmul(psc[:, i * KD + k:i * KD + k + 1], acc[:, part * D + k * P:part * D + k * P + P],
                                          b.ones[:, 0:1], start=True, stop=True)
            mm.then_inc(cols, 1)
            for i in range(4):
                c = (2, 5)[i // 2] * D + i % 2 * CH
                nc.tensor.matmul(psr[i][:], b.ones[:], acc[:, c:c + CH], start=True, stop=True).then_inc(rows, 1)


def stage_norm(b, name, mul, add, first=False, rows_out=None,
               residual_row=None, save=None):
    nc = b.nc
    y = b.u_big[:, 0:NT * D].rearrange("p (t d) -> p t d", t=NT)
    ss = b.small[:, 0:16]
    squared, var, root, inv, scaled, turned, ev_a, ev_d, wrote, passd = (
        b.sem(f"{name}_{n}") for n in ("sq", "var", "root", "inv", "y", "turn", "eva", "evd", "rows", "pass"))
    row, row_in = b.scr[:, 0:D], b.sem(f"{name}_rowin")
    passes = 2 if residual_row is not None else 1
    with ExitStack() as ps_ctx:
        ps = [ps_ctx.enter_context(nc.psum_tensor(f"{name}_ps{i}", [P, CH], F32)) for i in range(4)]
        block = ps_ctx.enter_context(nc.Block())

        @block.sync
        def _(sp):
            if residual_row is not None:
                sp.dma_start(row, b.a[residual_row].partition_broadcast(P)).then_inc(row_in, 16)
            if rows_out is not None:
                sp.wait_ge(scaled, 1)
                sp.dma_start(rows_out.rearrange("(t p) d -> p t d", p=P), y).then_inc(wrote, 16)
                sp.wait_ge(wrote, 16)
            if save is not None:
                sp.wait_ge(ev_a, KD // 2)
                sp.wait_ge(ev_d, KD // 2)
                sp.dma_start(save, b.hTflat[:]).then_inc(wrote, 16)
                sp.wait_ge(wrote, 16)

        @block.scalar
        def _(act):
            if first:
                act.wait_ge(b.x_in, 16)
            for r in range(passes):
                if r:
                    act.wait_ge(passd, 1)
                for t in range(NT):
                    act_ = nc.scalar.activation(y[:, t, :], b.x[:, t, :], ACT.Square, accum_out=ss[:, 4 * r + t:4 * r + t + 1])
                act_.then_inc(squared, 1)
                act.wait_ge(var, r + 1)
                nc.scalar.activation(ss[:, 4 * r:4 * r + 4], ss[:, 4 * r:4 * r + 4], ACT.Sqrt).then_inc(root, 1)
            for k in range(1, KD, 2):
                act.wait_ge(turned, k + 1)
                nc.scalar.activation(b.hT[:, k, :], ps[k % 4][:], ACT.Identity, scale=mul[:, k:k + 1],
                                     bias=add[:, k:k + 1] if add is not None else 0.0).then_inc(ev_a, 1)

        @block.vector
        def _(dve):
            if first:
                dve.wait_ge(b.x_in, 16)
            for r in range(passes):
                s = ss[:, 4 * r:4 * r + 4]
                dve.wait_ge(squared, r + 1)
                nc.vector.tensor_scalar(s, s, 1.0 / D, EPS, ALU.mult, ALU.add).then_inc(var, 1)
                dve.wait_ge(root, r + 1)
                nc.vector.reciprocal(s, s).then_inc(inv, 1)
                dve.wait_ge(inv, r + 1)
                if r < passes - 1:
                    dve.wait_ge(row_in, 16)
                for t in range(NT):
                    rs = ss[:, 4 * r + t:4 * r + t + 1]
                    if r < passes - 1:
                        last = nc.vector.scalar_tensor_tensor(out=b.x[:, t, :], in0=b.x[:, t, :], scalar=rs,
                                                              in1=row, op0=ALU.mult, op1=ALU.mult)
                    else:
                        last = nc.vector.tensor_scalar(y[:, t, :], b.x[:, t, :], rs, None, ALU.mult)
                last.then_inc(passd if r < passes - 1 else scaled, 1)
                if r < passes - 1:
                    dve.wait_ge(passd, 1)
            for k in range(0, KD, 2):
                dve.wait_ge(turned, k + 1)
                if add is not None:
                    nc.vector.tensor_scalar(b.hT[:, k, :], ps[k % 4][:], mul[:, k:k + 1], add[:, k:k + 1],
                                            ALU.mult, ALU.add).then_inc(ev_d, 1)
                else:
                    nc.vector.tensor_scalar(b.hT[:, k, :], ps[k % 4][:], mul[:, k:k + 1], None,
                                            ALU.mult).then_inc(ev_d, 1)

        @block.tensor
        def _(pe):
            pe.wait_ge(scaled, 1)
            for k in range(KD):
                if k >= 4:
                    pe.wait_ge((ev_d, ev_a)[k % 2], (k - 4) // 2 + 1)
                for t in range(NT):
                    mm = nc.tensor.transpose(ps[k % 4][:, t * P:t * P + P], y[:, t, k * P:k * P + P], b.ident[:])
                mm.then_inc(turned, 1)


def product_T(nc, ps, w, n0, hT, kt):
    for k in range(kt):
        mm = nc.tensor.matmul(ps, w[:, k, n0:n0 + P], hT[:, k, :], start=(k == 0), stop=(k == kt - 1))
    return mm


def product_rows(nc, ps, hT, t, w, kt, start=True, stop=True):
    for k in range(kt):
        mm = nc.tensor.matmul(ps, hT[:, k, t * P:t * P + P], w[:, k, :],
                              start=start and k == 0, stop=stop and k == kt - 1)
    return mm


def stage_project1(b):
    nc = b.nc
    b.qT = b.s_a[:, 0:4 * T].rearrange("p (n t) -> p n t", n=4)
    b.sqT = b.s_a[:, 4 * T:8 * T].rearrange("p (n t) -> p n t", n=4)
    b.skT = b.s_a[:, 8 * T:12 * T].rearrange("p (n t) -> p n t", n=4)
    b.sv = b.s_a[:, 12 * T:16 * T].rearrange("p (t n) -> p t n", t=NT)
    b.kk = [b.s_b[:, i * 2 * T:(i + 1) * 2 * T].rearrange("p (g t) -> p g t", g=2) for i in range(2)]
    b.kcT, b.vcT = b.s_b[:, 4 * T:5 * T], b.s_b[:, 5 * T:6 * T]
    b.vv = [b.s_b[:, (6 + i) * T:(7 + i) * T].rearrange("p (t n) -> p t n", t=NT) for i in range(2)]
    b.gate = b.sb("gate", [P, NT, 24])

    def copy_rows(dst, w4):
        return ("rows4", dst, w4)

    tiles = [(0, n * P, "q", b.qT[:, n, :]) for n in range(4)]
    tiles += [(1, 0, "T", b.kcT), (1, P, "T", b.vcT), (1, 2 * P, "dup", b.kk[0]), (1, 3 * P, "rows", b.vv[0])]
    tiles += [(2, 0, "dup", b.kk[1]), (2, P, "rows", b.vv[1]), (2, 2 * P, "gate", b.gate)]
    tiles += [(3, n * P, "q", b.sqT[:, n, :]) for n in range(4)]
    tiles += [(4, n * P, "T", b.skT[:, n, :]) for n in range(4)]
    tiles += [(5, t, "wide", b.sv[:, t, :]) for t in range(4)]
    NB = 6
    ready, ev_a, ev_d = (b.sem(f"p1_{n}") for n in ("ready", "eva", "evd"))
    with ExitStack() as ps_ctx:
        ps = [ps_ctx.enter_context(nc.psum_tensor(f"p1_ps{i}", [P, CH], F32)) for i in range(NB)]
        block = ps_ctx.enter_context(nc.Block())

        @block.sync
        def _(sp):
            b.load_until(sp, b.c_in[-1] + 1 + RING)

        @block.tensor
        def _(pe):
            for i, (c, n0, kind, _) in enumerate(tiles):
                if i == 0 or tiles[i - 1][0] != c:
                    b.wait_chunk(pe, b.c_in[c])
                if i >= NB:
                    pe.wait_ge((ev_d, ev_a)[i % 2], (i - NB) // 2 + 1)
                w, bank = b.chunk(b.c_in[c]), ps[i % NB]
                if kind in ("q", "T", "dup"):
                    mm = product_T(nc, bank[:], w, n0, b.hT, KD)
                elif kind == "wide":
                    mm = product_rows(nc, bank[:], b.hT, n0, w, KD)
                else:
                    n = P if kind == "rows" else 24
                    for t in range(NT):
                        mm = product_rows(nc, bank[:, t * n:t * n + n], b.hT, t, w[:, :, n0:n0 + n], KD)
                mm.then_inc(ready, 1)
                if i + 1 == len(tiles) or tiles[i + 1][0] != c:
                    pe.wait_ge(ready, i + 1)
                    nc.tensor.sem_inc(b.ring_used, 1)

        def move(eng, copy, scaled, i, done):
            _, _, kind, dst = tiles[i]
            bank = ps[i % NB]
            eng.wait_ge(ready, i + 1)
            if kind == "q":
                last = scaled(dst, bank[:])
            elif kind in ("T", "wide"):
                last = copy(dst, bank[:])
            elif kind == "dup":
                for half in range(2):
                    for g in range(2):
                        last = copy(dst[64 * half:64 * half + 64, g, :], bank[64 * g:64 * g + 64, :])
            elif kind == "rows":
                last = copy(dst, bank[:].rearrange("p (t n) -> p t n", t=NT))
            else:
                last = copy(dst[:], bank[:, 0:NT * 24].rearrange("p (t n) -> p t n", t=NT))
            last.then_inc(done, 1)

        @block.vector
        def _(dve):
            for i in range(0, len(tiles), 2):
                move(dve, nc.vector.tensor_copy, lambda o, s: nc.vector.tensor_scalar(o, s, SCALE, None, ALU.mult), i, ev_d)

        @block.scalar
        def _(act):
            for i in range(1, len(tiles), 2):
                move(act, nc.scalar.copy, lambda o, s: nc.scalar.mul(o, s, SCALE), i, ev_a)


def stage_compress(b):
    nc, a = b.nc, b.a
    b.bias = b.u_big[:, 0:HEADS * T].rearrange("p (h k) -> p h k", h=HEADS)
    b.sbmask = b.u_big[:, 8 * T:9 * T]
    b.oa = b.u_big[:, 9 * T:13 * T].rearrange("p (t n) -> p t n", t=NT)
    nd = b.scr[:, 0:T]
    ndc = b.scr[:, T:T + NT * NC].rearrange("p (t n) -> p t n", t=NT)
    posr = b.scr[0:32, 640:896]
    posT = b.scr[:, 896:960].rearrange("p (b l) -> p b l", b=2)
    kp = b.hTflat[:, 0:2 * 1024].rearrange("p (b l n) -> p b l n", b=2, l=32)
    w1 = [r[:].rearrange("p (l n) -> p l n", l=CMP_BLOCK) for r in (b.reg_a, b.w1flat)]
    w2 = b.scr[:, 960:1216]
    hid = b.hTflat[:, 2048:2048 + 4 * NC].rearrange("p (b g n) -> p b g n", b=2, g=2)
    kc = b.hTflat[:, 2304:2304 + 2 * NC].rearrange("p (g n) -> p g n", g=2)
    vbd = b.hTflat[:, 2560:2560 + 2 * REP * HD].rearrange("p (g n) -> p g n", g=2)
    cs = [b.hTflat[:, 3072 + i * 256:3072 + i * 256 + 256].rearrange("p (h n) -> p h n", h=HEADS) for i in range(4)]
    pTc = b.scr[:, 1216:1216 + 2 * 2 * P].rearrange("p (i g q) -> p i g q", i=2, g=2)
    st = b.small
    w_in, pool, sel, win, hsum, hact, kcp, kco, dchain, sc, scm, expd, pt, pte, o, oe, gsig, vz = (
        b.sem(f"cmp_{n}") for n in ("w", "pool", "sel", "win", "hsum", "hact", "kcp", "kco", "chain", "sc", "scm",
                                    "exp", "pt", "pte", "o", "oe", "gsig", "vz"))
    slopes = [2.0 ** -(h + 1) for h in range(HEADS)]
    with ExitStack() as ps_ctx:
        def bank(n):
            return ps_ctx.enter_context(nc.psum_tensor(f"cmp_{n}", [P, CH], F32))
        ps_k, ps_t, ps_o = (bank(n) for n in ("k", "t", "o"))
        ps_pos, ps_h, ps_s = ps_t, [bank("h0"), bank("h1")], [bank("s0"), bank("s1")]
        block = ps_ctx.enter_context(nc.Block())

        @block.sync
        def _(sp):
            for i, n in enumerate("kv"):
                w = a[f"cmp_w1_{n}"][0].rearrange("(l d) n -> d l n", d=HD)
                for half in range(2):
                    sp.dma_start(w1[i][64 * half:64 * half + 64], w).then_inc(w_in, 16)
                    sp.dma_start(posr[:, (2 * i + half) * HD:(2 * i + half + 1) * HD], a[f"cmp_pos_{n}"][0]).then_inc(w_in, 16)
                    sp.dma_start(w2[:, (2 * i + half) * HD:(2 * i + half + 1) * HD], a[f"cmp_w2_{n}"][0]).then_inc(w_in, 16)

        @block.gpsimd
        def _(pool_):
            nc.gpsimd.iota(nd, pattern=[[1, T]], base=-(T - P), channel_multiplier=-1,
                           allow_small_or_imprecise_dtypes=True).then_inc(pool, 1)
            nc.gpsimd.iota(ndc, pattern=[[-P, NT], [CMP_STRIDE, NC]], base=CMP_BLOCK - 1, channel_multiplier=-1,
                           allow_small_or_imprecise_dtypes=True).then_inc(pool, 1)
            nc.gpsimd.memset(b.sbmask, 0.0).then_inc(pool, 1)
            nc.gpsimd.memset(st[:, 40:41], 1.0).then_inc(pool, 1)
            pool_.wait_ge(pool, 4)
            nc.gpsimd.affine_select(out=nd, in_=nd, compare_op=ALU.is_ge, fill=MASKED, base=T - P,
                                    pattern=[[-1, T]], channel_multiplier=1).then_inc(sel, 1)
            nc.gpsimd.affine_select(out=ndc, in_=ndc, compare_op=ALU.is_ge, fill=MASKED, base=-(CMP_BLOCK - 1),
                                    pattern=[[P, NT], [-CMP_STRIDE, NC]], channel_multiplier=1).then_inc(sel, 1)
            nc.gpsimd.affine_select(out=b.sbmask, in_=b.sbmask, compare_op=ALU.is_gt, fill=NEG, base=T - P,
                                    pattern=[[-1, T]], channel_multiplier=1).then_inc(sel, 1)
            nc.gpsimd.affine_select(out=st[:, 40:41], in_=st[:, 40:41], compare_op=ALU.is_ge, fill=0.0,
                                    base=-(CMP_BLOCK - 1), pattern=[[0, 1]], channel_multiplier=1).then_inc(sel, 1)

        @block.tensor
        def _(pe):
            pe.wait_ge(w_in, 16 * 12)
            for i in range(2):
                mm = nc.tensor.transpose(ps_pos[:, 32 * i:32 * i + 32], posr[:, 2 * i * HD:2 * (i + 1) * HD], b.ident[0:32, 0:32])
            mm.then_inc(kcp, 1)
            for i in range(2):
                pe.wait_ge(win, i + 1)
                for l in range(CMP_BLOCK):
                    for g in range(2):
                        rows = slice(64 * g, 64 * g + 64)
                        mm = nc.tensor.matmul(ps_h[g][:, i * NC:(i + 1) * NC], w1[i][rows, l, :], kp[rows, i, l, :],
                                              start=(l == 0), stop=(l == CMP_BLOCK - 1))
                mm.then_inc(hsum, 1)
            pe.wait_ge(hact, 1)
            for g in range(2):
                nc.tensor.matmul(ps_k[:, g * NC:(g + 1) * NC], w2[:, 0:2 * HD], hid[:, 0, g, :], start=True, stop=True)
            for g in range(2):
                mm = nc.tensor.matmul(ps_k[0:NC, P + g * HD:P + (g + 1) * HD], hid[:, 1, g, :], w2[:, 2 * HD:3 * HD],
                                      start=True, stop=True)
            mm.then_inc(kco, 1)
            pe.wait_ge(dchain, 1)
            for t in range(NT):
                if t:
                    pe.wait_ge(scm, t)
                for h in range(HEADS):
                    r = slice(64 * (h % 2), 64 * (h % 2) + 64)
                    mm = nc.tensor.matmul(ps_s[h % 2][:, h // 2 * NC:(h // 2 + 1) * NC], b.qT[r, h // 2, t * P:t * P + P],
                                          kc[r, h // REP, :], start=True, stop=True)
                mm.then_inc(sc, 1)
                pe.wait_ge(expd, t + 1)
                for g in range(2):
                    mm = nc.tensor.transpose(ps_t[:, g * P:g * P + P], cs[t][:, g * REP:(g + 1) * REP, :].rearrange("p h n -> p (h n)"), b.ident[:])
                mm.then_inc(pt, 1)
                pe.wait_ge(pte, t + 1)
                if t:
                    pe.wait_ge(oe, t)
                for g in range(2):
                    mm = nc.tensor.matmul(ps_o[:, g * REP * HD:(g + 1) * REP * HD], pTc[:, t % 2, g, :], vbd[:, g, :],
                                          start=True, stop=True)
                mm.then_inc(o, 1)

        @block.vector
        def _(dve):
            n = [0]

            def link(ins):
                n[0] += 1
                ins.then_inc(vz, 1)
                dve.wait_ge(vz, n[0])

            nc.vector.memset(kp[:, :, :, NCMP:NC], 0.0)
            link(nc.vector.memset(vbd, 0.0))
            dve.wait_ge(kcp, 1)
            link(nc.vector.tensor_copy(posT, ps_pos[:, 0:64].rearrange("p (b l) -> p b l", b=2)))
            for i, src in enumerate((b.kcT, b.vcT)):
                s = src.rearrange("p (n l) -> p l n", l=CMP_STRIDE)
                for half in range(2):
                    l = slice(half * CMP_STRIDE, (half + 1) * CMP_STRIDE)
                    last = nc.vector.tensor_tensor(kp[:, i, l, 0:NCMP], s[:, :, half:half + NCMP],
                                                   posT[:, i, l].unsqueeze(2).to_broadcast([P, CMP_STRIDE, NCMP]), ALU.add)
                last.then_inc(win, 1)
            dve.wait_ge(sel, 4)
            for h in range(HEADS):
                nc.vector.tensor_scalar(b.bias[:, h, :], nd, slopes[h], None, ALU.mult)
            dve.wait_ge(kco, 1)
            nc.vector.tensor_copy(kc, ps_k[:, 0:2 * NC].rearrange("p (g n) -> p g n", g=2))
            for g in range(2):
                for r in range(REP):
                    last = nc.vector.tensor_copy(vbd[NC * r:NC * r + NC, g, r * HD:(r + 1) * HD], ps_k[0:NC, P + g * HD:P + (g + 1) * HD])
            last.then_inc(dchain, 1)
            dve.wait_ge(gsig, 1)
            for t in range(NT):
                dve.wait_ge(sc, t + 1)
                for h in range(HEADS):
                    last = nc.vector.scalar_tensor_tensor(out=cs[t][:, h, :], in0=ndc[:, t, :], scalar=slopes[h],
                                                          in1=ps_s[h % 2][:, h // 2 * NC:(h // 2 + 1) * NC], op0=ALU.mult, op1=ALU.add)
                last.then_inc(scm, 1)
                dve.wait_ge(scm, t + 1)
                link(nc.vector.tensor_reduce(st[:, 0:8], cs[t], AX.X, ALU.max))
                link(nc.vector.tensor_tensor(cs[t], cs[t], st[:, 0:8].unsqueeze(2).to_broadcast([P, HEADS, NC]), ALU.subtract))
                nc.vector.sem_inc(dchain, 1)
                dve.wait_ge(expd, t + 1)
                link(nc.vector.tensor_reduce(st[:, 8:16], cs[t], AX.X, ALU.add))
                link(nc.vector.reciprocal(st[:, 16:24], st[:, 8:16]))
                gates = b.gate[:, t, :].rearrange("p (h b) -> p h b", b=3)
                link(nc.vector.tensor_tensor(st[:, 24:32], st[:, 16:24], gates[:, :, 0], ALU.mult))
                if t == 0:
                    link(nc.vector.tensor_scalar(st[:, 24:32], st[:, 24:32], st[:, 40:41], None, ALU.mult))
                dve.wait_ge(pt, t + 1)
                nc.vector.tensor_copy(pTc[:, t % 2], ps_t[:, 0:2 * P].rearrange("p (g q) -> p g q", g=2)).then_inc(pte, 1)
                dve.wait_ge(o, t + 1)
                nc.vector.tensor_tensor(b.oa[:, t, :].rearrange("p (h n) -> p h n", h=HEADS), ps_o[:].rearrange("p (h n) -> p h n", h=HEADS),
                                        st[:, 24:32].unsqueeze(2).to_broadcast([P, HEADS, HD]), ALU.mult).then_inc(oe, 1)

        @block.scalar
        def _(act):
            nc.scalar.activation(b.gate[:], b.gate[:], ACT.Sigmoid).then_inc(gsig, 1)
            act.wait_ge(hsum, 2)
            for g in range(2):
                last = nc.scalar.activation(hid[:, :, g, :], ps_h[g][:, 0:2 * NC].rearrange("p (b n) -> p b n", b=2), ACT.Gelu_apprx_tanh)
            last.then_inc(hact, 1)
            for t in range(NT):
                act.wait_ge(dchain, t + 2)
                nc.scalar.activation(cs[t], cs[t], ACT.Exp).then_inc(expd, 1)


def stage_attention(b):
    nc = b.nc
    b.ob = b.hTflat[:, 0:4 * T].rearrange("p (t n) -> p t n", t=NT)
    PER = 3 * HEADS
    units = [(t, i // 3, i % 3) for t in range(NT) for i in range(PER)]
    N = len(units)
    LAG_T, LAG_V = 4, 5

    def bufs(reg, u0, n):
        return reg[:, u0 * U:(u0 + n) * U].rearrange("p (i k) -> p i k", i=n)
    prob, ssb = bufs(b.w1flat, 0, 6), bufs(b.w1flat, 6, 2)
    zbuf, zc, ex = bufs(b.hTflat, 4, 2), bufs(b.hTflat, 6, 2), bufs(b.s_b, 4, 2)
    ptsb = b.scr[:, 0:3 * T].rearrange("p (i k) -> p i k", i=3)
    tmp = b.scr[:, 3 * T:4 * T]
    negm = b.small[:, 0:4]
    rows = b.small[:, 8:24].rearrange("p (h b) -> p h b", b=2)
    fac = b.small[:, 24:40].rearrange("p (h b) -> p h b", b=2)
    (sc_ready, s_taken, p_soft, z_ready, e_done, l_ready, chain, w_ready, p_stick, pt_ready, pt_a, pt_d, pv,
     o_moved) = (b.sem(f"at_{n}") for n in (
         "scores", "taken", "psoft", "z", "e", "l", "chain", "w", "pstick", "pt", "pta", "ptd", "pv", "omoved"))

    def keys(i):
        return (units[i][0] + 1) * P

    def soft_count(i):
        return (i // 3) * 2 + min(i % 3 + 1, 2)

    with ExitStack() as ps_ctx:
        def bank(n):
            return ps_ctx.enter_context(nc.psum_tensor(f"at_{n}", [P, CH], F32))
        ps_s = [bank(f"s{i}") for i in range(3)]
        ps_t = [bank(f"t{i}") for i in range(2)]
        ps_o = [bank(f"o{i}") for i in range(3)]
        block = ps_ctx.enter_context(nc.Block())

        @block.tensor
        def _(pe):
            for s in range(N + LAG_V):
                if s < N:
                    t, h, kind = units[s]
                    if s >= 3:
                        pe.wait_ge(s_taken, s - 2)
                    r = slice(64 * (h % 2), 64 * (h % 2) + 64)
                    q = (b.sqT if kind == 2 else b.qT)[r, h // 2, t * P:t * P + P]
                    k = b.skT[r, h // 2, 0:keys(s)] if kind == 2 else b.kk[kind][r, h // REP, 0:keys(s)]
                    nc.tensor.matmul(ps_s[s % 3][:, 0:keys(s)], q, k, start=True, stop=True).then_inc(sc_ready, 1)
                i = s - LAG_T
                if 0 <= i < N:
                    if i % 3 == 2:
                        pe.wait_ge(p_stick, i // 3 + 1)
                    else:
                        pe.wait_ge(p_soft, soft_count(i))
                    if i >= 2:
                        if (i - 2) % 3 == 2:
                            pe.wait_ge(pt_d, (i - 2) // 3 + 1)
                        else:
                            pe.wait_ge(pt_a, soft_count(i - 2))
                    for c in range(0, keys(i), P):
                        mm = nc.tensor.transpose(ps_t[i % 2][:, c:c + P], prob[:, i % 6, c:c + P], b.ident[:])
                    mm.then_inc(pt_ready, 1)
                i = s - LAG_V
                if 0 <= i < N:
                    t, h, kind = units[i]
                    if i % PER == 0 and i:
                        pe.wait_ge(o_moved, t)
                    if kind == 2:
                        pe.wait_ge(pt_d, i // 3 + 1)
                    else:
                        pe.wait_ge(pt_a, soft_count(i))
                    for c in range(t + 1):
                        v = b.sv[:, c, h * HD:(h + 1) * HD] if kind == 2 else b.vv[kind][:, c, h // REP * HD:(h // REP + 1) * HD]
                        mm = nc.tensor.matmul(ps_o[kind][:, h * HD:(h + 1) * HD], ptsb[:, i % 3, c * P:c * P + P], v,
                                              start=(c == 0), stop=(c == t))
                    mm.then_inc(pv, 1)

        @block.vector
        def _(dve):
            n = [0]

            def link(ins):
                n[0] += 1
                ins.then_inc(chain, 1)
                dve.wait_ge(chain, n[0])

            for s in range(N + LAG_V + 1):
                if s < N:
                    t, h, kind = units[s]
                    k, j = keys(s), s // 3
                    off = T - k
                    dve.wait_ge(sc_ready, s + 1)
                    if kind < 2:
                        m = soft_count(s) - 1
                        if m >= 2:
                            dve.wait_ge(p_soft, m - 1)
                        nc.vector.tensor_tensor_reduce(out=ssb[:, m % 2, 0:k], in0=ps_s[s % 3][:, 0:k], in1=b.bias[:, h, off:T],
                                                       scale=-1.0, scalar=3e38, op0=ALU.add, op1=ALU.min,
                                                       accum_out=negm[:, m % 2:m % 2 + 1]).then_inc(s_taken, 1)
                    else:
                        if j >= 2:
                            dve.wait_ge(p_stick, j - 1)
                        nc.vector.tensor_tensor(zbuf[:, j % 2, 0:k], ps_s[s % 3][:, 0:k], b.sbmask[:, off:T], ALU.add).then_inc(s_taken, 1)
                        dve.wait_ge(s_taken, s + 1)
                        nc.vector.tensor_scalar(zc[:, j % 2, 0:k], zbuf[:, j % 2, 0:k], SP_CAP, None, ALU.min).then_inc(z_ready, 1)
                        link(nc.vector.tensor_scalar(ex[:, j % 2, 0:k], zbuf[:, j % 2, 0:k], SP_CAP, 0.0, ALU.subtract, ALU.max))
                i = s - 2
                if 0 <= i < N and i % 3 == 2:
                    k, j = keys(i), i // 3
                    dve.wait_ge(l_ready, j + 1)
                    link(nc.vector.tensor_tensor_scan(out=ex[:, j % 2, 0:k][:, ::-1], data0=zc[:, j % 2, 0:k][:, ::-1],
                                                      data1=ex[:, j % 2, 0:k][:, ::-1], initial=0.0, op0=ALU.add, op1=ALU.add))
                    nc.vector.tensor_tensor(zc[:, j % 2, 0:k], zbuf[:, j % 2, 0:k], ex[:, j % 2, 0:k], ALU.subtract).then_inc(w_ready, 1)
                i = s - LAG_V
                if 0 <= i < N and i % 3 == 2:
                    dve.wait_ge(pt_ready, i + 1)
                    if i >= 3:
                        dve.wait_ge(pv, i - 2)
                    nc.vector.tensor_copy(ptsb[:, i % 3, 0:keys(i)], ps_t[i % 2][:, 0:keys(i)]).then_inc(pt_d, 1)
                i = s - LAG_V
                if i >= 0 and i % PER == PER - 1:
                    t = units[i][0]
                    dve.wait_ge(pv, i + 1)
                    gates = b.gate[:, t, :].rearrange("p (h b) -> p h b", b=3)
                    link(nc.vector.reciprocal(fac, b.rows2[:, t % 2]))
                    link(nc.vector.tensor_tensor(fac, fac, gates[:, :, 1:3], ALU.mult))
                    oa = b.oa[:, t, :].rearrange("p (h n) -> p h n", h=HEADS)
                    tm = tmp.rearrange("p (h n) -> p h n", h=HEADS)
                    for kind in range(2):
                        link(nc.vector.tensor_tensor(tm, ps_o[kind][:].rearrange("p (h n) -> p h n", h=HEADS),
                                                     fac[:, :, kind].unsqueeze(2).to_broadcast([P, HEADS, HD]), ALU.mult))
                        link(nc.vector.tensor_tensor(oa, oa, tm, ALU.add))
                    nc.vector.tensor_copy(b.ob[:, t, :], ps_o[2][:]).then_inc(o_moved, 1)

        @block.scalar
        def _(act):
            nc.scalar.preload_act_table_set("natural_log_exp_and_others")
            for s in range(N + LAG_V + 1):
                if s < N:
                    t, h, kind = units[s]
                    k, j = keys(s), s // 3
                    if kind < 2:
                        m = soft_count(s) - 1
                        act.wait_ge(s_taken, s + 1)
                        if s >= 6:
                            act.wait_ge(pt_ready, s - 5)
                        if t >= 2 and s % PER == 0:
                            act.wait_ge(o_moved, t - 1)
                        nc.scalar.activation(prob[:, s % 6, 0:k], ssb[:, m % 2, 0:k], ACT.Exp, scale=-1.0,
                                             bias=negm[:, m % 2:m % 2 + 1],
                                             accum_out=b.rows2[:, t % 2, h, kind:kind + 1]).then_inc(p_soft, 1)
                    else:
                        act.wait_ge(z_ready, j + 1)
                        nc.scalar.activation(zc[:, j % 2, 0:k], zc[:, j % 2, 0:k], ACT.Exp).then_inc(e_done, 1)
                        act.wait_ge(e_done, j + 1)
                        nc.scalar.activation(zc[:, j % 2, 0:k], zc[:, j % 2, 0:k], ACT.Ln, bias=1.0).then_inc(l_ready, 1)
                i = s - 2
                if 0 <= i < N and i % 3 == 2:
                    k, j = keys(i), i // 3
                    act.wait_ge(w_ready, j + 1)
                    if i >= 6:
                        act.wait_ge(pt_ready, i - 5)
                    nc.scalar.activation(prob[:, i % 6, 0:k], zc[:, j % 2, 0:k], ACT.Exp).then_inc(p_stick, 1)
                i = s - LAG_V
                if 0 <= i < N and i % 3 != 2:
                    act.wait_ge(pt_ready, i + 1)
                    if i >= 3:
                        act.wait_ge(pv, i - 2)
                    nc.scalar.copy(ptsb[:, i % 3, 0:keys(i)], ps_t[i % 2][:, 0:keys(i)]).then_inc(pt_a, 1)

        @block.sync
        def _(sp):
            sp.dma_start(b.reg_a[:], b.h_dram).then_inc(b.h_back, 16)


def stage_turn(b, name, jobs, reload=None):
    nc = b.nc
    turned, ev_a, ev_d = (b.sem(f"{name}_{n}") for n in ("turn", "eva", "evd"))
    tiles = [(rows, dst, col, k) for rows, dst, col in jobs for k in range(4)]
    with ExitStack() as ps_ctx:
        ps = [ps_ctx.enter_context(nc.psum_tensor(f"{name}_ps{i}", [P, CH], F32)) for i in range(4)]
        block = ps_ctx.enter_context(nc.Block())

        @block.tensor
        def _(pe):
            for i, (rows, _, _, k) in enumerate(tiles):
                if i >= 4:
                    pe.wait_ge((ev_d, ev_a)[i % 2], (i - 4) // 2 + 1)
                for t in range(NT):
                    mm = nc.tensor.transpose(ps[i % 4][:, t * P:t * P + P], rows[:, t, k * P:k * P + P], b.ident[:])
                mm.then_inc(turned, 1)

        @block.vector
        def _(dve):
            for i in range(0, len(tiles), 2):
                _, dst, col, k = tiles[i]
                dve.wait_ge(turned, i + 1)
                if col is None:
                    nc.vector.tensor_copy(dst[:, k, :], ps[i % 4][:]).then_inc(ev_d, 1)
                else:
                    nc.vector.tensor_scalar(dst[:, k, :], ps[i % 4][:], col[:, k:k + 1], None, ALU.mult).then_inc(ev_d, 1)

        @block.scalar
        def _(act):
            for i in range(1, len(tiles), 2):
                _, dst, col, k = tiles[i]
                act.wait_ge(turned, i + 1)
                nc.scalar.activation(dst[:, k, :], ps[i % 4][:], ACT.Copy, scale=1.0 if col is None else col[:, k:k + 1]).then_inc(ev_a, 1)


def stage_merge(b, name, chunks, yaT, ybT, mT, x_load=None, h_wait=None):
    nc = b.nc
    ready, ev, gates, prod, add_ = (b.sem(f"{name}_{n}") for n in ("ready", "ev", "gates", "prod", "add"))
    sg = b.scr[:, 0:4 * U].rearrange("p (i g n) -> p i g n", i=2, g=2)
    N = 2 * len(chunks)
    with ExitStack() as ps_ctx:
        ps = [[ps_ctx.enter_context(nc.psum_tensor(f"{name}_ps{i}{j}", [P, CH], F32)) for j in range(4)] for i in range(2)]
        block = ps_ctx.enter_context(nc.Block())

        @block.sync
        def _(sp):
            if x_load is not None:
                sp.dma_start(b.x, x_load).then_inc(b.x_in, 16)
            b.load_until(sp, chunks[-1][-1] + 1 + RING)

        @block.tensor
        def _(pe):
            if h_wait is not None:
                pe.wait_ge(h_wait, 16)
            for i in range(N):
                cg, cy = chunks[i // 2]
                n0 = i % 2 * P
                if i % 2 == 0:
                    b.wait_chunk(pe, cg)
                    b.wait_chunk(pe, cy)
                if i >= 2:
                    pe.wait_ge(ev, i - 1)
                bank = ps[i % 2]
                product_T(nc, bank[0][:], b.chunk(cg, 0), n0, b.hT, KD)
                product_T(nc, bank[1][:], b.chunk(cy, 0), n0, yaT, 4)
                product_T(nc, bank[2][:], b.chunk(cg, 1), n0, b.hT, KD)
                product_T(nc, bank[3][:], b.chunk(cy, 1), n0, ybT, 4).then_inc(ready, 1)
                if i % 2:
                    pe.wait_ge(ready, i + 1)
                    nc.tensor.sem_inc(b.ring_used, 2)

        @block.scalar
        def _(act):
            for i in range(N):
                act.wait_ge(ready, i + 1)
                if i >= 2:
                    act.wait_ge(ev, i - 1)
                nc.scalar.activation(sg[:, i % 2, 0], ps[i % 2][0][:], ACT.Sigmoid)
                nc.scalar.activation(sg[:, i % 2, 1], ps[i % 2][2][:], ACT.Sigmoid).then_inc(gates, 1)

        @block.vector
        def _(dve):
            for i in range(N):
                dve.wait_ge(gates, i + 1)
                nc.vector.tensor_tensor(sg[:, i % 2, 0], sg[:, i % 2, 0], ps[i % 2][1][:], ALU.mult)
                nc.vector.tensor_tensor(sg[:, i % 2, 1], sg[:, i % 2, 1], ps[i % 2][3][:], ALU.mult).then_inc(prod, 1)
                dve.wait_ge(prod, i + 1)
                nc.vector.tensor_tensor(mT[:, i, :], sg[:, i % 2, 0], sg[:, i % 2, 1], ALU.add).then_inc(ev, 1)


def stage_rows_out(b, name, srcT, chunks, gate_row=None):
    nc = b.nc
    ready, ev, prod = (b.sem(f"{name}_{n}") for n in ("ready", "ev", "prod"))
    kt = max(c[2] for c in chunks)
    tmp = b.scr[:, 0:4 * U].rearrange("p (i n) -> p i n", i=4)
    with ExitStack() as ps_ctx:
        ps = [ps_ctx.enter_context(nc.psum_tensor(f"{name}_ps{i}", [P, CH], F32)) for i in range(8)]
        block = ps_ctx.enter_context(nc.Block())

        @block.sync
        def _(sp):
            b.load_until(sp, chunks[-1][-1] + 1 + RING)

        @block.tensor
        def _(pe):
            for h, k0, k1, c in chunks:
                b.wait_chunk(pe, c)
                w = b.chunk(c)
                for t in range(NT):
                    for k in range(k0, k1):
                        mm = nc.tensor.matmul(ps[h * NT + t][:], srcT[:, k, t * P:t * P + P], w[:, k - k0, :],
                                              start=(k == 0), stop=(k == kt - 1))
                    mm.then_inc(ready, 1)
                pe.wait_ge(ready, NT * (chunks.index((h, k0, k1, c)) + 1))
                nc.tensor.sem_inc(b.ring_used, 1)

        @block.vector
        def _(dve):
            per = len(chunks) // 2
            n = 0
            for h in range(2):
                cols = slice(h * CH, h * CH + CH)
                for t in range(NT):
                    dve.wait_ge(ready, NT * (per * (h + 1) - 1) + t + 1)
                    src = ps[h * NT + t][:]
                    if gate_row is not None:
                        if n >= 4:
                            dve.wait_ge(ev, n - 3)
                        nc.vector.tensor_tensor(tmp[:, n % 4], src, gate_row[:, cols], ALU.mult).then_inc(prod, 1)
                        dve.wait_ge(prod, n + 1)
                        src = tmp[:, n % 4]
                    nc.vector.tensor_tensor(b.x[:, t, cols], b.x[:, t, cols], src, ALU.add).then_inc(ev, 1)
                    n += 1


def stage_ffn_up(b):
    nc = b.nc
    guT = b.s_ab[:, 0:KF * T].rearrange("p (k t) -> p k t", k=KF)
    ready, silu, ev = (b.sem(f"up_{n}") for n in ("ready", "silu", "ev"))
    with ExitStack() as ps_ctx:
        ps = [[ps_ctx.enter_context(nc.psum_tensor(f"up_ps{i}{j}", [P, CH], F32)) for j in range(2)] for i in range(4)]
        block = ps_ctx.enter_context(nc.Block())

        @block.sync
        def _(sp):
            b.load_until(sp, b.c_ffn[-1] + 1 + RING)

        @block.tensor
        def _(pe):
            for i in range(KF):
                c = b.c_ffn[i // 2]
                if i % 2 == 0:
                    b.wait_chunk(pe, c)
                if i >= 4:
                    pe.wait_ge(ev, i - 3)
                product_T(nc, ps[i % 4][0][:], b.chunk(c, 0), i % 2 * P, b.hT, KD)
                product_T(nc, ps[i % 4][1][:], b.chunk(c, 1), i % 2 * P, b.hT, KD).then_inc(ready, 1)
                if i % 2:
                    pe.wait_ge(ready, i + 1)
                    nc.tensor.sem_inc(b.ring_used, 1)

        @block.scalar
        def _(act):
            for i in range(KF):
                act.wait_ge(ready, i + 1)
                nc.scalar.activation(guT[:, i, :], ps[i % 4][0][:], ACT.Silu).then_inc(silu, 1)

        @block.vector
        def _(dve):
            for i in range(KF):
                dve.wait_ge(silu, i + 1)
                nc.vector.tensor_tensor(guT[:, i, :], guT[:, i, :], ps[i % 4][1][:], ALU.mult).then_inc(ev, 1)
    return guT


def stage_project2(b):
    nc = b.nc

    def four(u0, inner):
        return b.s_ab[:, u0 * U:(u0 + 4) * U].rearrange("p (a n) -> p a n", a=4)
    b.gu, b.gv, b.hqT, b.hfT, b.hi, b.hog = (four(4 * i, 4) for i in range(6))
    kinds = [(b.gu, ACT.Gelu_apprx_tanh, False), (b.gv, ACT.Gelu_apprx_tanh, False), (b.hqT, ACT.Silu, True),
             (b.hfT, ACT.Sigmoid, True), (b.hog, ACT.Sigmoid, False), (b.hi, ACT.Copy, False)]
    order = [0, 1, 2, 3, 5, 4]
    ready, ev, zero, filled = (b.sem(f"p2_{n}") for n in ("ready", "ev", "zero", "filled"))
    b.y_dram = nc.dram_tensor("slot_rows", (SLOTS, D), F32).ap()
    zeros = b.u_big[:, 0:D]
    with ExitStack() as ps_ctx:
        ps = [ps_ctx.enter_context(nc.psum_tensor(f"p2_ps{i}", [P, CH], F32)) for i in range(4)]
        block = ps_ctx.enter_context(nc.Block())

        @block.sync
        def _(sp):
            sp.wait_ge(zero, 1)
            sp.dma_start(b.y_dram[PAIRS * P:, :].rearrange("(i p) d -> p i d", p=P),
                         zeros.unsqueeze(1).to_broadcast([P, SPILL, D])).then_inc(filled, 16)
            b.load_until(sp, b.c_in2[-1] + 1 + RING)
            sp.wait_ge(filled, 16)

        @block.gpsimd
        def _(pool):
            nc.gpsimd.memset(zeros, 0.0).then_inc(zero, 1)

        @block.tensor
        def _(pe):
            for i in range(24):
                c = b.c_in2[i // 4]
                if i % 4 == 0:
                    b.wait_chunk(pe, c)
                if i >= 4:
                    pe.wait_ge(ev, i - 3)
                if kinds[order[i // 4]][2]:
                    mm = product_T(nc, ps[i % 4][:], b.chunk(c), i % 4 * P, b.hT, KD)
                else:
                    mm = product_rows(nc, ps[i % 4][:], b.hT, i % 4, b.chunk(c), KD)
                mm.then_inc(ready, 1)
                if i % 4 == 3:
                    pe.wait_ge(ready, i + 1)
                    nc.tensor.sem_inc(b.ring_used, 1)

        @block.scalar
        def _(act):
            for i in range(24):
                dst, func, _ = kinds[order[i // 4]]
                act.wait_ge(ready, i + 1)
                nc.scalar.activation(dst[:, i % 4, :], ps[i % 4][:], func).then_inc(ev, 1)


def stage_gmlp(b):
    nc, a = b.nc, b.a
    DG = CH // GM_GROUPS
    u, v = b.gu, b.gv
    lnrow = b.scr[:, 0:2 * U].rearrange("p (i n) -> p i n", i=2)
    wT = b.scr[:, 2 * U:4 * U].rearrange("p (g t) -> p g t", g=GM_GROUPS)
    w = b.w1flat[:, 0:2 * U].rearrange("p (g s) -> p g s", g=GM_GROUPS)
    sq = b.u_big[:, 0:4 * U].rearrange("p (t n) -> p t n", t=NT)
    st = b.small
    b.tri = b.sb("tri", [P, P])
    loads, pool, chain, squared, root, turned, wmask, normed, ready = (
        b.sem(f"gm_{n}") for n in ("loads", "pool", "chain", "sq", "root", "turn", "wmask", "normed", "ready"))
    with ExitStack() as ps_ctx:
        pw = [ps_ctx.enter_context(nc.psum_tensor(f"gm_w{i}", [P, CH], F32)) for i in range(2)]
        ps = [ps_ctx.enter_context(nc.psum_tensor(f"gm_ps{i}", [P, CH], F32)) for i in range(4)]
        block = ps_ctx.enter_context(nc.Block())

        @block.sync
        def _(sp):
            sp.dma_start(w, a["gm_w_sp_2"][0].rearrange("g t s -> t g s")).then_inc(loads, 16)
            for i, n in enumerate(("gm_ln_g_2", "gm_ln_b_2")):
                sp.dma_start(lnrow[:, i], a[n].partition_broadcast(P).rearrange("p o n -> p (o n)")).then_inc(loads, 16)

        @block.gpsimd
        def _(g):
            nc.gpsimd.memset(b.tri[:], 1.0).then_inc(pool, 1)
            g.wait_ge(pool, 1)
            nc.gpsimd.affine_select(out=b.tri[:], in_=b.tri[:], compare_op=ALU.is_ge, fill=0.0, base=0,
                                    pattern=[[1, P]], channel_multiplier=-1).then_inc(pool, 1)

        @block.tensor
        def _(pe):
            pe.wait_ge(loads, 48)
            for g in range(GM_GROUPS):
                mm = nc.tensor.transpose(pw[g // 4][:, g % 4 * P:g % 4 * P + P], w[:, g, :], b.ident[:])
            mm.then_inc(turned, 1)
            pe.wait_ge(wmask, 1)
            pe.wait_ge(normed, 1)
            for g in range(GM_GROUPS):
                o = ps[g // 2][:, g % 2 * 4 * DG:(g % 2 + 1) * 4 * DG].rearrange("p (c n) -> p c n", c=NT)
                mm = nc.tensor.matmul(o, wT[:, g, :], v[:, :, g * DG:(g + 1) * DG], start=True, stop=True)
                mm.then_inc(ready, 1)

        @block.scalar
        def _(act):
            act.wait_ge(chain, 6)
            for t in range(NT):
                last = nc.scalar.activation(sq[:, t, :], v[:, t, :], ACT.Square, accum_out=st[:, 8 + t:9 + t])
            last.then_inc(squared, 1)
            act.wait_ge(chain, 7)
            nc.scalar.activation(st[:, 8:12], st[:, 8:12], ACT.Sqrt).then_inc(root, 1)

        @block.vector
        def _(dve):
            n = [0]

            def link(ins):
                n[0] += 1
                ins.then_inc(chain, 1)
                dve.wait_ge(chain, n[0])

            link(nc.vector.tensor_reduce(st[:, 0:4], v, AX.X, ALU.add))
            link(nc.vector.tensor_scalar(st[:, 4:8], st[:, 0:4], 1.0 / CH, None, ALU.mult))
            for t in range(NT):
                link(nc.vector.tensor_scalar(v[:, t, :], v[:, t, :], st[:, 4 + t:5 + t], None, ALU.subtract))
            dve.wait_ge(squared, 1)
            link(nc.vector.tensor_scalar(st[:, 8:12], st[:, 8:12], 1.0 / CH, EPS, ALU.mult, ALU.add))
            dve.wait_ge(root, 1)
            link(nc.vector.reciprocal(st[:, 12:16], st[:, 8:12]))
            dve.wait_ge(loads, 48)
            for t in range(NT):
                last = nc.vector.scalar_tensor_tensor(out=v[:, t, :], in0=v[:, t, :], scalar=st[:, 12 + t:13 + t],
                                                      in1=lnrow[:, 0], op0=ALU.mult, op1=ALU.mult)
            link(last)
            nc.vector.tensor_tensor(v, v, lnrow[:, 1:2, :].to_broadcast([P, NT, CH]), ALU.add).then_inc(normed, 1)
            dve.wait_ge(turned, 1)
            dve.wait_ge(pool, 2)
            for i in range(2):
                last = nc.vector.tensor_tensor(wT[:, 4 * i:4 * i + 4, :], pw[i][:].rearrange("p (g t) -> p g t", g=4),
                                               b.tri[:].unsqueeze(1).to_broadcast([P, 4, P]), ALU.mult)
            last.then_inc(wmask, 1)
            for g in range(GM_GROUPS):
                dve.wait_ge(ready, g // 2 * 2 + 2)
                o = ps[g // 2][:, g % 2 * 4 * DG:(g % 2 + 1) * 4 * DG].rearrange("p (c n) -> p c n", c=NT)
                us = u[:, :, g * DG:(g + 1) * DG]
                bias = b.vcol[:, VAT["gm_b_sp_2"] + g:VAT["gm_b_sp_2"] + g + 1]
                nc.vector.scalar_tensor_tensor(out=us, in0=o, scalar=bias, in1=us, op0=ALU.add, op1=ALU.mult)


def stage_hgrn(b):
    nc = b.nc
    NCH = T // HG_CHUNK
    qT, fT, vrows, og = b.hqT, b.hfT, b.hi, b.hog

    def four(reg, u0):
        return reg[:, u0 * U:(u0 + 4) * U].rearrange("p (h t) -> p h t", h=4)
    kT, bT, eb = four(b.u_big, 0), four(b.u_big, 4), four(b.u_big, 8)
    kend, kinv = four(b.s_ab, 0), four(b.s_ab, 4)
    kerows = four(b.u_big, 0)
    attm = four(b.u_big, 4)
    state = [b.u_big[:, (8 + i) * U:(9 + i) * U] for i in range(4)] + [b.s_ab[:, (12 + i) * U:(13 + i) * U] for i in range(4)]
    reset = b.u_big[:, 12 * U:13 * U]
    st = b.small
    lb, omlb, e0, e1, dec = st[:, 0:4], st[:, 4:8], st[:, 8:12], st[:, 12:16], st[:, 16:48].rearrange("p (h c) -> p h c", h=4)
    ss = b.rows2[:].rearrange("p a h b -> p (a h b)")[:, 0:16]
    bmask = b.sb("hg_mask", [P, P], I32)
    bmf = b.scr[:, 0:P]
    sqj = b.scr[:, U:2 * U]
    sem = {n: b.sem(f"hg_{n}") for n in ("pool", "lb", "chain", "f", "ln", "b", "eb", "enb", "kd", "kde", "turn", "ev",
                                         "att", "attm", "ds", "s", "o", "sq", "var", "root", "act", "zero", "y", "bm")}
    l0 = b.vcol[:, VAT["hg_lb_param_2"]:VAT["hg_lb_param_2"] + 4]
    l1 = b.vcol[:, VAT["hg_lb_param_2"] + 4:VAT["hg_lb_param_2"] + 8]

    def per_chunk(x, h=None):
        return x.rearrange("p h (c t) -> p h c t", c=NCH) if h is None else x[:, h, :].rearrange("p (c t) -> p c t", c=NCH)

    with ExitStack() as ps_ctx:
        ps = [ps_ctx.enter_context(nc.psum_tensor(f"hg_ps{i}", [P, CH], F32)) for i in range(8)]
        block = ps_ctx.enter_context(nc.Block())

        @block.gpsimd
        def _(g):
            nc.gpsimd.memset(bmf, 1.0).then_inc(sem["pool"], 1)
            g.wait_ge(sem["pool"], 1)
            nc.gpsimd.affine_select(out=bmf, in_=bmf, compare_op=ALU.is_ge, fill=0.0, base=0,
                                    pattern=[[1, P]], channel_multiplier=-1).then_inc(sem["pool"], 1)
            g.wait_ge(sem["pool"], 2)
            nc.gpsimd.memset(bmf[0:64, 64:128], 0.0).then_inc(sem["pool"], 1)
            g.wait_ge(sem["pool"], 3)
            nc.gpsimd.tensor_copy(bmask[:], bmf).then_inc(sem["bm"], 1)

        @block.vector
        def _(dve):
            n = [0]

            def link(ins, by="chain"):
                n[0] += 1
                ins.then_inc(sem["chain"], 1)
                dve.wait_ge(sem["chain"], n[0])

            nc.vector.memset(reset, 1.0).then_inc(sem["zero"], 1)
            dve.wait_ge(sem["zero"], 1)
            link(nc.vector.memset(reset.rearrange("p (c t) -> p c t", c=NCH)[:, :, 0:1], 0.0))
            link(nc.vector.tensor_tensor(lb, l0, l1, ALU.max))
            link(nc.vector.tensor_tensor(e0, l0, lb, ALU.subtract))
            nc.vector.tensor_tensor(e1, l1, lb, ALU.subtract).then_inc(sem["lb"], 1)
            dve.wait_ge(sem["act"], 1)
            link(nc.vector.tensor_tensor(e1, e0, e1, ALU.add))
            link(nc.vector.reciprocal(e1, e1))
            link(nc.vector.tensor_tensor(lb, e0, e1, ALU.mult))
            link(nc.vector.tensor_scalar(omlb, lb, -1.0, 1.0, ALU.mult, ALU.add))
            for h in range(HG_HEADS):
                nc.vector.tensor_scalar(fT[:, h, :], fT[:, h, :], omlb[:, h:h + 1], lb[:, h:h + 1], ALU.mult, ALU.add).then_inc(sem["f"], 1)
            dve.wait_ge(sem["f"], 4)
            nc.vector.tensor_scalar(kT, fT, -1.0, 1.0, ALU.mult, ALU.add).then_inc(sem["kd"], 1)
            for h in range(HG_HEADS):
                dve.wait_ge(sem["ln"], h + 1)
                nc.vector.tensor_tensor_scan(out=bT[:, h, :], data0=reset, data1=fT[:, h, :], initial=0.0,
                                             op0=ALU.mult, op1=ALU.add).then_inc(sem["b"], 1)
            dve.wait_ge(sem["b"], 4)
            for h in range(HG_HEADS):
                bc = per_chunk(bT, h)
                nc.vector.tensor_tensor(per_chunk(fT, h), bc[:, :, HG_CHUNK - 1:HG_CHUNK].to_broadcast([P, NCH, HG_CHUNK]), bc,
                                        ALU.subtract).then_inc(sem["kde"], 1)
            dve.wait_ge(sem["eb"], 1)
            nc.vector.tensor_tensor(qT, qT, eb, ALU.mult)
            nc.vector.tensor_copy(dec, eb.rearrange("p h (c t) -> p h c t", c=NCH)[:, :, :, HG_CHUNK - 1]).then_inc(sem["kd"], 1)
            dve.wait_ge(sem["enb"], 1)
            nc.vector.tensor_tensor(kinv, kinv, kT, ALU.mult).then_inc(sem["kd"], 1)
            dve.wait_ge(sem["enb"], 2)
            nc.vector.tensor_tensor(kend, fT, kT, ALU.mult).then_inc(sem["kd"], 1)
            link(nc.vector.memset(attm, 0.0))
            for t in range(NT):
                dve.wait_ge(sem["turn"], t + 1)
                nc.vector.tensor_copy(kerows[:, t, :], ps[t][:]).then_inc(sem["ev"], 1)
            dve.wait_ge(sem["bm"], 1)
            for t in range(NT):
                dve.wait_ge(sem["att"], t + 1)
                for h in range(HG_HEADS):
                    last = nc.vector.copy_predicated(attm[:, t, h * P:h * P + P], bmask[:], ps[4 + t][:, h * P:h * P + P])
                last.then_inc(sem["attm"], 1)
            for c in range(NCH - 1):
                dve.wait_ge(sem["ds"], c + 1)
                if c == 0:
                    last = nc.vector.tensor_copy(state[0], ps[0][:])
                else:
                    dve.wait_ge(sem["s"], c)
                    for h in range(HG_HEADS):
                        r = slice(h * P, h * P + P)
                        last = nc.vector.scalar_tensor_tensor(out=state[c][:, r], in0=state[c - 1][:, r], scalar=dec[:, h, c:c + 1],
                                                              in1=ps[c % 2][:, r], op0=ALU.mult, op1=ALU.add)
                last.then_inc(sem["s"], 1)
            dve.wait_ge(sem["sq"], 4)
            link(nc.vector.tensor_scalar(ss, ss, 1.0 / P, EPS, ALU.mult, ALU.add))
            nc.vector.sem_inc(sem["var"], 1)
            dve.wait_ge(sem["root"], 1)
            link(nc.vector.reciprocal(ss, ss))
            for t in range(NT):
                for h in range(HG_HEADS):
                    r = slice(h * P, h * P + P)
                    nc.vector.scalar_tensor_tensor(out=og[:, t, r], in0=ps[(2, 3, 4, 5)[t]][:, r], scalar=ss[:, 4 * t + h:4 * t + h + 1],
                                                   in1=og[:, t, r], op0=ALU.mult, op1=ALU.mult)

        @block.scalar
        def _(act):
            act.wait_ge(sem["lb"], 1)
            nc.scalar.preload_act_table_set("natural_log_exp_and_others")
            nc.scalar.activation(st[:, 8:16], st[:, 8:16], ACT.Exp).then_inc(sem["act"], 1)
            act.wait_ge(sem["kd"], 1)
            for h in range(HG_HEADS):
                nc.scalar.activation(fT[:, h, :], fT[:, h, :], ACT.Ln).then_inc(sem["ln"], 1)
            act.wait_ge(sem["b"], 4)
            nc.scalar.activation(eb, bT, ACT.Exp).then_inc(sem["eb"], 1)
            nc.scalar.activation(kinv, bT, ACT.Exp, scale=-1.0).then_inc(sem["enb"], 1)
            act.wait_ge(sem["kde"], 4)
            nc.scalar.activation(fT, fT, ACT.Exp).then_inc(sem["enb"], 1)
            for t in range(NT):
                act.wait_ge(sem["o"], t + 1)
                if t:
                    act.wait_ge(sem["sq"], t)
                for h in range(HG_HEADS):
                    r = slice(h * P, h * P + P)
                    last = nc.scalar.activation(sqj[:, r], ps[(2, 3, 4, 5)[t]][:, r], ACT.Square, accum_out=ss[:, 4 * t + h:4 * t + h + 1])
                last.then_inc(sem["sq"], 1)
            act.wait_ge(sem["var"], 1)
            nc.scalar.activation(ss, ss, ACT.Sqrt).then_inc(sem["root"], 1)

        @block.tensor
        def _(pe):
            pe.wait_ge(sem["kd"], 4)
            for t in range(NT):
                for h in range(HG_HEADS):
                    mm = nc.tensor.transpose(ps[t][:, h * P:h * P + P], kend[:, h, t * P:t * P + P], b.ident[:])
                mm.then_inc(sem["turn"], 1)
            for t in range(NT):
                for h in range(HG_HEADS):
                    r = slice(t * P, t * P + P)
                    mm = nc.tensor.matmul(ps[4 + t][:, h * P:h * P + P], kinv[:, h, r], qT[:, h, r], start=True, stop=True)
                mm.then_inc(sem["att"], 1)
            pe.wait_ge(sem["ev"], 4)
            for c in range(NCH - 1):
                r = slice(64 * (c % 2), 64 * (c % 2) + 64)
                if c >= 2:
                    pe.wait_ge(sem["s"], c - 1)
                for h in range(HG_HEADS):
                    k = slice(h * P, h * P + P)
                    mm = nc.tensor.matmul(ps[c % 2][:, k], kerows[r, c // 2, k], vrows[r, c // 2, k], start=True, stop=True)
                mm.then_inc(sem["ds"], 1)
            pe.wait_ge(sem["attm"], 4)
            pe.wait_ge(sem["s"], NCH - 1)
            for t in range(NT):
                bank = ps[(2, 3, 4, 5)[t]]
                for h in range(HG_HEADS):
                    k = slice(h * P, h * P + P)
                    for j in range(2):
                        c, o = 2 * t + j, bank[64 * j:64 * j + 64, k]
                        if c:
                            nc.tensor.matmul(o, qT[:, h, c * HG_CHUNK:(c + 1) * HG_CHUNK], state[c - 1][:, k], start=True, stop=False)
                        mm = nc.tensor.matmul(o, attm[:, t, h * P + 64 * j:h * P + 64 * j + 64], vrows[:, t, k],
                                              start=(c == 0), stop=True)
                mm.then_inc(sem["o"], 1)


def stage_router(b):
    nc, a = b.nc, b.a
    at = [0]

    def take(*shape):
        n = int(np.prod(shape))
        v = b.w1flat[:, at[0]:at[0] + n]
        at[0] += n
        if len(shape) == 2:
            v = v.rearrange("p (a b) -> p a b", a=shape[0])
        return v
    b.slot = b.sb("slot", [P, 2 * NT], U32)
    b.weight = b.sb("weight", [P, 2 * NT])
    b.tok = b.sb("tok", [P, SLOTS // P], U32)
    b.spill = b.sb("spill", [P, SPILL + 1], I32)
    b.tok_dram = nc.dram_tensor("tok_list", (SLOTS, 1), F32).ap()
    NE = EGROUPS + EXPERTS
    wr = b.scr[:, 0:KD * NE].rearrange("p (k n) -> p k n", k=KD)
    io32, lg, tg, ohg = take(EXPERTS), take(NT, NE), take(NT, EGROUPS), take(NT, EGROUPS)
    eg, sel, oh1, oh2, m, tt = take(NT, EGROUPS), *(take(NT, EXPERTS) for _ in range(5))
    rank, over, cnt, X, Xi, A, B, tokid = take(NT, EXPERTS), take(NT, EXPERTS), *(take(EXPERTS) for _ in range(5)), take(NT)
    (mg, pg, m1, m2, e2, r2, s1), slotf = (take(NT) for _ in range(7)), take(2 * NT)
    before = take(P)
    spf, cmp_ = take(SPILL), take(SPILL, EXPERTS)
    io16 = take(SPILL)
    zeros = take(P)
    toks = take(P)
    loads, pool, sel_ = b.sem("ro_loads"), b.sem("ro_pool"), b.sem("ro_sel")
    logits, chain, expin, expd, ranks, masks, slots_, scat, back, tt_, zero, turned, nsc = (
        b.sem(f"ro_{n}") for n in ("logits", "chain", "expin", "expd", "ranks", "masks", "slots", "scat", "back", "tt",
                                   "zero", "turned", "nsc"))
    with ExitStack() as ps_ctx:
        ps_l, ps_r, ps_t = (ps_ctx.enter_context(nc.psum_tensor(f"ro_{n}", [P, CH], F32)) for n in "lrt")
        block = ps_ctx.enter_context(nc.Block())

        @block.sync
        def _(sp):
            sp.dma_start(wr[:, :, 0:EGROUPS], feature_tiles(a["w_grp_2"][0], 0, EGROUPS)).then_inc(loads, 16)
            sp.dma_start(wr[:, :, EGROUPS:NE], feature_tiles(a["w_exp_2"][0], 0, EXPERTS)).then_inc(loads, 16)
            sp.wait_ge(pool, 7)
            sp.dma_start(b.tok_dram.rearrange("(b s) o -> b (s o)", s=P), zeros[0:SLOTS // P, :]).then_inc(zero, 16)
            sp.wait_ge(scat, 16 * 2 * NT)
            sp.dma_start(toks[0:SLOTS // P, :], b.tok_dram.rearrange("(b s) o -> b (s o)", s=P)).then_inc(back, 16)

        @block.gpsimd
        def _(g):
            def iota(out, pattern, cm=0, base=0):
                nc.gpsimd.iota(out, pattern=pattern, base=base, channel_multiplier=cm,
                               allow_small_or_imprecise_dtypes=True).then_inc(pool, 1)
            iota(io32, [[1, EXPERTS]])
            iota(A, [[CAP, EXPERTS]])
            iota(tokid, [[P, NT]], cm=1)
            iota(io16, [[1, SPILL]])
            nc.gpsimd.memset(before, 1.0).then_inc(pool, 1)
            g.wait_ge(pool, 5)
            nc.gpsimd.affine_select(out=before, in_=before, compare_op=ALU.is_gt, fill=0.0, base=0,
                                    pattern=[[1, P]], channel_multiplier=-1).then_inc(pool, 1)
            nc.gpsimd.memset(zeros, 0.0).then_inc(pool, 1)
            g.wait_ge(slots_, 1)
            g.wait_ge(zero, 16)
            for i in range(2 * NT):
                nc.gpsimd.indirect_dma_start(b.tok_dram, bass.IndirectOffsetOnAxis(b.slot[:, i:i + 1], 0),
                                             tokid[:, i % NT:i % NT + 1], None).then_inc(scat, 16)

        @block.tensor
        def _(pe):
            pe.wait_ge(loads, 32)
            for t in range(NT):
                mm = product_rows(nc, ps_l[:, t * NE:(t + 1) * NE], b.hT, t, wr, KD)
            mm.then_inc(logits, 1)
            pe.wait_ge(pool, 7)
            pe.wait_ge(masks, 1)
            for t in range(NT):
                for u in range(t + 1):
                    mm = nc.tensor.matmul(ps_r[:, t * EXPERTS:(t + 1) * EXPERTS], before if u == t else b.ones[:], m[:, u, :],
                                          start=(u == 0), stop=(u == t))
            for u in range(NT):
                mm = nc.tensor.matmul(ps_r[:, NT * EXPERTS:(NT + 1) * EXPERTS], b.ones[:], m[:, u, :], start=(u == 0), stop=(u == NT - 1))
            mm.then_inc(ranks, 1)
            pe.wait_ge(back, 16)
            nc.tensor.transpose(ps_t[:, 0:SLOTS // P], toks[0:SLOTS // P, :], b.ident[0:SLOTS // P, 0:SLOTS // P]).then_inc(turned, 1)

        @block.scalar
        def _(act):
            act.wait_ge(expin, 1)
            nc.scalar.activation(eg, eg, ACT.Exp).then_inc(expd, 1)
            act.wait_ge(expin, 2)
            nc.scalar.activation(e2, e2, ACT.Exp).then_inc(expd, 1)

        @block.vector
        def _(dve):
            n = [0]

            def link(ins):
                n[0] += 1
                ins.then_inc(chain, 1)
                dve.wait_ge(chain, n[0])

            def wide(v, k):
                return v.unsqueeze(2).to_broadcast([P, NT, k])

            def first_max(values, k, best, onehot):
                link(nc.vector.tensor_reduce(best, values, AX.X, ALU.max))
                link(nc.vector.tensor_tensor(onehot, values, wide(best, k), ALU.is_ge))
                link(nc.vector.scalar_tensor_tensor(out=onehot, in0=onehot, scalar=-64.0, in1=io32[:, 0:k].unsqueeze(1).to_broadcast([P, NT, k]),
                                                    op0=ALU.mult, op1=ALU.add))
                link(nc.vector.tensor_reduce(s1, onehot, AX.X, ALU.min))
                link(nc.vector.tensor_tensor(onehot, onehot, wide(s1, k), ALU.is_equal))

            dve.wait_ge(pool, 7)
            dve.wait_ge(logits, 1)
            link(nc.vector.tensor_copy(lg, ps_l[:, 0:NT * NE].rearrange("p (t n) -> p t n", t=NT)))
            gl, el = lg[:, :, 0:EGROUPS], lg[:, :, EGROUPS:NE]
            first_max(gl, EGROUPS, mg, ohg)
            nc.vector.tensor_tensor(eg, gl, wide(mg, EGROUPS), ALU.subtract).then_inc(expin, 1)
            link(nc.vector.tensor_scalar(tg, ohg, 1.0, 1e30, ALU.subtract, ALU.mult))
            for t in range(NT):
                last = nc.vector.tensor_tensor(sel[:, t, :].rearrange("p (g e) -> p g e", g=EGROUPS), el[:, t, :].rearrange("p (g e) -> p g e", g=EGROUPS),
                                               tg[:, t, :].unsqueeze(2).to_broadcast([P, EGROUPS, EPG]), ALU.add)
            link(last)
            first_max(sel, EXPERTS, m1, oh1)
            link(nc.vector.scalar_tensor_tensor(out=sel, in0=oh1, scalar=-3e30, in1=sel, op0=ALU.mult, op1=ALU.add))
            first_max(sel, EXPERTS, m2, oh2)
            nc.vector.tensor_tensor(m, oh1, oh2, ALU.add).then_inc(masks, 1)
            nc.vector.tensor_tensor(e2, m2, m1, ALU.subtract).then_inc(expin, 1)
            dve.wait_ge(expd, 2)
            link(nc.vector.tensor_reduce(pg, eg, AX.X, ALU.add))
            link(nc.vector.tensor_scalar(r2, e2, 1.0, None, ALU.add))
            link(nc.vector.tensor_tensor(r2, r2, pg, ALU.mult))
            link(nc.vector.reciprocal(b.weight[:, 0:NT], r2))
            nc.vector.tensor_tensor(b.weight[:, NT:2 * NT], b.weight[:, 0:NT], e2, ALU.mult)
            dve.wait_ge(ranks, 1)
            nc.vector.tensor_copy(rank, ps_r[:, 0:NT * EXPERTS].rearrange("p (t n) -> p t n", t=NT))
            link(nc.vector.tensor_copy(cnt, ps_r[:, NT * EXPERTS:(NT + 1) * EXPERTS]))
            link(nc.vector.tensor_scalar(X, cnt, float(CAP), None, ALU.is_gt))
            for more in range(CAP + P, T, P):
                link(nc.vector.scalar_tensor_tensor(out=X, in0=cnt, scalar=float(more), in1=X, op0=ALU.is_gt, op1=ALU.add))
            link(nc.vector.tensor_tensor_scan(out=Xi, data0=X, data1=X, initial=0.0, op0=ALU.add, op1=ALU.bypass))
            link(nc.vector.tensor_tensor(B, Xi, X, ALU.subtract))
            link(nc.vector.tensor_scalar(B, B, float(P), float(PAIRS * P - CAP), ALU.mult, ALU.add))
            link(nc.vector.tensor_tensor(B, B, A, ALU.subtract))
            link(nc.vector.tensor_scalar(over, rank, float(CAP), None, ALU.is_ge))
            wideA, wideB = (v.unsqueeze(1).to_broadcast([P, NT, EXPERTS]) for v in (A, B))
            link(nc.vector.tensor_tensor(over, over, wideB, ALU.mult))
            link(nc.vector.tensor_tensor(over, over, rank, ALU.add))
            link(nc.vector.tensor_tensor(over, over, wideA, ALU.add))
            for k, oh in enumerate((oh1, oh2)):
                link(nc.vector.tensor_tensor(tt, oh, over, ALU.mult))
                link(nc.vector.tensor_reduce(slotf[:, k * NT:(k + 1) * NT], tt, AX.X, ALU.add))
            nc.vector.tensor_copy(b.slot[:], slotf).then_inc(slots_, 1)
            link(nc.vector.tensor_tensor(cmp_, Xi.unsqueeze(1).to_broadcast([P, SPILL, EXPERTS]),
                                         io16.unsqueeze(2).to_broadcast([P, SPILL, EXPERTS]), ALU.is_le))
            link(nc.vector.tensor_reduce(spf, cmp_, AX.X, ALU.add))
            link(nc.vector.tensor_scalar(spf, spf, float(EXPERTS - 1), None, ALU.min))
            nc.vector.tensor_copy(b.spill[:, 0:SPILL], spf)
            nc.vector.tensor_copy(b.spill[:, SPILL:SPILL + 1], Xi[:, EXPERTS - 1:EXPERTS])
            dve.wait_ge(turned, 1)
            nc.vector.tensor_copy(b.tok[:], ps_t[:, 0:SLOTS // P])


def expert_buffers(b):
    b.wslot = [b.ring[:, i] for i in range(RING)] + [b.w1flat[:], b.s_ab[:, 0:8 * U]]
    b.xg = b.s_ab[:, 8 * U:10 * U]
    b.xT = b.s_ab[:, 10 * U:12 * U].rearrange("p (k s) -> p k s", k=KD)
    b.hs, b.hm = b.s_ab[:, 12 * U:13 * U], b.s_ab[:, 13 * U:14 * U]
    b.ys = b.s_ab[:, 14 * U:18 * U].rearrange("p (j n) -> p j n", j=2)
    b.gcol = b.vcol[:, VAT["g_ffn_2"]:VAT["g_ffn_2"] + KD].unsqueeze(2).to_broadcast([P, KD, P])


def weight_views(b, j):
    w1, w3, w2 = b.wslot[3 * j:3 * j + 3]
    return (w1.rearrange("p (k n) -> p k n", k=KD), w3.rearrange("p (k n) -> p k n", k=KD), w2.rearrange("p (k n) -> p k n", k=KE))


def expert_weights(b, e):
    w1, w3, w2 = (b.a[n][0][bass.ds(e, 1)] for n in ("w1_2", "w3_2", "w2_2"))
    return (w1.rearrange("o (k p) n -> p (o k) n", p=P), w3.rearrange("o (k p) n -> p (o k) n", p=P),
            w2.rearrange("o (k p) n -> p (o k) n", p=P))


def turn_rows(nc, ps, xg, ident):
    for k in range(KD):
        mm = nc.tensor.transpose(ps[k // 4][:, k % 4 * P:k % 4 * P + P], xg[:, k * P:(k + 1) * P], ident)
    return mm


def rows_in(nc, b, ps):
    for i in range(2):
        last = nc.vector.tensor_tensor(b.xT[:, 4 * i:4 * i + 4, :], ps[i][:].rearrange("p (k s) -> p k s", k=4),
                                       b.gcol[:, 4 * i:4 * i + 4, :], ALU.mult)
    return last


def expert_in(nc, ps, w, xT, n):
    for i in range(2):
        for f in range(KE):
            for k in range(KD):
                mm = nc.tensor.matmul(ps[i][:, f * n:(f + 1) * n], w[i][:, k, f * P:f * P + P], xT[:, k, :],
                                      start=(k == 0), stop=(k == KD - 1))
    return mm


def expert_out(nc, ps, w2, hm, n):
    for h in range(2):
        for f in range(KE):
            mm = nc.tensor.matmul(ps[h][0:n, :], hm[:, f * n:(f + 1) * n], w2[:, f, h * CH:(h + 1) * CH],
                                  start=(f == 0), stop=(f == KE - 1))
    return mm


def stage_experts(b):
    nc = b.nc
    wfull = [b.sem(f"ex_w{i}") for i in range(6)]
    yout = [b.sem(f"ex_out{i}") for i in range(2)]
    xfull, turned, xt, h_done, silu, hm, y_done, y0, y1 = (
        b.sem(f"ex_{n}") for n in ("x", "turn", "xt", "h", "silu", "hm", "y", "y0", "y1"))
    half = [slice(j * KE * CAP, (j + 1) * KE * CAP) for j in range(2)]
    last = PAIRS - 1
    with ExitStack() as ps_ctx:
        ps_x, ps_h1, ps_h3, ps_y = ([ps_ctx.enter_context(nc.psum_tensor(f"ex_{n}{i}", [P, CH], F32)) for i in range(2)]
                                    for n in ("x", "h1", "h3", "y"))
        block = ps_ctx.enter_context(nc.Block())

        @block.sync
        def _(sp):
            def load(s, j, again):
                for i, dram in enumerate(expert_weights(b, 2 * s + j)):
                    if again and i == 0:
                        sp.wait_ge(h_done, 2 * s + j - 1)
                    if again and i == 2:
                        sp.wait_ge(y_done, 2 * s + j - 1)
                    sp.dma_start(weight_views(b, j)[i], dram).then_inc(wfull[3 * j + i], 16)
            load(0, 0, False)
            load(0, 1, False)
            with sp.Fori(1, PAIRS) as s:
                load(s, 0, True)
                load(s, 1, True)

        @block.gpsimd
        def _(pool):
            for s in range(PAIRS):
                if s:
                    pool.wait_ge(turned, s)
                nc.gpsimd.indirect_dma_start(b.xg, None, b.rows_dram, bass.IndirectOffsetOnAxis(b.tok[:, s:s + 1], 0)).then_inc(xfull, 16)

        @block.tensor
        def _(pe):
            def turn(s):
                pe.wait_ge(xfull, 16 * (s + 1))
                turn_rows(nc, ps_x, b.xg, b.ident[:]).then_inc(turned, 1)

            def inputs(s, j):
                if j == 0:
                    pe.wait_ge(xt, s + 1)
                for i in range(2):
                    pe.wait_ge(wfull[3 * j + i], 16 * (s + 1))
                expert_in(nc, (ps_h1[j], ps_h3[j]), weight_views(b, j), b.xT[:, :, j * CAP:(j + 1) * CAP], CAP).then_inc(h_done, 1)

            def outputs(s, j):
                pe.wait_ge(hm, 2 * s + j + 1)
                pe.wait_ge(wfull[3 * j + 2], 16 * (s + 1))
                pe.wait_ge(y0, 2 * s + j)
                pe.wait_ge(y1, 2 * s + j)
                expert_out(nc, ps_y, weight_views(b, j)[2], b.hm[:, half[j]], CAP).then_inc(y_done, 1)

            turn(0)
            inputs(0, 0)
            inputs(0, 1)
            turn(1)
            outputs(0, 0)
            with pe.Fori(1, last) as s:
                inputs(s, 0)
                outputs(s - 1, 1)
                inputs(s, 1)
                turn(s + 1)
                outputs(s, 0)
            inputs(last, 0)
            outputs(last - 1, 1)
            inputs(last, 1)
            outputs(last, 0)
            outputs(last, 1)

        @block.vector
        def _(dve):
            def x_in(s, again=True):
                dve.wait_ge(turned, s + 1)
                if again:
                    dve.wait_ge(h_done, 2 * s)
                rows_in(nc, b, ps_x).then_inc(xt, 1)

            def product(s, j, again=True):
                dve.wait_ge(silu, 2 * s + j + 1)
                if again:
                    dve.wait_ge(y_done, 2 * s + j - 1)
                nc.vector.tensor_tensor(b.hm[:, half[j]], b.hs[:, half[j]], ps_h3[j][:, 0:KE * CAP], ALU.mult).then_inc(hm, 1)

            def y_half(s, j):
                dve.wait_ge(y_done, 2 * s + j + 1)
                dve.wait_ge(yout[j], 16 * (s + 1))
                nc.vector.tensor_copy(b.ys[0:CAP, j, 0:CH], ps_y[0][0:CAP, :]).then_inc(y0, 1)

            x_in(0, False)
            product(0, 0, False)
            product(0, 1, False)
            x_in(1)
            y_half(0, 0)
            with dve.Fori(1, last) as s:
                product(s, 0)
                y_half(s - 1, 1)
                product(s, 1)
                x_in(s + 1)
                y_half(s, 0)
            product(last, 0)
            y_half(last - 1, 1)
            product(last, 1)
            y_half(last, 0)
            y_half(last, 1)

        @block.scalar
        def _(act):
            def gate(s, j, again=True):
                act.wait_ge(h_done, 2 * s + j + 1)
                if again:
                    act.wait_ge(hm, 2 * s + j - 1)
                nc.scalar.activation(b.hs[:, half[j]], ps_h1[j][:, 0:KE * CAP], ACT.Silu).then_inc(silu, 1)

            def y_half(s, j):
                act.wait_ge(y_done, 2 * s + j + 1)
                act.wait_ge(yout[j], 16 * (s + 1))
                nc.scalar.copy(b.ys[0:CAP, j, CH:2 * CH], ps_y[1][0:CAP, :]).then_inc(y1, 1)
                act.wait_ge(y0, 2 * s + j + 1)
                act.wait_ge(y1, 2 * s + j + 1)
                act.dma_start(b.y_dram[bass.ds((2 * s + j) * CAP, CAP), :], b.ys[0:CAP, j, :]).then_inc(yout[j], 16)

            for j in range(2):
                nc.scalar.sem_inc(yout[j], 16)
            gate(0, 0, False)
            gate(0, 1, False)
            y_half(0, 0)
            with act.Fori(1, last) as s:
                gate(s, 0)
                y_half(s - 1, 1)
                gate(s, 1)
                y_half(s, 0)
            gate(last, 0)
            y_half(last - 1, 1)
            gate(last, 1)
            y_half(last, 0)
            y_half(last, 1)
            for j in range(2):
                act.wait_ge(yout[j], 16 * (PAIRS + 1))


def stage_spill(b):
    nc = b.nc
    wfull, idx, go, xfull, turned, xt, h_done, silu, hm, y_done, ysb, yout = (
        b.sem(f"sp_{n}") for n in ("w", "idx", "go", "x", "turn", "xt", "h", "silu", "hm", "y", "ysb", "out"))
    stage = b.sb("spill_idx", [P, 1], U32)
    with ExitStack() as ps_ctx:
        ps_x, ps_h, ps_y = ([ps_ctx.enter_context(nc.psum_tensor(f"sp_{n}{i}", [P, CH], F32)) for i in range(2)] for n in "xhy")
        block = ps_ctx.enter_context(nc.Block())

        def each(eng, body):
            n = eng.value_load(b.spill[0:1, SPILL:SPILL + 1], min_val=0, max_val=SPILL)
            with eng.If(n > 0):
                with eng.Fori(0, n) as j:
                    body(j)

        @block.sync
        def _(sp):
            def body(j):
                sp.wait_ge(yout, 16 * (j + 1))
                e = sp.value_load(b.spill[0:1, bass.ds(j, 1)], min_val=0, max_val=EXPERTS - 1)
                for w, dram in zip(weight_views(b, 0), expert_weights(b, e)):
                    sp.dma_start(w, dram).then_inc(wfull, 16)
            each(sp, body)

        @block.gpsimd
        def _(pool):
            def body(j):
                pool.wait_ge(yout, 16 * (j + 1))
                nc.gpsimd.tensor_copy(stage[:], b.tok[:, bass.ds(j + PAIRS, 1)]).then_inc(idx, 1)
                pool.wait_ge(idx, j + 1)
                nc.gpsimd.sem_inc(go, 1)
                nc.gpsimd.indirect_dma_start(b.xg, None, b.rows_dram, bass.IndirectOffsetOnAxis(stage[:], 0)).then_inc(xfull, 16)
            each(pool, body)

        @block.tensor
        def _(pe):
            def body(j):
                pe.wait_ge(xfull, 16 * (j + 1))
                turn_rows(nc, ps_x, b.xg, b.ident[:]).then_inc(turned, 1)
                pe.wait_ge(xt, j + 1)
                pe.wait_ge(wfull, 48 * (j + 1))
                expert_in(nc, ps_h, weight_views(b, 0), b.xT, P).then_inc(h_done, 1)
                pe.wait_ge(hm, j + 1)
                expert_out(nc, ps_y, weight_views(b, 0)[2], b.hm, P).then_inc(y_done, 1)
            each(pe, body)

        @block.vector
        def _(dve):
            def body(j):
                dve.wait_ge(turned, j + 1)
                rows_in(nc, b, ps_x).then_inc(xt, 1)
                dve.wait_ge(silu, j + 1)
                nc.vector.tensor_tensor(b.hm, b.hs, ps_h[1][:], ALU.mult).then_inc(hm, 1)
                dve.wait_ge(y_done, j + 1)
                for h in range(2):
                    last = nc.vector.tensor_copy(b.ys[:, 0, h * CH:(h + 1) * CH], ps_y[h][:])
                last.then_inc(ysb, 1)
                dve.wait_ge(yout, 16 * (j + 2))
            each(dve, body)

        @block.scalar
        def _(act):
            def body(j):
                act.wait_ge(h_done, j + 1)
                nc.scalar.activation(b.hs, ps_h[0][:], ACT.Silu).then_inc(silu, 1)
                act.wait_ge(ysb, j + 1)
                act.dma_start(b.y_dram[bass.ds((j + PAIRS) * P, P), :], b.ys[:, 0, :]).then_inc(yout, 16)
                act.wait_ge(yout, 16 * (j + 2))
            nc.scalar.sem_inc(yout, 16)
            each(act, body)


def stage_combine(b):
    nc, a = b.nc, b.a
    b.pg = b.ring[:, 0:2].rearrange("p i n -> p (i n)").rearrange("p (k n) -> p k n", k=KD)
    b.ple = b.ring[:, 2, 0:2 * D].rearrange("p (k n) -> p k n", k=2)
    b.prow = b.ring[:, 2, 2 * D:2 * D + 4 * 256].rearrange("p (t n) -> p t n", t=NT)
    b.frow = b.ring[:, 3, 0:D]
    b.last_in = b.sem("last_in")
    rows, done = [b.sem(f"co_rows{i}") for i in range(2 * NT)], b.sem("co_done")
    ybuf = b.s_ab[:, 8 * U:24 * U].rearrange("p (i n) -> p i n", i=2 * NT)
    with nc.Block() as block:
        @block.sync
        def _(sp):
            sp.dma_start(b.pg, feature_tiles(a["w_pg_2"][0], 0, D)).then_inc(b.last_in, 16)
            sp.dma_start(b.ple, feature_tiles(a["w_ple_2"][0], 0, D)).then_inc(b.last_in, 16)
            sp.dma_start(b.prow, a["p_2"][0, 0].rearrange("(t p) n -> p t n", p=P)).then_inc(b.last_in, 16)
            sp.dma_start(b.frow, a["g_final_2"].partition_broadcast(P)).then_inc(b.last_in, 16)

        @block.gpsimd
        def _(pool):
            for i in range(2 * NT):
                nc.gpsimd.indirect_dma_start(ybuf[:, i, :], None, b.y_dram, bass.IndirectOffsetOnAxis(b.slot[:, i:i + 1], 0)).then_inc(rows[i], 16)

        @block.vector
        def _(dve):
            for i in range(2 * NT):
                t = i % NT
                dve.wait_ge(rows[i], 16)
                if i >= NT:
                    dve.wait_ge(done, i - NT + 1)
                nc.vector.scalar_tensor_tensor(out=b.x[:, t, :], in0=ybuf[:, i, :], scalar=b.weight[:, i:i + 1], in1=b.x[:, t, :],
                                               op0=ALU.mult, op1=ALU.add).then_inc(done, 1)


def stage_embedding(b):
    nc = b.nc
    pT = b.s_ab[:, 0:2 * U].rearrange("p (k t) -> p k t", k=2)
    sg = b.scr[:, 0:4 * U].rearrange("p (i n) -> p i n", i=4)
    turned, pt, ready, gate, prod, ev = (b.sem(f"em_{n}") for n in ("turn", "pt", "ready", "gate", "prod", "ev"))
    with ExitStack() as ps_ctx:
        ps_g, ps_p = ([ps_ctx.enter_context(nc.psum_tensor(f"em_{n}{i}", [P, CH], F32)) for i in range(4)] for n in "gp")
        block = ps_ctx.enter_context(nc.Block())

        @block.tensor
        def _(pe):
            pe.wait_ge(b.last_in, 64)
            for k in range(2):
                for t in range(NT):
                    mm = nc.tensor.transpose(ps_p[k][:, t * P:t * P + P], b.prow[:, t, k * P:k * P + P], b.ident[:])
            mm.then_inc(turned, 1)
            pe.wait_ge(pt, 1)
            for i in range(2 * NT):
                h, t = i // NT, i % NT
                if i >= 4:
                    pe.wait_ge(ev, i - 3)
                product_rows(nc, ps_g[i % 4][:], b.hT, t, b.pg[:, :, h * CH:(h + 1) * CH], KD)
                product_rows(nc, ps_p[i % 4][:], pT, t, b.ple[:, :, h * CH:(h + 1) * CH], 2).then_inc(ready, 1)

        @block.scalar
        def _(act):
            for i in range(2 * NT):
                act.wait_ge(ready, i + 1)
                if i >= 4:
                    act.wait_ge(ev, i - 3)
                nc.scalar.activation(sg[:, i % 4], ps_g[i % 4][:], ACT.Sigmoid).then_inc(gate, 1)

        @block.vector
        def _(dve):
            dve.wait_ge(turned, 1)
            for k in range(2):
                last = nc.vector.tensor_copy(pT[:, k, :], ps_p[k][:])
            last.then_inc(pt, 1)
            for i in range(2 * NT):
                h, t = i // NT, i % NT
                xs = b.x[:, t, h * CH:(h + 1) * CH]
                dve.wait_ge(gate, i + 1)
                nc.vector.tensor_tensor(sg[:, i % 4], sg[:, i % 4], ps_p[i % 4][:], ALU.mult).then_inc(prod, 1)
                dve.wait_ge(prod, i + 1)
                nc.vector.tensor_tensor(xs, xs, sg[:, i % 4], ALU.add).then_inc(ev, 1)


def stage_final(b):
    nc = b.nc
    y = b.u_big[:, 0:NT * D].rearrange("p (t d) -> p t d", t=NT)
    ss = b.small[:, 0:4]
    sq, var, root, inv, done, stored = (b.sem(f"fi_{n}") for n in ("sq", "var", "root", "inv", "done", "stored"))
    with nc.Block() as block:
        @block.scalar
        def _(act):
            for t in range(NT):
                last = nc.scalar.activation(y[:, t, :], b.x[:, t, :], ACT.Square, accum_out=ss[:, t:t + 1])
            last.then_inc(sq, 1)
            act.wait_ge(var, 1)
            nc.scalar.activation(ss, ss, ACT.Sqrt).then_inc(root, 1)

        @block.vector
        def _(dve):
            dve.wait_ge(sq, 1)
            nc.vector.tensor_scalar(ss, ss, 1.0 / D, EPS, ALU.mult, ALU.add).then_inc(var, 1)
            dve.wait_ge(root, 1)
            nc.vector.reciprocal(ss, ss).then_inc(inv, 1)
            dve.wait_ge(inv, 1)
            for t in range(NT):
                nc.vector.scalar_tensor_tensor(out=y[:, t, :], in0=b.x[:, t, :], scalar=ss[:, t:t + 1], in1=b.frow,
                                               op0=ALU.mult, op1=ALU.mult).then_inc(done, 1)

        @block.sync
        def _(sp):
            for t in range(NT):
                sp.wait_ge(done, t + 1)
                sp.dma_start(b.out[0, t * P:(t + 1) * P, :], y[:, t, :]).then_inc(stored, 16)
            sp.wait_ge(stored, 16 * NT)


_INS = ["x", "c", "w_ada", "b_ada", "norm_mix_g", "w_in", "cmp_pos_k", "cmp_w1_k", "cmp_w2_k", "cmp_pos_v",
        "cmp_w1_v", "cmp_w2_v", "w_proj_a", "w_proj_b", "w_out", "norm_ffn_g", "w_ffn_gate", "w_ffn_up",
        "w_ffn_down", "norm_final_g", "p_2", "g_mix_2", "w_in_2", "gm_ln_g_2", "gm_ln_b_2", "gm_w_sp_2",
        "gm_b_sp_2", "w_up_a_2", "hg_lb_param_2", "hg_norm_g_2", "w_up_b_2", "w_out_2", "g_ffn_2", "w_grp_2",
        "w_exp_2", "w1_2", "w3_2", "w2_2", "g_ple_2", "w_pg_2", "w_ple_2", "g_final_2"]


def build(nc, a, out, stop=99):
    with ExitStack() as ctx:
        ctx.enter_context(nc.allow_non_contiguous_dma(reason="small vectors"))
        b = Build(nc, ctx, a, out)
        plan_weights(b)
        b.rows_dram = nc.dram_tensor("normed_rows", (T, D), F32).ap()
        b.h_back = b.sem("h_back")
        yT = [b.s_ab[:, i * 4 * U:(i + 1) * 4 * U].rearrange("p (k t) -> p k t", k=4) for i in range(2)]
        y2T = [b.w1flat[:, i * 4 * U:(i + 1) * 4 * U].rearrange("p (k t) -> p k t", k=4) for i in range(2)]
        mT = b.s_ab[:, 8 * U:16 * U].rearrange("p (k t) -> p k t", k=KD)
        guT = b.s_ab[:, 0:KF * T].rearrange("p (k t) -> p k t", k=KF)

        def vec(name, n=KD):
            return b.vcol[:, VAT[name]:VAT[name] + n]

        def block1_merge(b):
            b.take_x(b.reg_b)
            b.take_h(b.reg_a)
            stage_merge(b, "merge1", b.c_merge1, yT[0], yT[1], mT,
                        x_load=a["x"][0].rearrange("(t p) d -> p t d", p=P), h_wait=b.h_back)

        stages = [
            lambda: stage_constants(b),
            lambda: stage_modulation(b),
            lambda: stage_norm(b, "n1", b.mulcol[:, 0:KD], b.modcol[:, 0:KD], first=True, save=b.h_dram),
            lambda: stage_project1(b),
            lambda: stage_compress(b),
            lambda: stage_attention(b),
            lambda: stage_turn(b, "turn1", [(b.oa, yT[0], None), (b.ob, yT[1], None)]),
            lambda: block1_merge(b),
            lambda: stage_rows_out(b, "out1", mT, b.c_out1, b.g1row),
            lambda: stage_norm(b, "n2", b.mulcol[:, KD:2 * KD], b.modcol[:, 2 * KD:3 * KD]),
            lambda: stage_ffn_up(b),
            lambda: stage_rows_out(b, "down", guT, b.c_down, b.g2row),
            b.next_block,
            lambda: stage_norm(b, "n3", vec("g_mix_2"), None, residual_row="norm_final_g"),
            lambda: stage_project2(b),
            lambda: stage_gmlp(b),
            lambda: stage_turn(b, "turn2", [(b.gu, y2T[0], None)]),
            lambda: stage_hgrn(b),
            lambda: stage_turn(b, "turn3", [(b.hog, y2T[1], vec("hg_norm_g_2", 4))]),
            lambda: stage_merge(b, "merge2", b.c_merge2, y2T[0], y2T[1], mT),
            lambda: stage_rows_out(b, "out2", mT, b.c_out2),
            lambda: stage_norm(b, "n4", vec("g_ffn_2"), None, rows_out=b.rows_dram),
            lambda: stage_router(b),
            lambda: (expert_buffers(b), stage_experts(b)),
            lambda: stage_spill(b),
            lambda: stage_combine(b),
            lambda: stage_norm(b, "n5", vec("g_ple_2"), None),
            lambda: stage_embedding(b),
            lambda: stage_final(b),
        ]
        for s in stages[:stop]:
            s()
    return b


def kernel(**inputs):
    import concourse.bacc as bacc
    from concourse.bass_utils import run_bass_kernel_spmd

    nc = bacc.Bacc("TRN2", target_bir_lowering=False, num_devices=1)
    arrays, a = {}, {}
    for name in _INS:
        v = np.ascontiguousarray(inputs[name])
        arrays[f"in_{name}"] = v
        a[name] = nc.dram_tensor(f"in_{name}", v.shape, mybir.dt.from_np(v.dtype), kind="ExternalInput").ap()
    out = nc.dram_tensor("out", (1, T, D), F32, kind="ExternalOutput").ap()
    build(nc, a, out)
    r = run_bass_kernel_spmd(nc, [arrays], core_ids=[0])
    return r.results[0]["out"]
```

```python
from contextlib import ExitStack, contextmanager

import numpy as np

import concourse.bass as bass
from concourse import mybir

ALU = mybir.AluOpType
ACT = mybir.ActivationFunctionType
AX = mybir.AxisListType
F32 = mybir.dt.float32
F32R = mybir.dt.float32r
I32 = mybir.dt.int32
U32 = mybir.dt.uint32

P = 128
D = 1024
KD = D // P
T = 512
NT = T // P
CH = 512
HEADS = 8
HD = 64
GROUPS = 2
REP = HEADS // GROUPS
SCALE = HD ** -0.5
CMP_BLOCK, CMP_STRIDE = 32, 16
NCMP = (T - CMP_BLOCK) // CMP_STRIDE + 1
NC = 32
FF = 2816
KF = FF // P
EPS = 1e-6
EXPERTS, EGROUPS = 32, 4
EPG = EXPERTS // EGROUPS
DE = 512
KE = DE // P
CAP = 64
SPILL = 16
PAIRS = EXPERTS // 2
SLOTS = (PAIRS + SPILL) * P
ADA = 6 * D // CH
RING = 4
U = CH
HG_HEADS, HG_CHUNK = 4, 64
GM_GROUPS = 8
NEG = -1e30
MASKED = -1e33
SP_CAP = 60.0


class Chunks:

    def __init__(self):
        self.items = []
        self.landed = []

    def add(self, *parts):
        i = len(self.items)
        before = self.landed[i - RING] if i >= RING else 0
        self.items.append(parts)
        self.landed.append(before + 16 * len(parts))
        return i


def feature_tiles(w, c0, c1):
    return w[:, c0:c1].rearrange("(k p) n -> p k n", p=P)


class Build:

    def __init__(self, nc, ctx, a, out):
        self.nc, self.ctx, self.a, self.out = nc, ctx, a, out
        self.passing = []
        self.ring = self.sb("ring", [P, RING, 8 * CH])
        self.reg_a = self.sb("reg_a", [P, 8 * U])
        self.reg_b = self.sb("reg_b", [P, 8 * U])
        self.s_ab = self.sb("s_ab", [P, 24 * U])
        self.s_a, self.s_b = self.s_ab[:, 0:16 * U], self.s_ab[:, 16 * U:24 * U]
        self.small = self.sb("small", [P, 64])
        self.rows2 = self.sb("rows2", [P, 2, HEADS, 2])
        self.reopened = 0
        self.open_work()
        self.take_x(self.reg_a)
        self.take_h(self.reg_b)
        self.h_dram = nc.dram_tensor("h_saved", (P, 8 * U), F32).ap()
        self.ring_full = [self.lasting_sem(f"ring_full{i}") for i in range(RING)]
        self.ring_used = self.lasting_sem("ring_used")
        self.ada_used = [self.sem(f"ada_used{i}") for i in range(2)]
        self.ch = Chunks()
        self.loaded = 0

    def sb(self, name, shape, dt=F32):
        return self.ctx.enter_context(self.nc.sbuf_tensor(name, shape, dt))

    def open_work(self):
        self.work = ExitStack()
        self.ctx.callback(self.close_work)
        self.w1flat, self.u_big, self.scr = (
            self.work.enter_context(self.nc.sbuf_tensor(f"{n}_{self.reopened}", [P, k * U], F32, side="right"))
            for n, k in (("w1flat", 8), ("u_big", 13), ("scr", 4)))
        self.reopened += 1

    def close_work(self):
        self.work.close()

    @contextmanager
    def parts_area(self):
        self.close_work()
        with ExitStack() as area:
            self.area = area
            yield area
        self.open_work()

    def parts(self, name, shape):
        return self.area.enter_context(self.nc.sbuf_tensor(name, shape, F32R, side="right"))

    def sem(self, name):
        s = self.nc.alloc_semaphore(name=name)
        self.passing.append(s)
        return s

    def lasting_sem(self, name):
        return self.nc.alloc_semaphore(name=name)

    def fresh_sems(self):
        self.nc.clear_and_free_semaphores(self.passing)
        self.passing = []
        self.nc.all_engine_barrier()

    def take_x(self, reg):
        self.x = reg[:].rearrange("p (t d) -> p t d", t=NT)

    def take_h(self, reg):
        self.hT = reg[:].rearrange("p (k t) -> p k t", k=KD)
        self.hTflat = reg

    def chunk(self, i, part=0):
        at = 0
        for p in self.ch.items[i][:part]:
            at += p.shape[1] * p.shape[2]
        _, k, n = self.ch.items[i][part].shape
        return self.ring[:, i % RING, at:at + k * n].rearrange("p (k n) -> p k n", k=k)

    def wait_chunk(self, eng, i):
        eng.wait_ge(self.ring_full[i % RING], self.ch.landed[i])

    def load_until(self, sp, end):
        for i in range(self.loaded, min(end, len(self.ch.items))):
            if i >= RING:
                if i - RING < ADA:
                    sp.wait_ge(self.ada_used[i % 2], (i - RING) // 2 + 1)
                else:
                    sp.wait_ge(self.ring_used, i - RING - ADA + 1)
            for part, dram in enumerate(self.ch.items[i]):
                sp.dma_start(self.chunk(i, part), dram).then_inc(self.ring_full[i % RING], 16)
        self.loaded = max(self.loaded, min(end, len(self.ch.items)))


def plan_weights(b):
    a, add = b.a, b.ch.add

    def by_rows(w):
        k_end = w.shape[0] // P
        return [(k, min(k + 4, k_end), add(feature_tiles(w[k * P:min(k + 4, k_end) * P, :], 0, D)))
                for k in range(0, k_end, 4)]

    b.c_ada = [add(feature_tiles(a["w_ada"][0], j * CH, j * CH + CH)) for j in range(ADA)]
    w = a["w_in"][0]
    ends = [0, 512, 1024, 1304, 1816, 2328, 2840]
    b.c_in = [add(feature_tiles(w, c0, c1)) for c0, c1 in zip(ends, ends[1:])]
    b.c_merge1 = plan_merge(add, w, ends[-1], a["w_proj_a"][0], a["w_proj_b"][0])
    b.c_out1 = by_rows(a["w_out"][0])
    b.c_ffn = [add(feature_tiles(a["w_ffn_gate"][0], j, j + 256), feature_tiles(a["w_ffn_up"][0], j, j + 256))
               for j in range(0, FF, 256)]
    b.c_down = by_rows(a["w_ffn_down"][0])
    w = a["w_in_2"][0]
    b.c_in2 = [add(feature_tiles(w, j * CH, j * CH + CH)) for j in range(6)]
    b.c_merge2 = plan_merge(add, w, 6 * CH, a["w_up_a_2"][0], a["w_up_b_2"][0])
    b.c_out2 = by_rows(a["w_out_2"][0])


def plan_merge(add, w, c0, wa, wb):
    out = []
    for n in range(0, D, 256):
        out.append((add(feature_tiles(w, c0 + n, c0 + n + 256), feature_tiles(w, c0 + D + n, c0 + D + n + 256)),
                    add(feature_tiles(wa, n, n + 256), feature_tiles(wb, n, n + 256))))
    return out


VROWS = [("c", 8), ("norm_mix_g", 8), ("norm_ffn_g", 8), ("g_mix_2", 8), ("g_ffn_2", 8),
         ("g_ple_2", 8), ("hg_norm_g_2", 4), ("hg_lb_param_2", 8), ("gm_b_sp_2", 8)]
VAT = {}
_n = 0
for _name, _k in VROWS:
    VAT[_name] = _n
    _n += _k
NV = _n


def stage_constants(b):
    nc, a = b.nc, b.a
    b.ident = b.sb("ident", [P, P])
    b.ones = b.sb("ones", [P, P])
    b.vcol = b.sb("vcol", [P, NV])
    b.sc = b.sb("silu_c", [P, KD])
    vrow = b.scr[0:NV, 0:P]
    loads, pool_done, cols, cols_out = (b.sem(n) for n in ("k_loads", "k_pool", "k_cols", "k_out"))
    b.x_in = b.sem("x_in")
    with nc.psum_tensor("k_ps", [P, CH], F32) as ps, nc.Block() as block:
        @block.sync
        def _(sp):
            for name, k in VROWS:
                n = "a b c -> (a b) c" if len(a[name].shape) == 3 else None
                v = a[name].rearrange(n) if n else a[name].rearrange("a (k p) -> (a k) p", p=P)
                sp.dma_start(vrow[VAT[name]:VAT[name] + k, :], v).then_inc(loads, 16)
            sp.dma_start(b.x[:], a["x"][0].rearrange("(t p) d -> p t d", p=P)).then_inc(b.x_in, 16)
            b.load_until(sp, RING)

        @block.gpsimd
        def _(pool):
            nc.gpsimd.memset(b.ident[:], 0.0).then_inc(pool_done, 1)
            nc.gpsimd.memset(b.ones[:], 1.0).then_inc(pool_done, 1)
            pool.wait_ge(pool_done, 2)
            nc.gpsimd.affine_select(out=b.ident[:], in_=b.ident[:], compare_op=ALU.not_equal, fill=1.0,
                                    base=0, pattern=[[-1, P]], channel_multiplier=1).then_inc(pool_done, 1)

        @block.tensor
        def _(pe):
            pe.wait_ge(pool_done, 3)
            pe.wait_ge(loads, 16 * len(VROWS))
            nc.tensor.transpose(ps[:, 0:NV], vrow, b.ident[0:NV, 0:NV]).then_inc(cols, 1)

        @block.vector
        def _(dve):
            dve.wait_ge(cols, 1)
            nc.vector.tensor_copy(b.vcol[:], ps[:, 0:NV]).then_inc(cols_out, 1)

        @block.scalar
        def _(act):
            act.wait_ge(cols_out, 1)
            nc.scalar.activation(b.sc[:], b.vcol[:, 0:KD], ACT.Silu)


def stage_modulation(b):
    nc, a = b.nc, b.a
    acc = b.u_big[:, 0:6 * D]
    b.modcol = b.sb("modcol", [P, 4 * KD])
    b.mulcol = b.sb("mulcol", [P, 2 * KD])
    b.g1row = b.sb("g1row", [P, D])
    b.g2row = b.sb("g2row", [P, D])
    bias_in, step, row_sum, summed, cols, rows = (
        b.sem(n) for n in ("ada_bias", "ada_step", "ada_row_sum", "ada_summed", "ada_cols", "ada_rows"))
    COLS = [0, 1, 3, 4]
    with ExitStack() as ps_ctx:
        psc = ps_ctx.enter_context(nc.psum_tensor("ada_psc", [P, CH], F32))
        psr = [ps_ctx.enter_context(nc.psum_tensor(f"ada_psr{i}", [P, CH], F32)) for i in range(4)]
        block = ps_ctx.enter_context(nc.Block())

        @block.sync
        def _(sp):
            sp.wait_ge(step, 1)
            sp.dma_start(acc[0:1, :], a["b_ada"]).then_inc(bias_in, 16)
            b.load_until(sp, b.c_ada[-1] + 1 + RING)

        @block.vector
        def _(dve):
            nc.vector.memset(acc, 0.0).then_inc(step, 1)
            dve.wait_ge(bias_in, 16)
            n = 1
            for j, c in enumerate(b.c_ada):
                if j % 2:
                    dve.wait_ge(row_sum, j // 2 + 1)
                    first = acc[0:1, j * CH:j * CH + CH]
                    nc.vector.tensor_tensor(first, first, psr[j // 2 % 4][0:1, :], ALU.add).then_inc(step, 1)
                    n += 1
                    continue
                b.wait_chunk(dve, c)
                w, s = b.chunk(c), acc[:, j * CH:j * CH + CH]
                for k in range(KD):
                    dve.wait_ge(step, n)
                    last = nc.vector.scalar_tensor_tensor(out=s, in0=w[:, k, :], scalar=b.sc[:, k:k + 1], in1=s,
                                                          op0=ALU.mult, op1=ALU.add).then_inc(step, 1)
                    n += 1
                dve.wait_ge(step, n)
                nc.vector.sem_inc(b.ada_used[0], 1)
            dve.wait_ge(step, n)
            nc.vector.sem_inc(summed, 1)
            dve.wait_ge(cols, 1)
            nc.vector.tensor_copy(b.modcol[:], psc[:, 0:4 * KD]).then_inc(step, 1)
            n += 1
            dve.wait_ge(step, n)
            for i, g in enumerate(("norm_mix_g", "norm_ffn_g")):
                nc.vector.scalar_tensor_tensor(
                    out=b.mulcol[:, i * KD:i * KD + KD], in0=b.modcol[:, (2 * i + 1) * KD:(2 * i + 2) * KD],
                    scalar=1.0, in1=b.vcol[:, VAT[g]:VAT[g] + KD], op0=ALU.add, op1=ALU.mult)
            dve.wait_ge(rows, 4)
            for i in range(4):
                dst = (b.g1row, b.g2row)[i // 2]
                nc.vector.tensor_copy(dst[:, i % 2 * CH:i % 2 * CH + CH], psr[i][:])

        @block.tensor
        def _(pe):
            for i, c in enumerate(b.c_ada[1::2]):
                b.wait_chunk(pe, c)
                if i >= 4:
                    pe.wait_ge(step, 1 + KD * (i - 3) + (i - 3))
                w = b.chunk(c)
                for k in range(KD):
                    mm = nc.tensor.matmul(psr[i % 4][0:1, :], b.sc[:, k:k + 1], w[:, k, :], start=(k == 0), stop=(k == KD - 1))
                mm.then_inc(row_sum, 1)
                pe.wait_ge(row_sum, i + 1)
                nc.tensor.sem_inc(b.ada_used[1], 1)
            pe.wait_ge(summed, 1)
            for i, part in enumerate(COLS):
                for k in range(KD):
                    mm = nc.tensor.matmul(psc[:, i * KD + k:i * KD + k + 1], acc[:, part * D + k * P:part * D + k * P + P],
                                          b.ones[:, 0:1], start=True, stop=True)
            mm.then_inc(cols, 1)
            for i in range(4):
                c = (2, 5)[i // 2] * D + i % 2 * CH
                nc.tensor.matmul(psr[i][:], b.ones[:], acc[:, c:c + CH], start=True, stop=True).then_inc(rows, 1)


def stage_norm(b, name, mul, add, first=False, rows_out=None,
               residual_row=None, save=None):
    nc = b.nc
    y = b.u_big[:, 0:NT * D].rearrange("p (t d) -> p t d", t=NT)
    ss = b.small[:, 0:16]
    squared, var, root, inv, scaled, turned, ev_a, ev_d, wrote, passd = (
        b.sem(f"{name}_{n}") for n in ("sq", "var", "root", "inv", "y", "turn", "eva", "evd", "rows", "pass"))
    row, row_in = b.scr[:, 0:D], b.sem(f"{name}_rowin")
    passes = 2 if residual_row is not None else 1
    with ExitStack() as ps_ctx:
        ps = [ps_ctx.enter_context(nc.psum_tensor(f"{name}_ps{i}", [P, CH], F32)) for i in range(4)]
        block = ps_ctx.enter_context(nc.Block())

        @block.sync
        def _(sp):
            if residual_row is not None:
                sp.dma_start(row, b.a[residual_row].partition_broadcast(P)).then_inc(row_in, 16)
            if rows_out is not None:
                sp.wait_ge(scaled, 1)
                sp.dma_start(rows_out.rearrange("(t p) d -> p t d", p=P), y).then_inc(wrote, 16)
                sp.wait_ge(wrote, 16)
            if save is not None:
                sp.wait_ge(ev_a, KD // 2)
                sp.wait_ge(ev_d, KD // 2)
                sp.dma_start(save, b.hTflat[:]).then_inc(wrote, 16)
                sp.wait_ge(wrote, 16)

        @block.scalar
        def _(act):
            if first:
                act.wait_ge(b.x_in, 16)
            for r in range(passes):
                if r:
                    act.wait_ge(passd, 1)
                for t in range(NT):
                    act_ = nc.scalar.activation(y[:, t, :], b.x[:, t, :], ACT.Square, accum_out=ss[:, 4 * r + t:4 * r + t + 1])
                act_.then_inc(squared, 1)
                act.wait_ge(var, r + 1)
                nc.scalar.activation(ss[:, 4 * r:4 * r + 4], ss[:, 4 * r:4 * r + 4], ACT.Sqrt).then_inc(root, 1)
            for k in range(1, KD, 2):
                act.wait_ge(turned, k + 1)
                nc.scalar.activation(b.hT[:, k, :], ps[k % 4][:], ACT.Identity, scale=mul[:, k:k + 1],
                                     bias=add[:, k:k + 1] if add is not None else 0.0).then_inc(ev_a, 1)

        @block.vector
        def _(dve):
            if first:
                dve.wait_ge(b.x_in, 16)
            for r in range(passes):
                s = ss[:, 4 * r:4 * r + 4]
                dve.wait_ge(squared, r + 1)
                nc.vector.tensor_scalar(s, s, 1.0 / D, EPS, ALU.mult, ALU.add).then_inc(var, 1)
                dve.wait_ge(root, r + 1)
                nc.vector.reciprocal(s, s).then_inc(inv, 1)
                dve.wait_ge(inv, r + 1)
                if r < passes - 1:
                    dve.wait_ge(row_in, 16)
                for t in range(NT):
                    rs = ss[:, 4 * r + t:4 * r + t + 1]
                    if r < passes - 1:
                        last = nc.vector.scalar_tensor_tensor(out=b.x[:, t, :], in0=b.x[:, t, :], scalar=rs,
                                                              in1=row, op0=ALU.mult, op1=ALU.mult)
                    else:
                        last = nc.vector.tensor_scalar(y[:, t, :], b.x[:, t, :], rs, None, ALU.mult)
                last.then_inc(passd if r < passes - 1 else scaled, 1)
                if r < passes - 1:
                    dve.wait_ge(passd, 1)
            for k in range(0, KD, 2):
                dve.wait_ge(turned, k + 1)
                if add is not None:
                    nc.vector.tensor_scalar(b.hT[:, k, :], ps[k % 4][:], mul[:, k:k + 1], add[:, k:k + 1],
                                            ALU.mult, ALU.add).then_inc(ev_d, 1)
                else:
                    nc.vector.tensor_scalar(b.hT[:, k, :], ps[k % 4][:], mul[:, k:k + 1], None,
                                            ALU.mult).then_inc(ev_d, 1)

        @block.tensor
        def _(pe):
            pe.wait_ge(scaled, 1)
            for k in range(KD):
                if k >= 4:
                    pe.wait_ge((ev_d, ev_a)[k % 2], (k - 4) // 2 + 1)
                for t in range(NT):
                    mm = nc.tensor.transpose(ps[k % 4][:, t * P:t * P + P], y[:, t, k * P:k * P + P], b.ident[:])
                mm.then_inc(turned, 1)


def product_T(nc, ps, w, n0, hT, kt):
    for k in range(kt):
        mm = nc.tensor.matmul(ps, w[:, k, n0:n0 + P], hT[:, k, :], start=(k == 0), stop=(k == kt - 1))
    return mm


def product_rows(nc, ps, hT, t, w, kt, start=True, stop=True):
    for k in range(kt):
        mm = nc.tensor.matmul(ps, hT[:, k, t * P:t * P + P], w[:, k, :],
                              start=start and k == 0, stop=stop and k == kt - 1)
    return mm



def lower(nc, lo, v, hi):
    return nc.vector.tensor_tensor(lo, v, hi.bitcast(F32), ALU.subtract)


def product_parts(nc, ps, x, y, start, stop):
    nc.tensor.matmul(ps, x[0], y[0], start=start, stop=False)
    nc.tensor.matmul(ps, x[0], y[1], start=False, stop=False)
    return nc.tensor.matmul(ps, x[1], y[0], start=False, stop=stop)


class Parts:

    def __init__(self, b, name, units, release=True):
        self.b, self.nc, self.units, self.release = b, b.nc, units, release
        self.h = [b.parts(f"{name}_h{i}", [P, KD, T]) for i in range(2)]
        self.w = [[b.parts(f"{name}_w{i}{j}", [P, D]) for j in range(2)] for i in range(2)]
        self.h_hi, self.h_lo, self.hi, self.lo, self.used = (
            b.sem(f"{name}_{n}") for n in ("h_hi", "h_lo", "w_hi", "w_lo", "w_used"))

    def unit(self, u, part):
        v = self.units[u][1]
        return self.w[u % 2][part][:].rearrange("p (k n) -> p k n", k=v.shape[1])

    def act_h(self, act):
        for k in range(KD):
            self.nc.scalar.copy(self.h[0][:, k, :], self.b.hT[:, k, :]).then_inc(self.h_hi, 1)

    def dve_h(self, dve):
        for k in range(KD):
            dve.wait_ge(self.h_hi, k + 1)
            lower(self.nc, self.h[1][:, k, :], self.b.hT[:, k, :], self.h[0][:, k, :]).then_inc(self.h_lo, 1)

    def act_w(self, act, u):
        if u >= len(self.units):
            return
        c, v, _ = self.units[u]
        self.b.wait_chunk(act, c)
        if u >= 2:
            act.wait_ge(self.used, u - 1)
        self.nc.scalar.copy(self.unit(u, 0), v).then_inc(self.hi, 1)

    def dve_w(self, dve, u):
        if u >= len(self.units):
            return
        c, v, last = self.units[u]
        self.b.wait_chunk(dve, c)
        dve.wait_ge(self.hi, u + 1)
        lower(self.nc, self.unit(u, 1), v, self.unit(u, 0)).then_inc(self.lo, 1)
        if last and self.release:
            dve.wait_ge(self.lo, u + 1)
            self.nc.vector.sem_inc(self.b.ring_used, 1)

    def pe_T(self, pe, u, bank, done=None):
        pe.wait_ge(self.lo, u + 1)
        for k in range(KD):
            if u == 0:
                pe.wait_ge(self.h_lo, k + 1)
            mm = product_parts(self.nc, bank, [self.unit(u, j)[:, k, :] for j in range(2)],
                               [self.h[j][:, k, :] for j in range(2)], k == 0, k == KD - 1)
        mm.then_inc(self.used, 1)

    def pe_rows(self, pe, u, banks, k0):
        pe.wait_ge(self.lo, u + 1)
        for t in range(NT):
            for k in range(2):
                if u == 0 and t == 0:
                    pe.wait_ge(self.h_lo, k0 + k + 1)
                mm = product_parts(self.nc, banks[t][:], [self.h[j][:, k0 + k, t * P:t * P + P] for j in range(2)],
                                   [self.unit(u, j)[:, k, :] for j in range(2)], k0 + k == 0, k0 + k == KD - 1)
        mm.then_inc(self.used, 1)


def units_T(b, c, part=0, n=CH):
    return [(c, b.chunk(c, part)[:, :, n0:n0 + P], n0 + P == n) for n0 in range(0, n, P)]


def units_rows(b, c):
    return [(c, b.chunk(c)[:, k0:k0 + 2, :], k0 + 2 == KD) for k0 in range(0, KD, 2)]


def compression_weights(b):
    posr = b.scr[0:32, 640:896]
    w1 = [r[:].rearrange("p (l n) -> p l n", l=CMP_BLOCK) for r in (b.reg_a, b.w1flat)]
    w2 = b.scr[:, 960:1216]
    return posr, w1, w2


def stage_project1(b):
    nc, a = b.nc, b.a
    posr, w1, w2 = compression_weights(b)
    b.cmp_in = b.sem("cmp_in")
    b.qT = b.s_a[:, 0:4 * T].rearrange("p (n t) -> p n t", n=4)
    b.sqT = b.s_a[:, 4 * T:8 * T].rearrange("p (n t) -> p n t", n=4)
    b.skT = b.s_a[:, 8 * T:12 * T].rearrange("p (n t) -> p n t", n=4)
    b.sv = b.s_a[:, 12 * T:16 * T].rearrange("p (t n) -> p t n", t=NT)
    b.kk = [b.s_b[:, i * 2 * T:(i + 1) * 2 * T].rearrange("p (g t) -> p g t", g=2) for i in range(2)]
    b.kcT, b.vcT = b.s_b[:, 4 * T:5 * T], b.s_b[:, 5 * T:6 * T]
    b.vv = [b.s_b[:, (6 + i) * T:(7 + i) * T].rearrange("p (t n) -> p t n", t=NT) for i in range(2)]
    b.gate = b.sb("gate", [P, NT, 24])

    def copy_rows(dst, w4):
        return ("rows4", dst, w4)

    tiles = [(0, n * P, "q", b.qT[:, n, :]) for n in range(4)]
    tiles += [(1, 0, "T", b.kcT), (1, P, "T", b.vcT), (1, 2 * P, "dup", b.kk[0]), (1, 3 * P, "rows", b.vv[0])]
    tiles += [(2, 0, "dup", b.kk[1]), (2, P, "rows", b.vv[1]), (2, 2 * P, "gate", b.gate)]
    tiles += [(3, n * P, "q", b.sqT[:, n, :]) for n in range(4)]
    tiles += [(4, n * P, "T", b.skT[:, n, :]) for n in range(4)]
    tiles += [(5, t, "wide", b.sv[:, t, :]) for t in range(4)]
    NB = 6
    ready, ev_a, ev_d = (b.sem(f"p1_{n}") for n in ("ready", "eva", "evd"))
    with ExitStack() as ps_ctx:
        ps = [ps_ctx.enter_context(nc.psum_tensor(f"p1_ps{i}", [P, CH], F32)) for i in range(NB)]
        block = ps_ctx.enter_context(nc.Block())

        @block.sync
        def _(sp):
            for i, n in enumerate("kv"):
                w = a[f"cmp_w1_{n}"][0].rearrange("(l d) n -> d l n", d=HD)
                for half in range(2):
                    sp.dma_start(w1[i][64 * half:64 * half + 64], w).then_inc(b.cmp_in, 16)
                    sp.dma_start(posr[:, (2 * i + half) * HD:(2 * i + half + 1) * HD], a[f"cmp_pos_{n}"][0]).then_inc(b.cmp_in, 16)
                    sp.dma_start(w2[:, (2 * i + half) * HD:(2 * i + half + 1) * HD], a[f"cmp_w2_{n}"][0]).then_inc(b.cmp_in, 16)
            b.load_until(sp, b.c_in[-1] + 1 + RING)

        @block.tensor
        def _(pe):
            for i, (c, n0, kind, _) in enumerate(tiles):
                if i == 0 or tiles[i - 1][0] != c:
                    b.wait_chunk(pe, b.c_in[c])
                if i >= NB:
                    pe.wait_ge((ev_d, ev_a)[i % 2], (i - NB) // 2 + 1)
                w, bank = b.chunk(b.c_in[c]), ps[i % NB]
                if kind in ("q", "T", "dup"):
                    mm = product_T(nc, bank[:], w, n0, b.hT, KD)
                elif kind == "wide":
                    mm = product_rows(nc, bank[:], b.hT, n0, w, KD)
                else:
                    n = P if kind == "rows" else 24
                    for t in range(NT):
                        mm = product_rows(nc, bank[:, t * n:t * n + n], b.hT, t, w[:, :, n0:n0 + n], KD)
                mm.then_inc(ready, 1)
                if i + 1 == len(tiles) or tiles[i + 1][0] != c:
                    pe.wait_ge(ready, i + 1)
                    nc.tensor.sem_inc(b.ring_used, 1)

        def move(eng, copy, scaled, i, done):
            _, _, kind, dst = tiles[i]
            bank = ps[i % NB]
            eng.wait_ge(ready, i + 1)
            if kind == "q":
                last = scaled(dst, bank[:])
            elif kind in ("T", "wide"):
                last = copy(dst, bank[:])
            elif kind == "dup":
                for half in range(2):
                    for g in range(2):
                        last = copy(dst[64 * half:64 * half + 64, g, :], bank[64 * g:64 * g + 64, :])
            elif kind == "rows":
                last = copy(dst, bank[:].rearrange("p (t n) -> p t n", t=NT))
            else:
                last = copy(dst[:], bank[:, 0:NT * 24].rearrange("p (t n) -> p t n", t=NT))
            last.then_inc(done, 1)

        @block.vector
        def _(dve):
            for i in range(0, len(tiles), 2):
                move(dve, nc.vector.tensor_copy, lambda o, s: nc.vector.tensor_scalar(o, s, SCALE, None, ALU.mult), i, ev_d)

        @block.scalar
        def _(act):
            for i in range(1, len(tiles), 2):
                move(act, nc.scalar.copy, lambda o, s: nc.scalar.mul(o, s, SCALE), i, ev_a)


def stage_compress(b):
    nc, a = b.nc, b.a
    b.bias = b.u_big[:, 0:HEADS * T].rearrange("p (h k) -> p h k", h=HEADS)
    b.sbmask = b.u_big[:, 8 * T:9 * T]
    b.oa = b.u_big[:, 9 * T:13 * T].rearrange("p (t n) -> p t n", t=NT)
    nd = b.scr[:, 0:T]
    ndc = b.scr[:, T:T + NT * NC].rearrange("p (t n) -> p t n", t=NT)
    posT = b.scr[:, 896:960].rearrange("p (b l) -> p b l", b=2)
    posr, w1, w2 = compression_weights(b)
    kp = b.hTflat[:, 0:2 * 1024].rearrange("p (b l n) -> p b l n", b=2, l=32)
    hid = b.hTflat[:, 2048:2048 + 4 * NC].rearrange("p (b g n) -> p b g n", b=2, g=2)
    kc = b.hTflat[:, 2304:2304 + 2 * NC].rearrange("p (g n) -> p g n", g=2)
    vbd = b.hTflat[:, 2560:2560 + 2 * REP * HD].rearrange("p (g n) -> p g n", g=2)
    cs = [b.hTflat[:, 3072 + i * 256:3072 + i * 256 + 256].rearrange("p (h n) -> p h n", h=HEADS) for i in range(4)]
    pTc = b.scr[:, 1216:1216 + 2 * 2 * P].rearrange("p (i g q) -> p i g q", i=2, g=2)
    st = b.small
    pool, sel, win, hsum, hact, kcp, kco, dchain, sc, scm, expd, pt, pte, o, oe, gsig, vz = (
        b.sem(f"cmp_{n}") for n in ("pool", "sel", "win", "hsum", "hact", "kcp", "kco", "chain", "sc", "scm",
                                    "exp", "pt", "pte", "o", "oe", "gsig", "vz"))
    slopes = [2.0 ** -(h + 1) for h in range(HEADS)]
    with ExitStack() as ps_ctx:
        def bank(n):
            return ps_ctx.enter_context(nc.psum_tensor(f"cmp_{n}", [P, CH], F32))
        ps_k, ps_t, ps_o = (bank(n) for n in ("k", "t", "o"))
        ps_pos, ps_h, ps_s = ps_t, [bank("h0"), bank("h1")], [bank("s0"), bank("s1")]
        block = ps_ctx.enter_context(nc.Block())

        @block.gpsimd
        def _(pool_):
            nc.gpsimd.iota(nd, pattern=[[1, T]], base=-(T - P), channel_multiplier=-1,
                           allow_small_or_imprecise_dtypes=True).then_inc(pool, 1)
            nc.gpsimd.iota(ndc, pattern=[[-P, NT], [CMP_STRIDE, NC]], base=CMP_BLOCK - 1, channel_multiplier=-1,
                           allow_small_or_imprecise_dtypes=True).then_inc(pool, 1)
            nc.gpsimd.memset(b.sbmask, 0.0).then_inc(pool, 1)
            nc.gpsimd.memset(st[:, 40:41], 1.0).then_inc(pool, 1)
            pool_.wait_ge(pool, 4)
            nc.gpsimd.affine_select(out=nd, in_=nd, compare_op=ALU.is_ge, fill=MASKED, base=T - P,
                                    pattern=[[-1, T]], channel_multiplier=1).then_inc(sel, 1)
            nc.gpsimd.affine_select(out=ndc, in_=ndc, compare_op=ALU.is_ge, fill=MASKED, base=-(CMP_BLOCK - 1),
                                    pattern=[[P, NT], [-CMP_STRIDE, NC]], channel_multiplier=1).then_inc(sel, 1)
            nc.gpsimd.affine_select(out=b.sbmask, in_=b.sbmask, compare_op=ALU.is_gt, fill=NEG, base=T - P,
                                    pattern=[[-1, T]], channel_multiplier=1).then_inc(sel, 1)
            nc.gpsimd.affine_select(out=st[:, 40:41], in_=st[:, 40:41], compare_op=ALU.is_ge, fill=0.0,
                                    base=-(CMP_BLOCK - 1), pattern=[[0, 1]], channel_multiplier=1).then_inc(sel, 1)

        @block.tensor
        def _(pe):
            pe.wait_ge(b.cmp_in, 16 * 12)
            for i in range(2):
                mm = nc.tensor.transpose(ps_pos[:, 32 * i:32 * i + 32], posr[:, 2 * i * HD:2 * (i + 1) * HD], b.ident[0:32, 0:32])
            mm.then_inc(kcp, 1)
            for i in range(2):
                pe.wait_ge(win, i + 1)
                for l in range(CMP_BLOCK):
                    for g in range(2):
                        rows = slice(64 * g, 64 * g + 64)
                        mm = nc.tensor.matmul(ps_h[g][:, i * NC:(i + 1) * NC], w1[i][rows, l, :], kp[rows, i, l, :],
                                              start=(l == 0), stop=(l == CMP_BLOCK - 1))
                mm.then_inc(hsum, 1)
            pe.wait_ge(hact, 1)
            for g in range(2):
                nc.tensor.matmul(ps_k[:, g * NC:(g + 1) * NC], w2[:, 0:2 * HD], hid[:, 0, g, :], start=True, stop=True)
            for g in range(2):
                mm = nc.tensor.matmul(ps_k[0:NC, P + g * HD:P + (g + 1) * HD], hid[:, 1, g, :], w2[:, 2 * HD:3 * HD],
                                      start=True, stop=True)
            mm.then_inc(kco, 1)
            pe.wait_ge(dchain, 1)
            for t in range(NT):
                if t:
                    pe.wait_ge(scm, t)
                for h in range(HEADS):
                    r = slice(64 * (h % 2), 64 * (h % 2) + 64)
                    mm = nc.tensor.matmul(ps_s[h % 2][:, h // 2 * NC:(h // 2 + 1) * NC], b.qT[r, h // 2, t * P:t * P + P],
                                          kc[r, h // REP, :], start=True, stop=True)
                mm.then_inc(sc, 1)
                pe.wait_ge(expd, t + 1)
                for g in range(2):
                    mm = nc.tensor.transpose(ps_t[:, g * P:g * P + P], cs[t][:, g * REP:(g + 1) * REP, :].rearrange("p h n -> p (h n)"), b.ident[:])
                mm.then_inc(pt, 1)
                pe.wait_ge(pte, t + 1)
                if t:
                    pe.wait_ge(oe, t)
                for g in range(2):
                    mm = nc.tensor.matmul(ps_o[:, g * REP * HD:(g + 1) * REP * HD], pTc[:, t % 2, g, :], vbd[:, g, :],
                                          start=True, stop=True)
                mm.then_inc(o, 1)

        @block.vector
        def _(dve):
            n = [0]

            def link(ins):
                n[0] += 1
                ins.then_inc(vz, 1)
                dve.wait_ge(vz, n[0])

            nc.vector.memset(kp[:, :, :, NCMP:NC], 0.0)
            link(nc.vector.memset(vbd, 0.0))
            dve.wait_ge(kcp, 1)
            link(nc.vector.tensor_copy(posT, ps_pos[:, 0:64].rearrange("p (b l) -> p b l", b=2)))
            for i, src in enumerate((b.kcT, b.vcT)):
                s = src.rearrange("p (n l) -> p l n", l=CMP_STRIDE)
                for half in range(2):
                    l = slice(half * CMP_STRIDE, (half + 1) * CMP_STRIDE)
                    last = nc.vector.tensor_tensor(kp[:, i, l, 0:NCMP], s[:, :, half:half + NCMP],
                                                   posT[:, i, l].unsqueeze(2).to_broadcast([P, CMP_STRIDE, NCMP]), ALU.add)
                last.then_inc(win, 1)
            dve.wait_ge(sel, 4)
            for h in range(HEADS):
                nc.vector.tensor_scalar(b.bias[:, h, :], nd, slopes[h], None, ALU.mult)
            dve.wait_ge(kco, 1)
            nc.vector.tensor_copy(kc, ps_k[:, 0:2 * NC].rearrange("p (g n) -> p g n", g=2))
            for g in range(2):
                for r in range(REP):
                    last = nc.vector.tensor_copy(vbd[NC * r:NC * r + NC, g, r * HD:(r + 1) * HD], ps_k[0:NC, P + g * HD:P + (g + 1) * HD])
            last.then_inc(dchain, 1)
            dve.wait_ge(gsig, 1)
            for t in range(NT):
                dve.wait_ge(sc, t + 1)
                for h in range(HEADS):
                    last = nc.vector.scalar_tensor_tensor(out=cs[t][:, h, :], in0=ndc[:, t, :], scalar=slopes[h],
                                                          in1=ps_s[h % 2][:, h // 2 * NC:(h // 2 + 1) * NC], op0=ALU.mult, op1=ALU.add)
                last.then_inc(scm, 1)
                dve.wait_ge(scm, t + 1)
                link(nc.vector.tensor_reduce(st[:, 0:8], cs[t], AX.X, ALU.max))
                link(nc.vector.tensor_tensor(cs[t], cs[t], st[:, 0:8].unsqueeze(2).to_broadcast([P, HEADS, NC]), ALU.subtract))
                nc.vector.sem_inc(dchain, 1)
                dve.wait_ge(expd, t + 1)
                link(nc.vector.tensor_reduce(st[:, 8:16], cs[t], AX.X, ALU.add))
                link(nc.vector.reciprocal(st[:, 16:24], st[:, 8:16]))
                gates = b.gate[:, t, :].rearrange("p (h b) -> p h b", b=3)
                link(nc.vector.tensor_tensor(st[:, 24:32], st[:, 16:24], gates[:, :, 0], ALU.mult))
                if t == 0:
                    link(nc.vector.tensor_scalar(st[:, 24:32], st[:, 24:32], st[:, 40:41], None, ALU.mult))
                dve.wait_ge(pt, t + 1)
                nc.vector.tensor_copy(pTc[:, t % 2], ps_t[:, 0:2 * P].rearrange("p (g q) -> p g q", g=2)).then_inc(pte, 1)
                dve.wait_ge(o, t + 1)
                nc.vector.tensor_tensor(b.oa[:, t, :].rearrange("p (h n) -> p h n", h=HEADS), ps_o[:].rearrange("p (h n) -> p h n", h=HEADS),
                                        st[:, 24:32].unsqueeze(2).to_broadcast([P, HEADS, HD]), ALU.mult).then_inc(oe, 1)

        @block.scalar
        def _(act):
            nc.scalar.activation(b.gate[:], b.gate[:], ACT.Sigmoid).then_inc(gsig, 1)
            act.wait_ge(hsum, 2)
            for g in range(2):
                last = nc.scalar.activation(hid[:, :, g, :], ps_h[g][:, 0:2 * NC].rearrange("p (b n) -> p b n", b=2), ACT.Gelu_apprx_tanh)
            last.then_inc(hact, 1)
            for t in range(NT):
                act.wait_ge(dchain, t + 2)
                nc.scalar.activation(cs[t], cs[t], ACT.Exp).then_inc(expd, 1)


def stage_attention(b):
    nc = b.nc
    b.ob = b.hTflat[:, 0:4 * T].rearrange("p (t n) -> p t n", t=NT)
    PER = 3 * HEADS
    units = [(t, i // 3, i % 3) for t in range(NT) for i in range(PER)]
    N = len(units)
    STEPS = N + 8

    def bufs(reg, u0, n):
        return reg[:, u0 * U:(u0 + n) * U].rearrange("p (i k) -> p i k", i=n)
    prob, ssb = bufs(b.w1flat, 0, 6), bufs(b.w1flat, 6, 2)
    zbuf, zc, ex = bufs(b.hTflat, 4, 2), bufs(b.hTflat, 6, 2), bufs(b.s_b, 4, 2)
    ptsb = b.scr[:, 0:3 * T].rearrange("p (i k) -> p i k", i=3)
    tmp = b.scr[:, 3 * T:4 * T]
    negm = b.small[:, 0:4]
    fac = b.small[:, 24:40].rearrange("p (h b) -> p h b", b=2)
    (sc_ready, s_taken, p_soft, z_ready, e_done, l_ready, chain, w_ready, p_stick, pt_ready, pt_a, pt_d, pv,
     o_moved) = (b.sem(f"at_{n}") for n in (
         "scores", "taken", "psoft", "z", "e", "l", "chain", "w", "pstick", "pt", "pta", "ptd", "pv", "omoved"))

    def keys(i):
        return (units[i][0] + 1) * P

    def at(s, lag):
        return s - lag if 0 <= s - lag < N else None

    def soft_count(i):
        return (i // 3) * 2 + min(i % 3 + 1, 2)

    def wait_moved(eng, i):
        if i % 3 == 2:
            eng.wait_ge(pt_d, i // 3 + 1)
        else:
            eng.wait_ge(pt_a, soft_count(i))

    with ExitStack() as ps_ctx:
        def bank(n):
            return ps_ctx.enter_context(nc.psum_tensor(f"at_{n}", [P, CH], F32))
        ps_s = [bank(f"s{i}") for i in range(3)]
        ps_t = [bank(f"t{i}") for i in range(2)]
        ps_o = [bank(f"o{i}") for i in range(3)]
        block = ps_ctx.enter_context(nc.Block())

        @block.tensor
        def _(pe):
            for s in range(STEPS):
                i = at(s, 0)
                if i is not None:
                    t, h, kind = units[i]
                    if i >= 3:
                        pe.wait_ge(s_taken, i - 2)
                    r = slice(64 * (h % 2), 64 * (h % 2) + 64)
                    q = (b.sqT if kind == 2 else b.qT)[r, h // 2, t * P:t * P + P]
                    k = b.skT[r, h // 2, 0:keys(i)] if kind == 2 else b.kk[kind][r, h // REP, 0:keys(i)]
                    nc.tensor.matmul(ps_s[i % 3][:, 0:keys(i)], q, k, start=True, stop=True).then_inc(sc_ready, 1)
                i = at(s, 5)
                if i is not None:
                    if i % 3 == 2:
                        pe.wait_ge(p_stick, i // 3 + 1)
                    else:
                        pe.wait_ge(p_soft, soft_count(i))
                    if i >= 2:
                        wait_moved(pe, i - 2)
                    for c in range(0, keys(i), P):
                        mm = nc.tensor.transpose(ps_t[i % 2][:, c:c + P], prob[:, i % 6, c:c + P], b.ident[:])
                    mm.then_inc(pt_ready, 1)
                i = at(s, 7)
                if i is not None:
                    t, h, kind = units[i]
                    if i % PER == 0 and i:
                        pe.wait_ge(o_moved, t)
                    wait_moved(pe, i)
                    for c in range(t + 1):
                        v = b.sv[:, c, h * HD:(h + 1) * HD] if kind == 2 else b.vv[kind][:, c, h // REP * HD:(h // REP + 1) * HD]
                        mm = nc.tensor.matmul(ps_o[kind][:, h * HD:(h + 1) * HD], ptsb[:, i % 3, c * P:c * P + P], v,
                                              start=(c == 0), stop=(c == t))
                    mm.then_inc(pv, 1)

        @block.vector
        def _(dve):
            n = [0]

            def link(ins):
                n[0] += 1
                ins.then_inc(chain, 1)
                return n[0]

            def linked(ins):
                dve.wait_ge(chain, link(ins))

            ex_made = {}
            for s in range(STEPS + 1):
                i = at(s, 1)
                if i is not None:
                    t, h, kind = units[i]
                    k, j = keys(i), i // 3
                    off = T - k
                    dve.wait_ge(sc_ready, i + 1)
                    if kind < 2:
                        m = soft_count(i) - 1
                        if m >= 2:
                            dve.wait_ge(p_soft, m - 1)
                        nc.vector.tensor_tensor_reduce(out=ssb[:, m % 2, 0:k], in0=ps_s[i % 3][:, 0:k], in1=b.bias[:, h, off:T],
                                                       scale=-1.0, scalar=3e38, op0=ALU.add, op1=ALU.min,
                                                       accum_out=negm[:, m % 2:m % 2 + 1]).then_inc(s_taken, 1)
                    else:
                        if j >= 2:
                            dve.wait_ge(p_stick, j - 1)
                        nc.vector.tensor_tensor(zbuf[:, j % 2, 0:k], ps_s[i % 3][:, 0:k], b.sbmask[:, off:T], ALU.add).then_inc(s_taken, 1)
                        dve.wait_ge(s_taken, i + 1)
                        nc.vector.tensor_scalar(zc[:, j % 2, 0:k], zbuf[:, j % 2, 0:k], SP_CAP, None, ALU.min).then_inc(z_ready, 1)
                        ex_made[j] = link(nc.vector.tensor_scalar(ex[:, j % 2, 0:k], zbuf[:, j % 2, 0:k], SP_CAP, 0.0, ALU.subtract, ALU.max))
                i = at(s, 6)
                if i is not None and i % 3 == 2:
                    dve.wait_ge(pt_ready, i + 1)
                    if i >= 3:
                        dve.wait_ge(pv, i - 2)
                    nc.vector.tensor_copy(ptsb[:, i % 3, 0:keys(i)], ps_t[i % 2][:, 0:keys(i)]).then_inc(pt_d, 1)
                i = at(s, 3)
                if i is not None and i % 3 == 2:
                    k, j = keys(i), i // 3
                    dve.wait_ge(l_ready, j + 1)
                    dve.wait_ge(chain, ex_made[j])
                    linked(nc.vector.tensor_tensor_scan(out=ex[:, j % 2, 0:k][:, ::-1], data0=zc[:, j % 2, 0:k][:, ::-1],
                                                        data1=ex[:, j % 2, 0:k][:, ::-1], initial=0.0, op0=ALU.add, op1=ALU.add))
                    nc.vector.tensor_tensor(zc[:, j % 2, 0:k], zbuf[:, j % 2, 0:k], ex[:, j % 2, 0:k], ALU.subtract).then_inc(w_ready, 1)
                i = s - 8
                if i >= 0 and i % PER == PER - 1:
                    t = units[i][0]
                    dve.wait_ge(pv, i + 1)
                    gates = b.gate[:, t, :].rearrange("p (h b) -> p h b", b=3)
                    linked(nc.vector.reciprocal(fac, b.rows2[:, t % 2]))
                    linked(nc.vector.tensor_tensor(fac, fac, gates[:, :, 1:3], ALU.mult))
                    oa = b.oa[:, t, :].rearrange("p (h n) -> p h n", h=HEADS)
                    tm = tmp.rearrange("p (h n) -> p h n", h=HEADS)
                    for kind in range(2):
                        linked(nc.vector.tensor_tensor(tm, ps_o[kind][:].rearrange("p (h n) -> p h n", h=HEADS),
                                                       fac[:, :, kind].unsqueeze(2).to_broadcast([P, HEADS, HD]), ALU.mult))
                        linked(nc.vector.tensor_tensor(oa, oa, tm, ALU.add))
                    nc.vector.tensor_copy(b.ob[:, t, :], ps_o[2][:]).then_inc(o_moved, 1)

        @block.scalar
        def _(act):
            nc.scalar.preload_act_table_set("natural_log_exp_and_others")
            for s in range(STEPS):
                i = at(s, 6)
                if i is not None and i % 3 != 2:
                    act.wait_ge(pt_ready, i + 1)
                    if i >= 3:
                        act.wait_ge(pv, i - 2)
                    nc.scalar.copy(ptsb[:, i % 3, 0:keys(i)], ps_t[i % 2][:, 0:keys(i)]).then_inc(pt_a, 1)
                i = at(s, 4)
                if i is not None and i % 3 == 2:
                    j = i // 3
                    act.wait_ge(w_ready, j + 1)
                    if i >= 6:
                        act.wait_ge(pt_ready, i - 5)
                    nc.scalar.activation(prob[:, i % 6, 0:keys(i)], zc[:, j % 2, 0:keys(i)], ACT.Exp).then_inc(p_stick, 1)
                i = at(s, 2)
                if i is not None:
                    t, h, kind = units[i]
                    k, j = keys(i), i // 3
                    if kind < 2:
                        m = soft_count(i) - 1
                        act.wait_ge(s_taken, i + 1)
                        if i >= 6:
                            act.wait_ge(pt_ready, i - 5)
                        if t >= 2 and i % PER == 0:
                            act.wait_ge(o_moved, t - 1)
                        nc.scalar.activation(prob[:, i % 6, 0:k], ssb[:, m % 2, 0:k], ACT.Exp, scale=-1.0,
                                             bias=negm[:, m % 2:m % 2 + 1],
                                             accum_out=b.rows2[:, t % 2, h, kind:kind + 1]).then_inc(p_soft, 1)
                    else:
                        act.wait_ge(z_ready, j + 1)
                        nc.scalar.activation(zc[:, j % 2, 0:k], zc[:, j % 2, 0:k], ACT.Exp).then_inc(e_done, 1)
                        act.wait_ge(e_done, j + 1)
                        nc.scalar.activation(zc[:, j % 2, 0:k], zc[:, j % 2, 0:k], ACT.Ln, bias=1.0).then_inc(l_ready, 1)

        @block.sync
        def _(sp):
            sp.dma_start(b.reg_a[:], b.h_dram).then_inc(b.h_back, 16)


def stage_turn(b, name, jobs, move=None):
    nc = b.nc
    turned, ev_a, ev_d = (b.sem(f"{name}_{n}") for n in ("turn", "eva", "evd"))
    tiles = [(rows, dst, col, k) for rows, dst, col in jobs for k in range(4)]
    with ExitStack() as ps_ctx:
        ps = [ps_ctx.enter_context(nc.psum_tensor(f"{name}_ps{i}", [P, CH], F32)) for i in range(4)]
        block = ps_ctx.enter_context(nc.Block())

        @block.tensor
        def _(pe):
            for i, (rows, _, _, k) in enumerate(tiles):
                if i >= 4:
                    pe.wait_ge((ev_d, ev_a)[i % 2], (i - 4) // 2 + 1)
                for t in range(NT):
                    mm = nc.tensor.transpose(ps[i % 4][:, t * P:t * P + P], rows[:, t, k * P:k * P + P], b.ident[:])
                mm.then_inc(turned, 1)

        @block.vector
        def _(dve):
            if move is not None:
                nc.vector.tensor_copy(*move)
            for i in range(0, len(tiles), 2):
                _, dst, col, k = tiles[i]
                dve.wait_ge(turned, i + 1)
                if col is None:
                    nc.vector.tensor_copy(dst[:, k, :], ps[i % 4][:]).then_inc(ev_d, 1)
                else:
                    nc.vector.tensor_scalar(dst[:, k, :], ps[i % 4][:], col[:, k:k + 1], None, ALU.mult).then_inc(ev_d, 1)

        @block.scalar
        def _(act):
            for i in range(1, len(tiles), 2):
                _, dst, col, k = tiles[i]
                act.wait_ge(turned, i + 1)
                nc.scalar.activation(dst[:, k, :], ps[i % 4][:], ACT.Copy, scale=1.0 if col is None else col[:, k:k + 1]).then_inc(ev_a, 1)


def stage_merge(b, name, chunks, yaT, ybT, mT, x_load=None, h_wait=None):
    nc = b.nc
    ready, ev, gates, prod, add_ = (b.sem(f"{name}_{n}") for n in ("ready", "ev", "gates", "prod", "add"))
    sg = b.s_ab[:, 16 * U:20 * U].rearrange("p (i g n) -> p i g n", i=2, g=2)
    N = 2 * len(chunks)
    units = [(chunks[i // 2][0], b.chunk(chunks[i // 2][0], j)[:, :, i % 2 * P:i % 2 * P + P], False)
             for i in range(N) for j in range(2)]
    with b.parts_area(), ExitStack() as ps_ctx:
        parts = Parts(b, name, units)
        ps = [[ps_ctx.enter_context(nc.psum_tensor(f"{name}_ps{i}{j}", [P, CH], F32)) for j in range(4)] for i in range(2)]
        block = ps_ctx.enter_context(nc.Block())

        @block.sync
        def _(sp):
            if x_load is not None:
                sp.dma_start(b.x, x_load).then_inc(b.x_in, 16)
            b.load_until(sp, chunks[-1][-1] + 1 + RING)

        @block.tensor
        def _(pe):
            for i in range(N):
                cg, cy = chunks[i // 2]
                n0 = i % 2 * P
                if i % 2 == 0:
                    b.wait_chunk(pe, cy)
                if i >= 2:
                    pe.wait_ge(ev, i - 1)
                bank = ps[i % 2]
                product_T(nc, bank[1][:], b.chunk(cy, 0), n0, yaT, 4)
                parts.pe_T(pe, 2 * i, bank[0][:])
                parts.pe_T(pe, 2 * i + 1, bank[2][:])
                product_T(nc, bank[3][:], b.chunk(cy, 1), n0, ybT, 4).then_inc(ready, 1)
                if i % 2:
                    pe.wait_ge(ready, i + 1)
                    nc.tensor.sem_inc(b.ring_used, 2)

        @block.scalar
        def _(act):
            if h_wait is not None:
                act.wait_ge(h_wait, 16)
            parts.act_w(act, 0)
            parts.act_h(act)
            parts.act_w(act, 1)
            for i in range(N):
                parts.act_w(act, 2 * i + 2)
                parts.act_w(act, 2 * i + 3)
                act.wait_ge(ready, i + 1)
                if i >= 2:
                    act.wait_ge(ev, i - 1)
                nc.scalar.activation(sg[:, i % 2, 0], ps[i % 2][0][:], ACT.Sigmoid)
                nc.scalar.activation(sg[:, i % 2, 1], ps[i % 2][2][:], ACT.Sigmoid).then_inc(gates, 1)

        @block.vector
        def _(dve):
            if h_wait is not None:
                dve.wait_ge(h_wait, 16)
            parts.dve_w(dve, 0)
            parts.dve_h(dve)
            parts.dve_w(dve, 1)
            for i in range(N):
                parts.dve_w(dve, 2 * i + 2)
                parts.dve_w(dve, 2 * i + 3)
                dve.wait_ge(gates, i + 1)
                nc.vector.tensor_tensor(sg[:, i % 2, 0], sg[:, i % 2, 0], ps[i % 2][1][:], ALU.mult)
                nc.vector.tensor_tensor(sg[:, i % 2, 1], sg[:, i % 2, 1], ps[i % 2][3][:], ALU.mult).then_inc(prod, 1)
                dve.wait_ge(prod, i + 1)
                nc.vector.tensor_tensor(mT[:, i, :], sg[:, i % 2, 0], sg[:, i % 2, 1], ALU.add).then_inc(ev, 1)


def stage_rows_out(b, name, srcT, chunks, gate_row=None):
    nc = b.nc
    STEPS = 3
    s_hi, hi, lo, used, ready, ev, prod = (b.sem(f"{name}_{n}") for n in ("s_hi", "w_hi", "lo", "used", "ready", "ev", "prod"))
    steps = [(k, c, k - k0, k == k1 - 1) for k0, k1, c in chunks for k in range(k0, k1)]
    with b.parts_area() as area, ExitStack() as ps_ctx:
        s2 = [b.parts(f"{name}_s{j}", [P, STEPS, T]) for j in range(2)]
        w2 = [b.parts(f"{name}_w{j}", [P, STEPS, D]) for j in range(2)]
        tmp = area.enter_context(nc.sbuf_tensor(f"{name}_tmp", [P, 4, CH], F32, side="right"))
        ps = [ps_ctx.enter_context(nc.psum_tensor(f"{name}_ps{i}", [P, CH], F32)) for i in range(8)]
        block = ps_ctx.enter_context(nc.Block())

        @block.sync
        def _(sp):
            b.load_until(sp, chunks[-1][-1] + 1 + RING)

        @block.scalar
        def _(act):
            for k, c, kc, _ in steps:
                b.wait_chunk(act, c)
                if k >= STEPS:
                    act.wait_ge(used, k - STEPS + 1)
                nc.scalar.copy(s2[0][:, k % STEPS], srcT[:, k, :]).then_inc(s_hi, 1)
                nc.scalar.copy(w2[0][:, k % STEPS], b.chunk(c)[:, kc, :]).then_inc(hi, 1)

        @block.tensor
        def _(pe):
            for k, c, kc, _ in steps:
                pe.wait_ge(lo, 2 * (k + 1))
                i, last = k % STEPS, k == len(steps) - 1
                for t in range(NT):
                    for h in range(2):
                        mm = product_parts(nc, ps[h * NT + t][:], [s2[j][:, i, t * P:t * P + P] for j in range(2)],
                                           [w2[j][:, i, h * CH:h * CH + CH] for j in range(2)], k == 0, last)
                        if last:
                            mm.then_inc(ready, 1)
                if not last:
                    mm.then_inc(used, 1)

        @block.vector
        def _(dve):
            for k, c, kc, chunk_done in steps:
                b.wait_chunk(dve, c)
                i = k % STEPS
                dve.wait_ge(s_hi, k + 1)
                lower(nc, s2[1][:, i], srcT[:, k, :], s2[0][:, i]).then_inc(lo, 1)
                dve.wait_ge(hi, k + 1)
                lower(nc, w2[1][:, i], b.chunk(c)[:, kc, :], w2[0][:, i]).then_inc(lo, 1)
                if chunk_done:
                    dve.wait_ge(lo, 2 * (k + 1))
                    nc.vector.sem_inc(b.ring_used, 1)
            n = 0
            for t in range(NT):
                for h in range(2):
                    cols = slice(h * CH, h * CH + CH)
                    dve.wait_ge(ready, n + 1)
                    src = ps[h * NT + t][:]
                    if gate_row is not None:
                        if n >= 4:
                            dve.wait_ge(ev, n - 3)
                        nc.vector.tensor_tensor(tmp[:, n % 4], src, gate_row[:, cols], ALU.mult).then_inc(prod, 1)
                        dve.wait_ge(prod, n + 1)
                        src = tmp[:, n % 4]
                    nc.vector.tensor_tensor(b.x[:, t, cols], b.x[:, t, cols], src, ALU.add).then_inc(ev, 1)
                    n += 1


def stage_ffn_up(b):
    nc = b.nc
    guT = b.s_ab[:, 0:KF * T].rearrange("p (k t) -> p k t", k=KF)
    silu, ev = (b.sem(f"up_{n}") for n in ("silu", "ev"))
    units = [(b.c_ffn[i // 2], b.chunk(b.c_ffn[i // 2], j)[:, :, i % 2 * P:i % 2 * P + P], i % 2 == 1 and j == 1)
             for i in range(KF) for j in range(2)]
    with b.parts_area(), ExitStack() as ps_ctx:
        parts = Parts(b, "up", units)
        ps = [[ps_ctx.enter_context(nc.psum_tensor(f"up_ps{i}{j}", [P, CH], F32)) for j in range(2)] for i in range(4)]
        block = ps_ctx.enter_context(nc.Block())

        @block.sync
        def _(sp):
            b.load_until(sp, b.c_ffn[-1] + 1 + RING)

        @block.tensor
        def _(pe):
            for i in range(KF):
                if i >= 4:
                    pe.wait_ge(ev, i - 3)
                for j in range(2):
                    parts.pe_T(pe, 2 * i + j, ps[i % 4][j][:])

        @block.scalar
        def _(act):
            parts.act_w(act, 0)
            parts.act_h(act)
            for u in range(len(units)):
                parts.act_w(act, u + 1)
                if u % 2:
                    act.wait_ge(parts.used, u + 1)
                    nc.scalar.activation(guT[:, u // 2, :], ps[u // 2 % 4][0][:], ACT.Silu).then_inc(silu, 1)

        @block.vector
        def _(dve):
            parts.dve_w(dve, 0)
            parts.dve_h(dve)
            for u in range(len(units)):
                parts.dve_w(dve, u + 1)
                if u % 2:
                    i = u // 2
                    dve.wait_ge(silu, i + 1)
                    nc.vector.tensor_tensor(guT[:, i, :], guT[:, i, :], ps[i % 4][1][:], ALU.mult).then_inc(ev, 1)
    return guT


def stage_project2(b):
    nc = b.nc

    def four(u0, inner):
        return b.s_ab[:, u0 * U:(u0 + 4) * U].rearrange("p (a n) -> p a n", a=4)
    b.gu, b.gv, b.hqT, b.hfT, b.hi, b.hog = (four(4 * i, 4) for i in range(6))
    kinds = [(b.gu, ACT.Gelu_apprx_tanh, False), (b.gv, ACT.Gelu_apprx_tanh, False), (b.hqT, ACT.Silu, True),
             (b.hfT, ACT.Sigmoid, True), (b.hog, ACT.Sigmoid, False), (b.hi, ACT.Copy, False)]
    order = [0, 1, 2, 3, 5, 4]
    ev, zero, filled = (b.sem(f"p2_{n}") for n in ("ev", "zero", "filled"))
    b.y_dram = nc.dram_tensor("slot_rows", (SLOTS, D), F32).ap()
    units = [u for j, c in enumerate(b.c_in2) for u in (units_T if kinds[order[j]][2] else units_rows)(b, c)]
    with b.parts_area() as area, ExitStack() as ps_ctx:
        parts = Parts(b, "p2", units)
        zeros = area.enter_context(nc.sbuf_tensor("p2_zeros", [P, CH], F32, side="right"))
        ps = [ps_ctx.enter_context(nc.psum_tensor(f"p2_ps{i}", [P, CH], F32)) for i in range(8)]
        block = ps_ctx.enter_context(nc.Block())

        @block.sync
        def _(sp):
            sp.wait_ge(zero, 1)
            for h in range(2):
                sp.dma_start(b.y_dram[PAIRS * P:, h * CH:(h + 1) * CH].rearrange("(i p) d -> p i d", p=P),
                             zeros[:].unsqueeze(1).to_broadcast([P, SPILL, CH])).then_inc(filled, 16)
            b.load_until(sp, b.c_in2[-1] + 1 + RING)
            sp.wait_ge(filled, 32)

        @block.gpsimd
        def _(pool):
            nc.gpsimd.memset(zeros[:], 0.0).then_inc(zero, 1)

        @block.tensor
        def _(pe):
            for u in range(len(units)):
                bank = ps[u // 4 % 2 * 4:u // 4 % 2 * 4 + 4]
                if kinds[order[u // 4]][2]:
                    if u >= 8:
                        pe.wait_ge(ev, u - 7)
                    parts.pe_T(pe, u, bank[u % 4][:])
                else:
                    if u >= 8 and u % 4 == 0:
                        pe.wait_ge(ev, u - 4)
                    parts.pe_rows(pe, u, bank, u % 4 * 2)

        @block.vector
        def _(dve):
            parts.dve_w(dve, 0)
            parts.dve_h(dve)
            for u in range(1, len(units)):
                parts.dve_w(dve, u)

        @block.scalar
        def _(act):
            parts.act_w(act, 0)
            parts.act_h(act)
            for u in range(len(units)):
                parts.act_w(act, u + 1)
                dst, func, tiled = kinds[order[u // 4]]
                for i in [u] if tiled else range(u - 3, u + 1) if u % 4 == 3 else []:
                    act.wait_ge(parts.used, u + 1)
                    nc.scalar.activation(dst[:, i % 4, :], ps[i % 8][:], func).then_inc(ev, 1)


def stage_gmlp(b):
    nc, a = b.nc, b.a
    DG = CH // GM_GROUPS
    u, v = b.gu, b.gv
    lnrow = b.scr[:, 0:2 * U].rearrange("p (i n) -> p i n", i=2)
    wT = b.scr[:, 2 * U:4 * U].rearrange("p (g t) -> p g t", g=GM_GROUPS)
    w = b.w1flat[:, 0:2 * U].rearrange("p (g s) -> p g s", g=GM_GROUPS)
    sq = b.u_big[:, 0:4 * U].rearrange("p (t n) -> p t n", t=NT)
    st = b.small
    b.tri = b.sb("tri", [P, P])
    loads, pool, chain, squared, root, turned, wmask, normed, ready = (
        b.sem(f"gm_{n}") for n in ("loads", "pool", "chain", "sq", "root", "turn", "wmask", "normed", "ready"))
    with ExitStack() as ps_ctx:
        pw = [ps_ctx.enter_context(nc.psum_tensor(f"gm_w{i}", [P, CH], F32)) for i in range(2)]
        ps = [ps_ctx.enter_context(nc.psum_tensor(f"gm_ps{i}", [P, CH], F32)) for i in range(4)]
        block = ps_ctx.enter_context(nc.Block())

        @block.sync
        def _(sp):
            sp.dma_start(w, a["gm_w_sp_2"][0].rearrange("g t s -> t g s")).then_inc(loads, 16)
            for i, n in enumerate(("gm_ln_g_2", "gm_ln_b_2")):
                sp.dma_start(lnrow[:, i], a[n].partition_broadcast(P).rearrange("p o n -> p (o n)")).then_inc(loads, 16)

        @block.gpsimd
        def _(g):
            nc.gpsimd.memset(b.tri[:], 1.0).then_inc(pool, 1)
            g.wait_ge(pool, 1)
            nc.gpsimd.affine_select(out=b.tri[:], in_=b.tri[:], compare_op=ALU.is_ge, fill=0.0, base=0,
                                    pattern=[[1, P]], channel_multiplier=-1).then_inc(pool, 1)

        @block.tensor
        def _(pe):
            pe.wait_ge(loads, 48)
            for g in range(GM_GROUPS):
                mm = nc.tensor.transpose(pw[g // 4][:, g % 4 * P:g % 4 * P + P], w[:, g, :], b.ident[:])
            mm.then_inc(turned, 1)
            pe.wait_ge(wmask, 1)
            pe.wait_ge(normed, 1)
            for g in range(GM_GROUPS):
                o = ps[g // 2][:, g % 2 * 4 * DG:(g % 2 + 1) * 4 * DG].rearrange("p (c n) -> p c n", c=NT)
                mm = nc.tensor.matmul(o, wT[:, g, :], v[:, :, g * DG:(g + 1) * DG], start=True, stop=True)
                mm.then_inc(ready, 1)

        @block.scalar
        def _(act):
            act.wait_ge(chain, 6)
            for t in range(NT):
                last = nc.scalar.activation(sq[:, t, :], v[:, t, :], ACT.Square, accum_out=st[:, 8 + t:9 + t])
            last.then_inc(squared, 1)
            act.wait_ge(chain, 7)
            nc.scalar.activation(st[:, 8:12], st[:, 8:12], ACT.Sqrt).then_inc(root, 1)

        @block.vector
        def _(dve):
            n = [0]

            def link(ins):
                n[0] += 1
                ins.then_inc(chain, 1)
                dve.wait_ge(chain, n[0])

            link(nc.vector.tensor_reduce(st[:, 0:4], v, AX.X, ALU.add))
            link(nc.vector.tensor_scalar(st[:, 4:8], st[:, 0:4], 1.0 / CH, None, ALU.mult))
            for t in range(NT):
                link(nc.vector.tensor_scalar(v[:, t, :], v[:, t, :], st[:, 4 + t:5 + t], None, ALU.subtract))
            dve.wait_ge(squared, 1)
            link(nc.vector.tensor_scalar(st[:, 8:12], st[:, 8:12], 1.0 / CH, EPS, ALU.mult, ALU.add))
            dve.wait_ge(root, 1)
            link(nc.vector.reciprocal(st[:, 12:16], st[:, 8:12]))
            dve.wait_ge(loads, 48)
            for t in range(NT):
                last = nc.vector.scalar_tensor_tensor(out=v[:, t, :], in0=v[:, t, :], scalar=st[:, 12 + t:13 + t],
                                                      in1=lnrow[:, 0], op0=ALU.mult, op1=ALU.mult)
            link(last)
            nc.vector.tensor_tensor(v, v, lnrow[:, 1:2, :].to_broadcast([P, NT, CH]), ALU.add).then_inc(normed, 1)
            dve.wait_ge(turned, 1)
            dve.wait_ge(pool, 2)
            for i in range(2):
                last = nc.vector.tensor_tensor(wT[:, 4 * i:4 * i + 4, :], pw[i][:].rearrange("p (g t) -> p g t", g=4),
                                               b.tri[:].unsqueeze(1).to_broadcast([P, 4, P]), ALU.mult)
            last.then_inc(wmask, 1)
            for g in range(GM_GROUPS):
                dve.wait_ge(ready, g // 2 * 2 + 2)
                o = ps[g // 2][:, g % 2 * 4 * DG:(g % 2 + 1) * 4 * DG].rearrange("p (c n) -> p c n", c=NT)
                us = u[:, :, g * DG:(g + 1) * DG]
                bias = b.vcol[:, VAT["gm_b_sp_2"] + g:VAT["gm_b_sp_2"] + g + 1]
                nc.vector.scalar_tensor_tensor(out=us, in0=o, scalar=bias, in1=us, op0=ALU.add, op1=ALU.mult)


def stage_hgrn(b):
    nc = b.nc
    NCH = T // HG_CHUNK
    qT, fT, vrows, og = b.hqT, b.hfT, b.hi, b.hog

    def four(reg, u0):
        return reg[:, u0 * U:(u0 + 4) * U].rearrange("p (h t) -> p h t", h=4)
    kT, bT, eb = four(b.u_big, 0), four(b.u_big, 4), four(b.u_big, 8)
    kend, kinv = four(b.s_ab, 0), four(b.s_ab, 4)
    kerows = four(b.u_big, 0)
    attm = four(b.u_big, 4)
    state = [b.u_big[:, (8 + i) * U:(9 + i) * U] for i in range(4)] + [b.s_ab[:, (12 + i) * U:(13 + i) * U] for i in range(4)]
    reset = b.u_big[:, 12 * U:13 * U]
    st = b.small
    lb, omlb, e0, e1, dec = st[:, 0:4], st[:, 4:8], st[:, 8:12], st[:, 12:16], st[:, 16:48].rearrange("p (h c) -> p h c", h=4)
    ss = b.rows2[:].rearrange("p a h b -> p (a h b)")[:, 0:16]
    bmask = b.sb("hg_mask", [P, P], I32)
    bmf = b.scr[:, 0:P]
    sqj = b.scr[:, U:2 * U]
    sem = {n: b.sem(f"hg_{n}") for n in ("pool", "lb", "chain", "f", "ln", "b", "eb", "enb", "kd", "kde", "turn", "ev",
                                         "att", "attm", "ds", "s", "o", "sq", "var", "root", "act", "zero", "y", "bm")}
    l0 = b.vcol[:, VAT["hg_lb_param_2"]:VAT["hg_lb_param_2"] + 4]
    l1 = b.vcol[:, VAT["hg_lb_param_2"] + 4:VAT["hg_lb_param_2"] + 8]

    def per_chunk(x, h=None):
        return x.rearrange("p h (c t) -> p h c t", c=NCH) if h is None else x[:, h, :].rearrange("p (c t) -> p c t", c=NCH)

    with ExitStack() as ps_ctx:
        ps = [ps_ctx.enter_context(nc.psum_tensor(f"hg_ps{i}", [P, CH], F32)) for i in range(8)]
        block = ps_ctx.enter_context(nc.Block())

        @block.gpsimd
        def _(g):
            nc.gpsimd.memset(bmf, 1.0).then_inc(sem["pool"], 1)
            g.wait_ge(sem["pool"], 1)
            nc.gpsimd.affine_select(out=bmf, in_=bmf, compare_op=ALU.is_ge, fill=0.0, base=0,
                                    pattern=[[1, P]], channel_multiplier=-1).then_inc(sem["pool"], 1)
            g.wait_ge(sem["pool"], 2)
            nc.gpsimd.memset(bmf[0:64, 64:128], 0.0).then_inc(sem["pool"], 1)
            g.wait_ge(sem["pool"], 3)
            nc.gpsimd.tensor_copy(bmask[:], bmf).then_inc(sem["bm"], 1)

        @block.vector
        def _(dve):
            n = [0]

            def link(ins, by="chain"):
                n[0] += 1
                ins.then_inc(sem["chain"], 1)
                dve.wait_ge(sem["chain"], n[0])

            nc.vector.memset(reset, 1.0).then_inc(sem["zero"], 1)
            dve.wait_ge(sem["zero"], 1)
            link(nc.vector.memset(reset.rearrange("p (c t) -> p c t", c=NCH)[:, :, 0:1], 0.0))
            link(nc.vector.tensor_tensor(lb, l0, l1, ALU.max))
            link(nc.vector.tensor_tensor(e0, l0, lb, ALU.subtract))
            nc.vector.tensor_tensor(e1, l1, lb, ALU.subtract).then_inc(sem["lb"], 1)
            dve.wait_ge(sem["act"], 1)
            link(nc.vector.tensor_tensor(e1, e0, e1, ALU.add))
            link(nc.vector.reciprocal(e1, e1))
            link(nc.vector.tensor_tensor(lb, e0, e1, ALU.mult))
            link(nc.vector.tensor_scalar(omlb, lb, -1.0, 1.0, ALU.mult, ALU.add))
            for h in range(HG_HEADS):
                nc.vector.tensor_scalar(fT[:, h, :], fT[:, h, :], omlb[:, h:h + 1], lb[:, h:h + 1], ALU.mult, ALU.add).then_inc(sem["f"], 1)
            dve.wait_ge(sem["f"], 4)
            nc.vector.tensor_scalar(kT, fT, -1.0, 1.0, ALU.mult, ALU.add).then_inc(sem["kd"], 1)
            for h in range(HG_HEADS):
                dve.wait_ge(sem["ln"], h + 1)
                nc.vector.tensor_tensor_scan(out=bT[:, h, :], data0=reset, data1=fT[:, h, :], initial=0.0,
                                             op0=ALU.mult, op1=ALU.add).then_inc(sem["b"], 1)
            dve.wait_ge(sem["b"], 4)
            for h in range(HG_HEADS):
                bc = per_chunk(bT, h)
                nc.vector.tensor_tensor(per_chunk(fT, h), bc[:, :, HG_CHUNK - 1:HG_CHUNK].to_broadcast([P, NCH, HG_CHUNK]), bc,
                                        ALU.subtract).then_inc(sem["kde"], 1)
            dve.wait_ge(sem["eb"], 1)
            nc.vector.tensor_tensor(qT, qT, eb, ALU.mult)
            nc.vector.tensor_copy(dec, eb.rearrange("p h (c t) -> p h c t", c=NCH)[:, :, :, HG_CHUNK - 1]).then_inc(sem["kd"], 1)
            dve.wait_ge(sem["enb"], 1)
            nc.vector.tensor_tensor(kinv, kinv, kT, ALU.mult).then_inc(sem["kd"], 1)
            dve.wait_ge(sem["enb"], 2)
            nc.vector.tensor_tensor(kend, fT, kT, ALU.mult).then_inc(sem["kd"], 1)
            link(nc.vector.memset(attm, 0.0))
            for t in range(NT):
                dve.wait_ge(sem["turn"], t + 1)
                nc.vector.tensor_copy(kerows[:, t, :], ps[t][:]).then_inc(sem["ev"], 1)
            dve.wait_ge(sem["bm"], 1)
            for t in range(NT):
                dve.wait_ge(sem["att"], t + 1)
                for h in range(HG_HEADS):
                    last = nc.vector.copy_predicated(attm[:, t, h * P:h * P + P], bmask[:], ps[4 + t][:, h * P:h * P + P])
                last.then_inc(sem["attm"], 1)
            for c in range(NCH - 1):
                dve.wait_ge(sem["ds"], c + 1)
                if c == 0:
                    last = nc.vector.tensor_copy(state[0], ps[0][:])
                else:
                    dve.wait_ge(sem["s"], c)
                    for h in range(HG_HEADS):
                        r = slice(h * P, h * P + P)
                        last = nc.vector.scalar_tensor_tensor(out=state[c][:, r], in0=state[c - 1][:, r], scalar=dec[:, h, c:c + 1],
                                                              in1=ps[c % 2][:, r], op0=ALU.mult, op1=ALU.add)
                last.then_inc(sem["s"], 1)
            dve.wait_ge(sem["sq"], 4)
            link(nc.vector.tensor_scalar(ss, ss, 1.0 / P, EPS, ALU.mult, ALU.add))
            nc.vector.sem_inc(sem["var"], 1)
            dve.wait_ge(sem["root"], 1)
            link(nc.vector.reciprocal(ss, ss))
            for t in range(NT):
                for h in range(HG_HEADS):
                    r = slice(h * P, h * P + P)
                    nc.vector.scalar_tensor_tensor(out=og[:, t, r], in0=ps[(2, 3, 4, 5)[t]][:, r], scalar=ss[:, 4 * t + h:4 * t + h + 1],
                                                   in1=og[:, t, r], op0=ALU.mult, op1=ALU.mult)

        @block.scalar
        def _(act):
            act.wait_ge(sem["lb"], 1)
            nc.scalar.preload_act_table_set("natural_log_exp_and_others")
            nc.scalar.activation(st[:, 8:16], st[:, 8:16], ACT.Exp).then_inc(sem["act"], 1)
            act.wait_ge(sem["kd"], 1)
            for h in range(HG_HEADS):
                nc.scalar.activation(fT[:, h, :], fT[:, h, :], ACT.Ln).then_inc(sem["ln"], 1)
            act.wait_ge(sem["b"], 4)
            nc.scalar.activation(eb, bT, ACT.Exp).then_inc(sem["eb"], 1)
            nc.scalar.activation(kinv, bT, ACT.Exp, scale=-1.0).then_inc(sem["enb"], 1)
            act.wait_ge(sem["kde"], 4)
            nc.scalar.activation(fT, fT, ACT.Exp).then_inc(sem["enb"], 1)
            for t in range(NT):
                act.wait_ge(sem["o"], t + 1)
                if t:
                    act.wait_ge(sem["sq"], t)
                for h in range(HG_HEADS):
                    r = slice(h * P, h * P + P)
                    last = nc.scalar.activation(sqj[:, r], ps[(2, 3, 4, 5)[t]][:, r], ACT.Square, accum_out=ss[:, 4 * t + h:4 * t + h + 1])
                last.then_inc(sem["sq"], 1)
            act.wait_ge(sem["var"], 1)
            nc.scalar.activation(ss, ss, ACT.Sqrt).then_inc(sem["root"], 1)

        @block.tensor
        def _(pe):
            pe.wait_ge(sem["kd"], 4)
            for t in range(NT):
                for h in range(HG_HEADS):
                    mm = nc.tensor.transpose(ps[t][:, h * P:h * P + P], kend[:, h, t * P:t * P + P], b.ident[:])
                mm.then_inc(sem["turn"], 1)
            for t in range(NT):
                for h in range(HG_HEADS):
                    r = slice(t * P, t * P + P)
                    mm = nc.tensor.matmul(ps[4 + t][:, h * P:h * P + P], kinv[:, h, r], qT[:, h, r], start=True, stop=True)
                mm.then_inc(sem["att"], 1)
            pe.wait_ge(sem["ev"], 4)
            for c in range(NCH - 1):
                r = slice(64 * (c % 2), 64 * (c % 2) + 64)
                if c >= 2:
                    pe.wait_ge(sem["s"], c - 1)
                for h in range(HG_HEADS):
                    k = slice(h * P, h * P + P)
                    mm = nc.tensor.matmul(ps[c % 2][:, k], kerows[r, c // 2, k], vrows[r, c // 2, k], start=True, stop=True)
                mm.then_inc(sem["ds"], 1)
            pe.wait_ge(sem["attm"], 4)
            pe.wait_ge(sem["s"], NCH - 1)
            for t in range(NT):
                bank = ps[(2, 3, 4, 5)[t]]
                for h in range(HG_HEADS):
                    k = slice(h * P, h * P + P)
                    for j in range(2):
                        c, o = 2 * t + j, bank[64 * j:64 * j + 64, k]
                        if c:
                            nc.tensor.matmul(o, qT[:, h, c * HG_CHUNK:(c + 1) * HG_CHUNK], state[c - 1][:, k], start=True, stop=False)
                        mm = nc.tensor.matmul(o, attm[:, t, h * P + 64 * j:h * P + 64 * j + 64], vrows[:, t, k],
                                              start=(c == 0), stop=True)
                mm.then_inc(sem["o"], 1)


def stage_router(b):
    nc, a = b.nc, b.a
    at = [0]

    def take(*shape):
        n = int(np.prod(shape))
        v = b.u_big[:, at[0]:at[0] + n]
        at[0] += n
        if len(shape) == 2:
            v = v.rearrange("p (a b) -> p a b", a=shape[0])
        return v
    b.slot = b.sb("slot", [P, 2 * NT], U32)
    b.weight = b.sb("weight", [P, 2 * NT])
    b.tok = b.sb("tok", [P, SLOTS // P], U32)
    b.spill = b.sb("spill", [P, SPILL + 1], I32)
    b.tok_dram = nc.dram_tensor("tok_list", (SLOTS, 1), F32).ap()
    b.wfull = [b.sem(f"ex_w{i}") for i in range(6)]
    expert_buffers(b)
    NE = EGROUPS + EXPERTS
    wr = b.scr[:, 0:KD * NE].rearrange("p (k n) -> p k n", k=KD)
    io32, lg, tg, ohg = take(EXPERTS), take(NT, NE), take(NT, EGROUPS), take(NT, EGROUPS)
    eg, sel, oh1, oh2, m, tt = take(NT, EGROUPS), *(take(NT, EXPERTS) for _ in range(5))
    rank, over, cnt, X, Xi, A, B, tokid = take(NT, EXPERTS), take(NT, EXPERTS), *(take(EXPERTS) for _ in range(5)), take(NT)
    (mg, pg, m1, m2, e2, r2, s1), slotf = (take(NT) for _ in range(7)), take(2 * NT)
    before = take(P)
    spf, cmp_ = take(SPILL), take(SPILL, EXPERTS)
    io16 = take(SPILL)
    zeros = take(P)
    toks = take(P)
    loads, pool, sel_ = b.sem("ro_loads"), b.sem("ro_pool"), b.sem("ro_sel")
    logits, chain, expin, expd, ranks, masks, slots_, scat, back, tt_, zero, turned, nsc = (
        b.sem(f"ro_{n}") for n in ("logits", "chain", "expin", "expd", "ranks", "masks", "slots", "scat", "back", "tt",
                                   "zero", "turned", "nsc"))
    with ExitStack() as ps_ctx:
        ps_l, ps_r, ps_t = (ps_ctx.enter_context(nc.psum_tensor(f"ro_{n}", [P, CH], F32)) for n in "lrt")
        block = ps_ctx.enter_context(nc.Block())

        @block.sync
        def _(sp):
            sp.dma_start(wr[:, :, 0:EGROUPS], feature_tiles(a["w_grp_2"][0], 0, EGROUPS)).then_inc(loads, 16)
            sp.dma_start(wr[:, :, EGROUPS:NE], feature_tiles(a["w_exp_2"][0], 0, EXPERTS)).then_inc(loads, 16)
            sp.wait_ge(pool, 7)
            sp.dma_start(b.tok_dram.rearrange("(b s) o -> b (s o)", s=P), zeros[0:SLOTS // P, :]).then_inc(zero, 16)
            for j in range(2):
                for i, dram in enumerate(expert_weights(b, j)):
                    sp.dma_start(weight_views(b, j)[i], dram).then_inc(b.wfull[3 * j + i], 16)
            sp.wait_ge(scat, 16 * 2 * NT)
            sp.dma_start(toks[0:SLOTS // P, :], b.tok_dram.rearrange("(b s) o -> b (s o)", s=P)).then_inc(back, 16)

        @block.gpsimd
        def _(g):
            def iota(out, pattern, cm=0, base=0):
                nc.gpsimd.iota(out, pattern=pattern, base=base, channel_multiplier=cm,
                               allow_small_or_imprecise_dtypes=True).then_inc(pool, 1)
            iota(io32, [[1, EXPERTS]])
            iota(A, [[CAP, EXPERTS]])
            iota(tokid, [[P, NT]], cm=1)
            iota(io16, [[1, SPILL]])
            nc.gpsimd.memset(before, 1.0).then_inc(pool, 1)
            g.wait_ge(pool, 5)
            nc.gpsimd.affine_select(out=before, in_=before, compare_op=ALU.is_gt, fill=0.0, base=0,
                                    pattern=[[1, P]], channel_multiplier=-1).then_inc(pool, 1)
            nc.gpsimd.memset(zeros, 0.0).then_inc(pool, 1)
            g.wait_ge(slots_, 1)
            g.wait_ge(zero, 16)
            for i in range(2 * NT):
                nc.gpsimd.indirect_dma_start(b.tok_dram, bass.IndirectOffsetOnAxis(b.slot[:, i:i + 1], 0),
                                             tokid[:, i % NT:i % NT + 1], None).then_inc(scat, 16)

        @block.tensor
        def _(pe):
            pe.wait_ge(loads, 32)
            for t in range(NT):
                mm = product_rows(nc, ps_l[:, t * NE:(t + 1) * NE], b.hT, t, wr, KD)
            mm.then_inc(logits, 1)
            pe.wait_ge(pool, 7)
            pe.wait_ge(masks, 1)
            for t in range(NT):
                for u in range(t + 1):
                    mm = nc.tensor.matmul(ps_r[:, t * EXPERTS:(t + 1) * EXPERTS], before if u == t else b.ones[:], m[:, u, :],
                                          start=(u == 0), stop=(u == t))
            for u in range(NT):
                mm = nc.tensor.matmul(ps_r[:, NT * EXPERTS:(NT + 1) * EXPERTS], b.ones[:], m[:, u, :], start=(u == 0), stop=(u == NT - 1))
            mm.then_inc(ranks, 1)
            pe.wait_ge(back, 16)
            nc.tensor.transpose(ps_t[:, 0:SLOTS // P], toks[0:SLOTS // P, :], b.ident[0:SLOTS // P, 0:SLOTS // P]).then_inc(turned, 1)

        @block.scalar
        def _(act):
            act.wait_ge(expin, 1)
            nc.scalar.activation(eg, eg, ACT.Exp).then_inc(expd, 1)
            act.wait_ge(expin, 2)
            nc.scalar.activation(e2, e2, ACT.Exp).then_inc(expd, 1)

        @block.vector
        def _(dve):
            n = [0]

            def link(ins):
                n[0] += 1
                ins.then_inc(chain, 1)
                dve.wait_ge(chain, n[0])

            def wide(v, k):
                return v.unsqueeze(2).to_broadcast([P, NT, k])

            def first_max(values, k, best, onehot):
                link(nc.vector.tensor_reduce(best, values, AX.X, ALU.max))
                link(nc.vector.tensor_tensor(onehot, values, wide(best, k), ALU.is_ge))
                link(nc.vector.scalar_tensor_tensor(out=onehot, in0=onehot, scalar=-64.0, in1=io32[:, 0:k].unsqueeze(1).to_broadcast([P, NT, k]),
                                                    op0=ALU.mult, op1=ALU.add))
                link(nc.vector.tensor_reduce(s1, onehot, AX.X, ALU.min))
                link(nc.vector.tensor_tensor(onehot, onehot, wide(s1, k), ALU.is_equal))

            dve.wait_ge(pool, 7)
            dve.wait_ge(logits, 1)
            link(nc.vector.tensor_copy(lg, ps_l[:, 0:NT * NE].rearrange("p (t n) -> p t n", t=NT)))
            gl, el = lg[:, :, 0:EGROUPS], lg[:, :, EGROUPS:NE]
            first_max(gl, EGROUPS, mg, ohg)
            nc.vector.tensor_tensor(eg, gl, wide(mg, EGROUPS), ALU.subtract).then_inc(expin, 1)
            link(nc.vector.tensor_scalar(tg, ohg, 1.0, 1e30, ALU.subtract, ALU.mult))
            for t in range(NT):
                last = nc.vector.tensor_tensor(sel[:, t, :].rearrange("p (g e) -> p g e", g=EGROUPS), el[:, t, :].rearrange("p (g e) -> p g e", g=EGROUPS),
                                               tg[:, t, :].unsqueeze(2).to_broadcast([P, EGROUPS, EPG]), ALU.add)
            link(last)
            first_max(sel, EXPERTS, m1, oh1)
            link(nc.vector.scalar_tensor_tensor(out=sel, in0=oh1, scalar=-3e30, in1=sel, op0=ALU.mult, op1=ALU.add))
            first_max(sel, EXPERTS, m2, oh2)
            nc.vector.tensor_tensor(m, oh1, oh2, ALU.add).then_inc(masks, 1)
            nc.vector.tensor_tensor(e2, m2, m1, ALU.subtract).then_inc(expin, 1)
            dve.wait_ge(expd, 2)
            link(nc.vector.tensor_reduce(pg, eg, AX.X, ALU.add))
            link(nc.vector.tensor_scalar(r2, e2, 1.0, None, ALU.add))
            link(nc.vector.tensor_tensor(r2, r2, pg, ALU.mult))
            link(nc.vector.reciprocal(b.weight[:, 0:NT], r2))
            nc.vector.tensor_tensor(b.weight[:, NT:2 * NT], b.weight[:, 0:NT], e2, ALU.mult)
            dve.wait_ge(ranks, 1)
            nc.vector.tensor_copy(rank, ps_r[:, 0:NT * EXPERTS].rearrange("p (t n) -> p t n", t=NT))
            link(nc.vector.tensor_copy(cnt, ps_r[:, NT * EXPERTS:(NT + 1) * EXPERTS]))
            link(nc.vector.tensor_scalar(X, cnt, float(CAP), None, ALU.is_gt))
            for more in range(CAP + P, T, P):
                link(nc.vector.scalar_tensor_tensor(out=X, in0=cnt, scalar=float(more), in1=X, op0=ALU.is_gt, op1=ALU.add))
            link(nc.vector.tensor_tensor_scan(out=Xi, data0=X, data1=X, initial=0.0, op0=ALU.add, op1=ALU.bypass))
            link(nc.vector.tensor_tensor(B, Xi, X, ALU.subtract))
            link(nc.vector.tensor_scalar(B, B, float(P), float(PAIRS * P - CAP), ALU.mult, ALU.add))
            link(nc.vector.tensor_tensor(B, B, A, ALU.subtract))
            link(nc.vector.tensor_scalar(over, rank, float(CAP), None, ALU.is_ge))
            wideA, wideB = (v.unsqueeze(1).to_broadcast([P, NT, EXPERTS]) for v in (A, B))
            link(nc.vector.tensor_tensor(over, over, wideB, ALU.mult))
            link(nc.vector.tensor_tensor(over, over, rank, ALU.add))
            link(nc.vector.tensor_tensor(over, over, wideA, ALU.add))
            for k, oh in enumerate((oh1, oh2)):
                link(nc.vector.tensor_tensor(tt, oh, over, ALU.mult))
                link(nc.vector.tensor_reduce(slotf[:, k * NT:(k + 1) * NT], tt, AX.X, ALU.add))
            nc.vector.tensor_copy(b.slot[:], slotf).then_inc(slots_, 1)
            link(nc.vector.tensor_tensor(cmp_, Xi.unsqueeze(1).to_broadcast([P, SPILL, EXPERTS]),
                                         io16.unsqueeze(2).to_broadcast([P, SPILL, EXPERTS]), ALU.is_le))
            link(nc.vector.tensor_reduce(spf, cmp_, AX.X, ALU.add))
            link(nc.vector.tensor_scalar(spf, spf, float(EXPERTS - 1), None, ALU.min))
            nc.vector.tensor_copy(b.spill[:, 0:SPILL], spf)
            nc.vector.tensor_copy(b.spill[:, SPILL:SPILL + 1], Xi[:, EXPERTS - 1:EXPERTS])
            dve.wait_ge(turned, 1)
            nc.vector.tensor_copy(b.tok[:], ps_t[:, 0:SLOTS // P])


def expert_buffers(b):
    b.wslot = [b.ring[:, i] for i in range(RING)] + [b.w1flat[:], b.s_ab[:, 0:8 * U]]
    b.xg = b.s_ab[:, 8 * U:10 * U]
    b.xT = b.s_ab[:, 10 * U:12 * U].rearrange("p (k s) -> p k s", k=KD)
    b.hs, b.hm = b.s_ab[:, 12 * U:13 * U], b.s_ab[:, 13 * U:14 * U]
    b.ys = b.s_ab[:, 14 * U:18 * U].rearrange("p (j n) -> p j n", j=2)
    b.gcol = b.vcol[:, VAT["g_ffn_2"]:VAT["g_ffn_2"] + KD].unsqueeze(2).to_broadcast([P, KD, P])


def weight_views(b, j):
    w1, w3, w2 = b.wslot[3 * j:3 * j + 3]
    return (w1.rearrange("p (k n) -> p k n", k=KD), w3.rearrange("p (k n) -> p k n", k=KD), w2.rearrange("p (k n) -> p k n", k=KE))


def expert_weights(b, e):
    w1, w3, w2 = (b.a[n][0][bass.ds(e, 1)] for n in ("w1_2", "w3_2", "w2_2"))
    return (w1.rearrange("o (k p) n -> p (o k) n", p=P), w3.rearrange("o (k p) n -> p (o k) n", p=P),
            w2.rearrange("o (k p) n -> p (o k) n", p=P))


def turn_rows(nc, ps, xg, ident):
    for k in range(KD):
        mm = nc.tensor.transpose(ps[k // 4][:, k % 4 * P:k % 4 * P + P], xg[:, k * P:(k + 1) * P], ident)
    return mm


def rows_in(nc, b, ps):
    for i in range(2):
        last = nc.vector.tensor_tensor(b.xT[:, 4 * i:4 * i + 4, :], ps[i][:].rearrange("p (k s) -> p k s", k=4),
                                       b.gcol[:, 4 * i:4 * i + 4, :], ALU.mult)
    return last


def expert_in(nc, ps, w, xT, n):
    for i in range(2):
        for f in range(KE):
            for k in range(KD):
                mm = nc.tensor.matmul(ps[i][:, f * n:(f + 1) * n], w[i][:, k, f * P:f * P + P], xT[:, k, :],
                                      start=(k == 0), stop=(k == KD - 1))
    return mm


def expert_out(nc, ps, w2, hm, n):
    for h in range(2):
        for f in range(KE):
            mm = nc.tensor.matmul(ps[h][0:n, :], hm[:, f * n:(f + 1) * n], w2[:, f, h * CH:(h + 1) * CH],
                                  start=(f == 0), stop=(f == KE - 1))
    return mm


def stage_experts(b):
    nc = b.nc
    wfull = b.wfull
    yout = [b.sem(f"ex_out{i}") for i in range(2)]
    xfull, turned, xt, h_done, silu, hm, y_done, y0, y1 = (
        b.sem(f"ex_{n}") for n in ("x", "turn", "xt", "h", "silu", "hm", "y", "y0", "y1"))
    half = [slice(j * KE * CAP, (j + 1) * KE * CAP) for j in range(2)]
    last = PAIRS - 1
    with ExitStack() as ps_ctx:
        ps_x, ps_h1, ps_h3, ps_y = ([ps_ctx.enter_context(nc.psum_tensor(f"ex_{n}{i}", [P, CH], F32)) for i in range(2)]
                                    for n in ("x", "h1", "h3", "y"))
        block = ps_ctx.enter_context(nc.Block())

        @block.sync
        def _(sp):
            def load(s, j):
                for i, dram in enumerate(expert_weights(b, 2 * s + j)):
                    if i == 0:
                        sp.wait_ge(h_done, 2 * s + j - 1)
                    if i == 2:
                        sp.wait_ge(y_done, 2 * s + j - 1)
                    sp.dma_start(weight_views(b, j)[i], dram).then_inc(wfull[3 * j + i], 16)
            with sp.Fori(1, PAIRS) as s:
                load(s, 0)
                load(s, 1)

        @block.gpsimd
        def _(pool):
            for s in range(PAIRS):
                if s:
                    pool.wait_ge(turned, s)
                nc.gpsimd.indirect_dma_start(b.xg, None, b.rows_dram, bass.IndirectOffsetOnAxis(b.tok[:, s:s + 1], 0)).then_inc(xfull, 16)

        @block.tensor
        def _(pe):
            def turn(s):
                pe.wait_ge(xfull, 16 * (s + 1))
                turn_rows(nc, ps_x, b.xg, b.ident[:]).then_inc(turned, 1)

            def inputs(s, j):
                if j == 0:
                    pe.wait_ge(xt, s + 1)
                for i in range(2):
                    pe.wait_ge(wfull[3 * j + i], 16 * (s + 1))
                expert_in(nc, (ps_h1[j], ps_h3[j]), weight_views(b, j), b.xT[:, :, j * CAP:(j + 1) * CAP], CAP).then_inc(h_done, 1)

            def outputs(s, j):
                pe.wait_ge(hm, 2 * s + j + 1)
                pe.wait_ge(wfull[3 * j + 2], 16 * (s + 1))
                pe.wait_ge(y0, 2 * s + j)
                pe.wait_ge(y1, 2 * s + j)
                expert_out(nc, ps_y, weight_views(b, j)[2], b.hm[:, half[j]], CAP).then_inc(y_done, 1)

            turn(0)
            inputs(0, 0)
            inputs(0, 1)
            turn(1)
            outputs(0, 0)
            with pe.Fori(1, last) as s:
                inputs(s, 0)
                outputs(s - 1, 1)
                inputs(s, 1)
                turn(s + 1)
                outputs(s, 0)
            inputs(last, 0)
            outputs(last - 1, 1)
            inputs(last, 1)
            outputs(last, 0)
            outputs(last, 1)

        @block.vector
        def _(dve):
            def x_in(s, again=True):
                dve.wait_ge(turned, s + 1)
                if again:
                    dve.wait_ge(h_done, 2 * s)
                rows_in(nc, b, ps_x).then_inc(xt, 1)

            def product(s, j, again=True):
                dve.wait_ge(silu, 2 * s + j + 1)
                if again:
                    dve.wait_ge(y_done, 2 * s + j - 1)
                nc.vector.tensor_tensor(b.hm[:, half[j]], b.hs[:, half[j]], ps_h3[j][:, 0:KE * CAP], ALU.mult).then_inc(hm, 1)

            def y_half(s, j):
                dve.wait_ge(y_done, 2 * s + j + 1)
                dve.wait_ge(yout[j], 16 * (s + 1))
                nc.vector.tensor_copy(b.ys[0:CAP, j, 0:CH], ps_y[0][0:CAP, :]).then_inc(y0, 1)

            x_in(0, False)
            product(0, 0, False)
            product(0, 1, False)
            x_in(1)
            y_half(0, 0)
            with dve.Fori(1, last) as s:
                product(s, 0)
                y_half(s - 1, 1)
                product(s, 1)
                x_in(s + 1)
                y_half(s, 0)
            product(last, 0)
            y_half(last - 1, 1)
            product(last, 1)
            y_half(last, 0)
            y_half(last, 1)

        @block.scalar
        def _(act):
            def gate(s, j, again=True):
                act.wait_ge(h_done, 2 * s + j + 1)
                if again:
                    act.wait_ge(hm, 2 * s + j - 1)
                nc.scalar.activation(b.hs[:, half[j]], ps_h1[j][:, 0:KE * CAP], ACT.Silu).then_inc(silu, 1)

            def y_half(s, j):
                act.wait_ge(y_done, 2 * s + j + 1)
                act.wait_ge(yout[j], 16 * (s + 1))
                nc.scalar.copy(b.ys[0:CAP, j, CH:2 * CH], ps_y[1][0:CAP, :]).then_inc(y1, 1)
                act.wait_ge(y0, 2 * s + j + 1)
                act.wait_ge(y1, 2 * s + j + 1)
                act.dma_start(b.y_dram[bass.ds((2 * s + j) * CAP, CAP), :], b.ys[0:CAP, j, :]).then_inc(yout[j], 16)

            for j in range(2):
                nc.scalar.sem_inc(yout[j], 16)
            gate(0, 0, False)
            gate(0, 1, False)
            y_half(0, 0)
            with act.Fori(1, last) as s:
                gate(s, 0)
                y_half(s - 1, 1)
                gate(s, 1)
                y_half(s, 0)
            gate(last, 0)
            y_half(last - 1, 1)
            gate(last, 1)
            y_half(last, 0)
            y_half(last, 1)
            for j in range(2):
                act.wait_ge(yout[j], 16 * (PAIRS + 1))


def stage_spill(b):
    nc = b.nc
    wfull, idx, go, xfull, turned, xt, h_done, silu, hm, y_done, ysb, yout = (
        b.sem(f"sp_{n}") for n in ("w", "idx", "go", "x", "turn", "xt", "h", "silu", "hm", "y", "ysb", "out"))
    stage = b.sb("spill_idx", [P, 1], U32)
    with ExitStack() as ps_ctx:
        ps_x, ps_h, ps_y = ([ps_ctx.enter_context(nc.psum_tensor(f"sp_{n}{i}", [P, CH], F32)) for i in range(2)] for n in "xhy")
        block = ps_ctx.enter_context(nc.Block())

        def each(eng, body):
            n = eng.value_load(b.spill[0:1, SPILL:SPILL + 1], min_val=0, max_val=SPILL)
            with eng.If(n > 0):
                with eng.Fori(0, n) as j:
                    body(j)

        @block.sync
        def _(sp):
            def body(j):
                sp.wait_ge(yout, 16 * (j + 1))
                e = sp.value_load(b.spill[0:1, bass.ds(j, 1)], min_val=0, max_val=EXPERTS - 1)
                for w, dram in zip(weight_views(b, 0), expert_weights(b, e)):
                    sp.dma_start(w, dram).then_inc(wfull, 16)
            each(sp, body)

        @block.gpsimd
        def _(pool):
            def body(j):
                pool.wait_ge(yout, 16 * (j + 1))
                nc.gpsimd.tensor_copy(stage[:], b.tok[:, bass.ds(j + PAIRS, 1)]).then_inc(idx, 1)
                pool.wait_ge(idx, j + 1)
                nc.gpsimd.sem_inc(go, 1)
                nc.gpsimd.indirect_dma_start(b.xg, None, b.rows_dram, bass.IndirectOffsetOnAxis(stage[:], 0)).then_inc(xfull, 16)
            each(pool, body)

        @block.tensor
        def _(pe):
            def body(j):
                pe.wait_ge(xfull, 16 * (j + 1))
                turn_rows(nc, ps_x, b.xg, b.ident[:]).then_inc(turned, 1)
                pe.wait_ge(xt, j + 1)
                pe.wait_ge(wfull, 48 * (j + 1))
                expert_in(nc, ps_h, weight_views(b, 0), b.xT, P).then_inc(h_done, 1)
                pe.wait_ge(hm, j + 1)
                expert_out(nc, ps_y, weight_views(b, 0)[2], b.hm, P).then_inc(y_done, 1)
            each(pe, body)

        @block.vector
        def _(dve):
            def body(j):
                dve.wait_ge(turned, j + 1)
                rows_in(nc, b, ps_x).then_inc(xt, 1)
                dve.wait_ge(silu, j + 1)
                nc.vector.tensor_tensor(b.hm, b.hs, ps_h[1][:], ALU.mult).then_inc(hm, 1)
                dve.wait_ge(y_done, j + 1)
                for h in range(2):
                    last = nc.vector.tensor_copy(b.ys[:, 0, h * CH:(h + 1) * CH], ps_y[h][:])
                last.then_inc(ysb, 1)
                dve.wait_ge(yout, 16 * (j + 2))
            each(dve, body)

        @block.scalar
        def _(act):
            def body(j):
                act.wait_ge(h_done, j + 1)
                nc.scalar.activation(b.hs, ps_h[0][:], ACT.Silu).then_inc(silu, 1)
                act.wait_ge(ysb, j + 1)
                act.dma_start(b.y_dram[bass.ds((j + PAIRS) * P, P), :], b.ys[:, 0, :]).then_inc(yout, 16)
                act.wait_ge(yout, 16 * (j + 2))
            nc.scalar.sem_inc(yout, 16)
            each(act, body)


def stage_combine(b):
    nc, a = b.nc, b.a
    b.pg = b.ring[:, 0:2].rearrange("p i n -> p (i n)").rearrange("p (k n) -> p k n", k=KD)
    b.ple = b.ring[:, 2, 0:2 * D].rearrange("p (k n) -> p k n", k=2)
    b.prow = b.ring[:, 2, 2 * D:2 * D + 4 * 256].rearrange("p (t n) -> p t n", t=NT)
    b.frow = b.ring[:, 3, 0:D]
    b.last_in = b.sem("last_in")
    rows, done = [b.sem(f"co_rows{i}") for i in range(2 * NT)], b.sem("co_done")
    ybuf = b.s_ab[:, 8 * U:24 * U].rearrange("p (i n) -> p i n", i=2 * NT)
    with nc.Block() as block:
        @block.sync
        def _(sp):
            sp.dma_start(b.pg, feature_tiles(a["w_pg_2"][0], 0, D)).then_inc(b.last_in, 16)
            sp.dma_start(b.ple, feature_tiles(a["w_ple_2"][0], 0, D)).then_inc(b.last_in, 16)
            sp.dma_start(b.prow, a["p_2"][0, 0].rearrange("(t p) n -> p t n", p=P)).then_inc(b.last_in, 16)
            sp.dma_start(b.frow, a["g_final_2"].partition_broadcast(P)).then_inc(b.last_in, 16)

        @block.gpsimd
        def _(pool):
            for i in range(2 * NT):
                nc.gpsimd.indirect_dma_start(ybuf[:, i, :], None, b.y_dram, bass.IndirectOffsetOnAxis(b.slot[:, i:i + 1], 0)).then_inc(rows[i], 16)

        @block.vector
        def _(dve):
            for i in range(2 * NT):
                t = i % NT
                dve.wait_ge(rows[i], 16)
                if i >= NT:
                    dve.wait_ge(done, i - NT + 1)
                nc.vector.scalar_tensor_tensor(out=b.x[:, t, :], in0=ybuf[:, i, :], scalar=b.weight[:, i:i + 1], in1=b.x[:, t, :],
                                               op0=ALU.mult, op1=ALU.add).then_inc(done, 1)


def stage_embedding(b):
    nc = b.nc
    pT = b.s_ab[:, 0:2 * U].rearrange("p (k t) -> p k t", k=2)
    sg = b.scr[:, 0:4 * U].rearrange("p (i n) -> p i n", i=4)
    turned, pt, ready, gate, prod, ev = (b.sem(f"em_{n}") for n in ("turn", "pt", "ready", "gate", "prod", "ev"))
    with ExitStack() as ps_ctx:
        ps_g, ps_p = ([ps_ctx.enter_context(nc.psum_tensor(f"em_{n}{i}", [P, CH], F32)) for i in range(4)] for n in "gp")
        block = ps_ctx.enter_context(nc.Block())

        @block.tensor
        def _(pe):
            pe.wait_ge(b.last_in, 64)
            for k in range(2):
                for t in range(NT):
                    mm = nc.tensor.transpose(ps_p[k][:, t * P:t * P + P], b.prow[:, t, k * P:k * P + P], b.ident[:])
            mm.then_inc(turned, 1)
            pe.wait_ge(pt, 1)
            for i in range(2 * NT):
                h, t = i // NT, i % NT
                if i >= 4:
                    pe.wait_ge(ev, i - 3)
                product_rows(nc, ps_g[i % 4][:], b.hT, t, b.pg[:, :, h * CH:(h + 1) * CH], KD)
                product_rows(nc, ps_p[i % 4][:], pT, t, b.ple[:, :, h * CH:(h + 1) * CH], 2).then_inc(ready, 1)

        @block.scalar
        def _(act):
            for i in range(2 * NT):
                act.wait_ge(ready, i + 1)
                if i >= 4:
                    act.wait_ge(ev, i - 3)
                nc.scalar.activation(sg[:, i % 4], ps_g[i % 4][:], ACT.Sigmoid).then_inc(gate, 1)

        @block.vector
        def _(dve):
            dve.wait_ge(turned, 1)
            for k in range(2):
                last = nc.vector.tensor_copy(pT[:, k, :], ps_p[k][:])
            last.then_inc(pt, 1)
            for i in range(2 * NT):
                h, t = i // NT, i % NT
                xs = b.x[:, t, h * CH:(h + 1) * CH]
                dve.wait_ge(gate, i + 1)
                nc.vector.tensor_tensor(sg[:, i % 4], sg[:, i % 4], ps_p[i % 4][:], ALU.mult).then_inc(prod, 1)
                dve.wait_ge(prod, i + 1)
                nc.vector.tensor_tensor(xs, xs, sg[:, i % 4], ALU.add).then_inc(ev, 1)


def stage_final(b):
    nc = b.nc
    y = b.u_big[:, 0:NT * D].rearrange("p (t d) -> p t d", t=NT)
    ss = b.small[:, 0:4]
    sq, var, root, inv, done, stored = (b.sem(f"fi_{n}") for n in ("sq", "var", "root", "inv", "done", "stored"))
    with nc.Block() as block:
        @block.scalar
        def _(act):
            for t in range(NT):
                last = nc.scalar.activation(y[:, t, :], b.x[:, t, :], ACT.Square, accum_out=ss[:, t:t + 1])
            last.then_inc(sq, 1)
            act.wait_ge(var, 1)
            nc.scalar.activation(ss, ss, ACT.Sqrt).then_inc(root, 1)

        @block.vector
        def _(dve):
            dve.wait_ge(sq, 1)
            nc.vector.tensor_scalar(ss, ss, 1.0 / D, EPS, ALU.mult, ALU.add).then_inc(var, 1)
            dve.wait_ge(root, 1)
            nc.vector.reciprocal(ss, ss).then_inc(inv, 1)
            dve.wait_ge(inv, 1)
            for t in range(NT):
                nc.vector.scalar_tensor_tensor(out=y[:, t, :], in0=b.x[:, t, :], scalar=ss[:, t:t + 1], in1=b.frow,
                                               op0=ALU.mult, op1=ALU.mult).then_inc(done, 1)

        @block.sync
        def _(sp):
            for t in range(NT):
                sp.wait_ge(done, t + 1)
                sp.dma_start(b.out[0, t * P:(t + 1) * P, :], y[:, t, :]).then_inc(stored, 16)
            sp.wait_ge(stored, 16 * NT)


_INS = ["x", "c", "w_ada", "b_ada", "norm_mix_g", "w_in", "cmp_pos_k", "cmp_w1_k", "cmp_w2_k", "cmp_pos_v",
        "cmp_w1_v", "cmp_w2_v", "w_proj_a", "w_proj_b", "w_out", "norm_ffn_g", "w_ffn_gate", "w_ffn_up",
        "w_ffn_down", "norm_final_g", "p_2", "g_mix_2", "w_in_2", "gm_ln_g_2", "gm_ln_b_2", "gm_w_sp_2",
        "gm_b_sp_2", "w_up_a_2", "hg_lb_param_2", "hg_norm_g_2", "w_up_b_2", "w_out_2", "g_ffn_2", "w_grp_2",
        "w_exp_2", "w1_2", "w3_2", "w2_2", "g_ple_2", "w_pg_2", "w_ple_2", "g_final_2"]


def build(nc, a, out, stop=99):
    with ExitStack() as ctx:
        ctx.enter_context(nc.allow_non_contiguous_dma(reason="small vectors"))
        b = Build(nc, ctx, a, out)
        plan_weights(b)
        b.rows_dram = nc.dram_tensor("normed_rows", (T, D), F32).ap()
        b.h_back = b.sem("h_back")
        yT = [b.s_ab[:, i * 4 * U:(i + 1) * 4 * U].rearrange("p (k t) -> p k t", k=4) for i in range(2)]

        def work_u():
            return b.w1flat[:, 0:4 * U].rearrange("p (k t) -> p k t", k=4)
        mT = b.s_ab[:, 8 * U:16 * U].rearrange("p (k t) -> p k t", k=KD)
        guT = b.s_ab[:, 0:KF * T].rearrange("p (k t) -> p k t", k=KF)

        def vec(name, n=KD):
            return b.vcol[:, VAT[name]:VAT[name] + n]

        def block1_merge(b):
            b.take_x(b.reg_b)
            b.take_h(b.reg_a)
            stage_merge(b, "merge1", b.c_merge1, yT[0], yT[1], mT,
                        x_load=a["x"][0].rearrange("(t p) d -> p t d", p=P), h_wait=b.h_back)

        stages = [
            lambda: stage_constants(b),
            lambda: stage_modulation(b),
            lambda: stage_norm(b, "n1", b.mulcol[:, 0:KD], b.modcol[:, 0:KD], first=True, save=b.h_dram),
            lambda: stage_project1(b),
            lambda: stage_compress(b),
            lambda: stage_attention(b),
            lambda: stage_turn(b, "turn1", [(b.oa, yT[0], None), (b.ob, yT[1], None)]),
            lambda: block1_merge(b),
            lambda: stage_rows_out(b, "out1", mT, b.c_out1, b.g1row),
            b.fresh_sems,
            lambda: stage_norm(b, "n2", b.mulcol[:, KD:2 * KD], b.modcol[:, 2 * KD:3 * KD]),
            lambda: stage_ffn_up(b),
            lambda: stage_rows_out(b, "down", guT, b.c_down, b.g2row),
            b.fresh_sems,
            lambda: stage_norm(b, "n3", vec("g_mix_2"), None, residual_row="norm_final_g"),
            lambda: stage_project2(b),
            lambda: stage_gmlp(b),
            lambda: stage_turn(b, "turn2", [(b.gu, work_u(), None)]),
            lambda: stage_hgrn(b),
            lambda: stage_turn(b, "turn3", [(b.hog, yT[0], vec("hg_norm_g_2", 4))], move=(yT[1], work_u())),
            lambda: stage_merge(b, "merge2", b.c_merge2, yT[1], yT[0], mT),
            lambda: stage_rows_out(b, "out2", mT, b.c_out2),
            b.fresh_sems,
            lambda: stage_norm(b, "n4", vec("g_ffn_2"), None, rows_out=b.rows_dram),
            lambda: stage_router(b),
            lambda: stage_experts(b),
            lambda: stage_spill(b),
            lambda: stage_combine(b),
            lambda: stage_norm(b, "n5", vec("g_ple_2"), None),
            lambda: stage_embedding(b),
            lambda: stage_final(b),
        ]
        for s in stages[:stop]:
            s()
    return b


def kernel(**inputs):
    import concourse.bacc as bacc
    from concourse.bass_utils import run_bass_kernel_spmd

    nc = bacc.Bacc("TRN2", target_bir_lowering=False, num_devices=1)
    arrays, a = {}, {}
    for name in _INS:
        v = np.ascontiguousarray(inputs[name])
        arrays[f"in_{name}"] = v
        a[name] = nc.dram_tensor(f"in_{name}", v.shape, mybir.dt.from_np(v.dtype), kind="ExternalInput").ap()
    out = nc.dram_tensor("out", (1, T, D), F32, kind="ExternalOutput").ap()
    build(nc, a, out)
    r = run_bass_kernel_spmd(nc, [arrays], core_ids=[0])
    return r.results[0]["out"]
```

```python
from contextlib import ExitStack, contextmanager

import numpy as np

import concourse.bass as bass
from concourse import mybir

ALU = mybir.AluOpType
ACT = mybir.ActivationFunctionType
AX = mybir.AxisListType
F32 = mybir.dt.float32
F32R = mybir.dt.float32r
I32 = mybir.dt.int32
U32 = mybir.dt.uint32

P = 128
D = 1024
KD = D // P
T = 512
NT = T // P
CH = 512
HEADS = 8
HD = 64
GROUPS = 2
REP = HEADS // GROUPS
SCALE = HD ** -0.5
CMP_BLOCK, CMP_STRIDE = 32, 16
NCMP = (T - CMP_BLOCK) // CMP_STRIDE + 1
NC = 32
FF = 2816
KF = FF // P
EPS = 1e-6
EXPERTS, EGROUPS = 32, 4
EPG = EXPERTS // EGROUPS
DE = 512
KE = DE // P
CAP = 64
SPILL = 16
PAIRS = EXPERTS // 2
SLOTS = (PAIRS + SPILL) * P
ADA = 6 * D // CH
RING = 4
U = CH
HG_HEADS, HG_CHUNK = 4, 64
GM_GROUPS = 8
NEG = -1e30
MASKED = -1e33
SP_CAP = 60.0


class Chunks:

    def __init__(self):
        self.items = []
        self.landed = []

    def add(self, *parts):
        i = len(self.items)
        before = self.landed[i - RING] if i >= RING else 0
        self.items.append(parts)
        self.landed.append(before + 16 * len(parts))
        return i


def feature_tiles(w, c0, c1):
    return w[:, c0:c1].rearrange("(k p) n -> p k n", p=P)


class Build:

    def __init__(self, nc, ctx, a, out):
        self.nc, self.ctx, self.a, self.out = nc, ctx, a, out
        self.passing = []
        self.ring = self.sb("ring", [P, RING, 8 * CH])
        self.reg_a = self.sb("reg_a", [P, 8 * U])
        self.reg_b = self.sb("reg_b", [P, 8 * U])
        self.s_ab = self.sb("s_ab", [P, 24 * U])
        self.s_a, self.s_b = self.s_ab[:, 0:16 * U], self.s_ab[:, 16 * U:24 * U]
        self.small = self.sb("small", [P, 64])
        self.rows2 = self.sb("rows2", [P, 2, HEADS, 2])
        self.reopened = 0
        self.open_work()
        self.take_x(self.reg_a)
        self.take_h(self.reg_b)
        self.h_dram = nc.dram_tensor("h_saved", (P, 8 * U), F32).ap()
        self.ring_full = [self.lasting_sem(f"ring_full{i}") for i in range(RING)]
        self.ring_used = self.lasting_sem("ring_used")
        self.ada_used = [self.sem(f"ada_used{i}") for i in range(2)]
        self.ch = Chunks()
        self.loaded = 0

    def sb(self, name, shape, dt=F32):
        return self.ctx.enter_context(self.nc.sbuf_tensor(name, shape, dt))

    def open_work(self):
        self.work = ExitStack()
        self.ctx.callback(self.close_work)
        self.w1flat, self.u_big, self.scr = (
            self.work.enter_context(self.nc.sbuf_tensor(f"{n}_{self.reopened}", [P, k * U], F32, side="right"))
            for n, k in (("w1flat", 8), ("u_big", 13), ("scr", 4)))
        self.reopened += 1

    def close_work(self):
        self.work.close()

    @contextmanager
    def parts_area(self):
        self.close_work()
        with ExitStack() as area:
            self.area = area
            yield area
        self.open_work()

    def parts(self, name, shape):
        return self.area.enter_context(self.nc.sbuf_tensor(name, shape, F32R, side="right"))

    def sem(self, name):
        s = self.nc.alloc_semaphore(name=name)
        self.passing.append(s)
        return s

    def lasting_sem(self, name):
        return self.nc.alloc_semaphore(name=name)

    def fresh_sems(self):
        self.nc.clear_and_free_semaphores(self.passing)
        self.passing = []
        self.nc.all_engine_barrier()

    def take_x(self, reg):
        self.x = reg[:].rearrange("p (t d) -> p t d", t=NT)

    def take_h(self, reg):
        self.hT = reg[:].rearrange("p (k t) -> p k t", k=KD)
        self.hTflat = reg

    def chunk(self, i, part=0):
        at = 0
        for p in self.ch.items[i][:part]:
            at += p.shape[1] * p.shape[2]
        _, k, n = self.ch.items[i][part].shape
        return self.ring[:, i % RING, at:at + k * n].rearrange("p (k n) -> p k n", k=k)

    def wait_chunk(self, eng, i):
        eng.wait_ge(self.ring_full[i % RING], self.ch.landed[i])

    def load_until(self, sp, end):
        for i in range(self.loaded, min(end, len(self.ch.items))):
            if i >= RING:
                if i - RING < ADA:
                    sp.wait_ge(self.ada_used[i % 2], (i - RING) // 2 + 1)
                else:
                    sp.wait_ge(self.ring_used, i - RING - ADA + 1)
            for part, dram in enumerate(self.ch.items[i]):
                sp.dma_start(self.chunk(i, part), dram).then_inc(self.ring_full[i % RING], 16)
        self.loaded = max(self.loaded, min(end, len(self.ch.items)))


def plan_weights(b):
    a, add = b.a, b.ch.add

    def by_rows(w):
        k_end = w.shape[0] // P
        return [(k, min(k + 4, k_end), add(feature_tiles(w[k * P:min(k + 4, k_end) * P, :], 0, D)))
                for k in range(0, k_end, 4)]

    b.c_ada = [add(feature_tiles(a["w_ada"][0], j * CH, j * CH + CH)) for j in range(ADA)]
    w = a["w_in"][0]
    ends = [0, 512, 1024, 1304, 1816, 2328, 2840]
    b.c_in = [add(feature_tiles(w, c0, c1)) for c0, c1 in zip(ends, ends[1:])]
    b.c_merge1 = plan_merge(add, w, ends[-1], a["w_proj_a"][0], a["w_proj_b"][0])
    b.c_out1 = by_rows(a["w_out"][0])
    b.c_ffn = [add(feature_tiles(a["w_ffn_gate"][0], j, j + 256), feature_tiles(a["w_ffn_up"][0], j, j + 256))
               for j in range(0, FF, 256)]
    b.c_down = by_rows(a["w_ffn_down"][0])
    w = a["w_in_2"][0]
    b.c_in2 = [add(feature_tiles(w, j * CH, j * CH + CH)) for j in range(6)]
    b.c_merge2 = plan_merge(add, w, 6 * CH, a["w_up_a_2"][0], a["w_up_b_2"][0])
    b.c_out2 = by_rows(a["w_out_2"][0])


def plan_merge(add, w, c0, wa, wb):
    out = []
    for n in range(0, D, 256):
        out.append((add(feature_tiles(w, c0 + n, c0 + n + 256), feature_tiles(w, c0 + D + n, c0 + D + n + 256)),
                    add(feature_tiles(wa, n, n + 256), feature_tiles(wb, n, n + 256))))
    return out


VROWS = [("c", 8), ("norm_mix_g", 8), ("norm_ffn_g", 8), ("g_mix_2", 8), ("g_ffn_2", 8),
         ("g_ple_2", 8), ("hg_norm_g_2", 4), ("hg_lb_param_2", 8), ("gm_b_sp_2", 8)]
VAT = {}
_n = 0
for _name, _k in VROWS:
    VAT[_name] = _n
    _n += _k
NV = _n


def stage_constants(b):
    nc, a = b.nc, b.a
    b.ident = b.sb("ident", [P, P])
    b.ones = b.sb("ones", [P, P])
    b.vcol = b.sb("vcol", [P, NV])
    b.sc = b.sb("silu_c", [P, KD])
    vrow = b.scr[0:NV, 0:P]
    loads, pool_done, cols, cols_out = (b.sem(n) for n in ("k_loads", "k_pool", "k_cols", "k_out"))
    b.x_in, b.bias_in, zeros = b.sem("x_in"), b.sem("ada_bias"), b.sem("ada_zeros")
    b.ada_acc = b.u_big[:, 0:6 * D]
    with nc.psum_tensor("k_ps", [P, CH], F32) as ps, nc.Block() as block:
        @block.sync
        def _(sp):
            for name, k in VROWS:
                n = "a b c -> (a b) c" if len(a[name].shape) == 3 else None
                v = a[name].rearrange(n) if n else a[name].rearrange("a (k p) -> (a k) p", p=P)
                sp.dma_start(vrow[VAT[name]:VAT[name] + k, :], v).then_inc(loads, 16)
            b.load_until(sp, 1)
            sp.wait_ge(zeros, 1)
            sp.dma_start(b.ada_acc[0:1, :], a["b_ada"]).then_inc(b.bias_in, 16)
            b.load_until(sp, RING)

        @block.gpsimd
        def _(pool):
            nc.gpsimd.memset(b.ident[:], 0.0).then_inc(pool_done, 1)
            nc.gpsimd.memset(b.ones[:], 1.0).then_inc(pool_done, 1)
            pool.wait_ge(pool_done, 2)
            nc.gpsimd.affine_select(out=b.ident[:], in_=b.ident[:], compare_op=ALU.not_equal, fill=1.0,
                                    base=0, pattern=[[-1, P]], channel_multiplier=1).then_inc(pool_done, 1)

        @block.tensor
        def _(pe):
            pe.wait_ge(pool_done, 3)
            pe.wait_ge(loads, 16 * len(VROWS))
            nc.tensor.transpose(ps[:, 0:NV], vrow, b.ident[0:NV, 0:NV]).then_inc(cols, 1)

        @block.vector
        def _(dve):
            nc.vector.memset(b.ada_acc, 0.0).then_inc(zeros, 1)
            dve.wait_ge(cols, 1)
            nc.vector.tensor_copy(b.vcol[:], ps[:, 0:NV]).then_inc(cols_out, 1)

        @block.scalar
        def _(act):
            act.wait_ge(cols_out, 1)
            nc.scalar.activation(b.sc[:], b.vcol[:, 0:KD], ACT.Silu)


def stage_modulation(b):
    nc, a = b.nc, b.a
    acc = b.ada_acc
    b.modcol = b.sb("modcol", [P, 4 * KD])
    b.mulcol = b.sb("mulcol", [P, 2 * KD])
    b.g1row = b.sb("g1row", [P, D])
    b.g2row = b.sb("g2row", [P, D])
    step, row_sum, summed, cols, rows, squared, var, root, inv = (
        b.sem(f"ada_{n}") for n in ("step", "row_sum", "summed", "cols", "rows", "squared", "var", "root", "inv"))
    b.n1_rows = b.s_ab[:, 0:8 * U].rearrange("p (t d) -> p t d", t=NT)
    ss = b.small[:, 0:NT]
    COLS = [0, 1, 3, 4]
    with ExitStack() as ps_ctx:
        psc = ps_ctx.enter_context(nc.psum_tensor("ada_psc", [P, CH], F32))
        psr = [ps_ctx.enter_context(nc.psum_tensor(f"ada_psr{i}", [P, CH], F32)) for i in range(4)]
        block = ps_ctx.enter_context(nc.Block())

        @block.sync
        def _(sp):
            b.load_until(sp, b.c_ada[-3])
            sp.dma_start(b.x[:], a["x"][0].rearrange("(t p) d -> p t d", p=P)).then_inc(b.x_in, 16)
            b.load_until(sp, b.c_ada[-1] + 1 + RING)

        @block.vector
        def _(dve):
            dve.wait_ge(b.bias_in, 16)
            n = 0
            for j, c in enumerate(b.c_ada):
                if j == ADA - 2:
                    dve.wait_ge(squared, 1)
                    nc.vector.tensor_scalar(ss, ss, 1.0 / D, EPS, ALU.mult, ALU.add).then_inc(var, 1)
                    dve.wait_ge(root, 1)
                    nc.vector.reciprocal(ss, ss).then_inc(inv, 1)
                if j % 2:
                    dve.wait_ge(row_sum, j // 2 + 1)
                    first = acc[0:1, j * CH:j * CH + CH]
                    nc.vector.tensor_tensor(first, first, psr[j // 2 % 4][0:1, :], ALU.add).then_inc(step, 1)
                    n += 1
                    continue
                b.wait_chunk(dve, c)
                w, s = b.chunk(c), acc[:, j * CH:j * CH + CH]
                for k in range(KD):
                    if n:
                        dve.wait_ge(step, n)
                    last = nc.vector.scalar_tensor_tensor(out=s, in0=w[:, k, :], scalar=b.sc[:, k:k + 1], in1=s,
                                                          op0=ALU.mult, op1=ALU.add).then_inc(step, 1)
                    n += 1
                dve.wait_ge(step, n)
                nc.vector.sem_inc(b.ada_used[0], 1)
            dve.wait_ge(step, n)
            nc.vector.sem_inc(summed, 1)
            dve.wait_ge(cols, 1)
            nc.vector.tensor_copy(b.modcol[:], psc[:, 0:4 * KD]).then_inc(step, 1)
            n += 1
            dve.wait_ge(step, n)
            for i, g in enumerate(("norm_mix_g", "norm_ffn_g")):
                nc.vector.scalar_tensor_tensor(
                    out=b.mulcol[:, i * KD:i * KD + KD], in0=b.modcol[:, (2 * i + 1) * KD:(2 * i + 2) * KD],
                    scalar=1.0, in1=b.vcol[:, VAT[g]:VAT[g] + KD], op0=ALU.add, op1=ALU.mult)
            dve.wait_ge(rows, 4)
            for i in range(4):
                dst = (b.g1row, b.g2row)[i // 2]
                nc.vector.tensor_copy(dst[:, i % 2 * CH:i % 2 * CH + CH], psr[i][:])

        @block.scalar
        def _(act):
            act.wait_ge(b.x_in, 16)
            for t in range(NT):
                last = nc.scalar.activation(b.n1_rows[:, t, :], b.x[:, t, :], ACT.Square, accum_out=ss[:, t:t + 1])
            last.then_inc(squared, 1)
            act.wait_ge(var, 1)
            nc.scalar.activation(ss, ss, ACT.Sqrt).then_inc(root, 1)
            act.wait_ge(inv, 1)
            for t in range(NT):
                nc.scalar.activation(b.n1_rows[:, t, :], b.x[:, t, :], ACT.Copy, scale=ss[:, t:t + 1])

        @block.tensor
        def _(pe):
            for i, c in enumerate(b.c_ada[1::2]):
                b.wait_chunk(pe, c)
                if i >= 4:
                    pe.wait_ge(step, (KD + 1) * (i - 3))
                if i == 5:
                    pe.wait_ge(step, (KD + 1) * i)
                    for j, part in enumerate(COLS):
                        for k in range(KD):
                            mm = nc.tensor.matmul(psc[:, j * KD + k:j * KD + k + 1], acc[:, part * D + k * P:part * D + k * P + P],
                                                  b.ones[:, 0:1], start=True, stop=True)
                    mm.then_inc(cols, 1)
                w = b.chunk(c)
                for k in range(KD):
                    mm = nc.tensor.matmul(psr[i % 4][0:1, :], b.sc[:, k:k + 1], w[:, k, :], start=(k == 0), stop=(k == KD - 1))
                mm.then_inc(row_sum, 1)
                pe.wait_ge(row_sum, i + 1)
                nc.tensor.sem_inc(b.ada_used[1], 1)
            pe.wait_ge(summed, 1)
            for i in range(4):
                c = (2, 5)[i // 2] * D + i % 2 * CH
                nc.tensor.matmul(psr[i][:], b.ones[:], acc[:, c:c + CH], start=True, stop=True).then_inc(rows, 1)


def stage_norm(b, name, mul, add, made=None, rows_out=None,
               residual_row=None, save=None):
    nc = b.nc
    y = b.u_big[:, 0:NT * D].rearrange("p (t d) -> p t d", t=NT)
    ss = b.small[:, 0:16]
    sq_a, sq_d, var, root, inv, y_a, y_d, turned, ev_a, ev_d, passd = (
        b.sem(f"{name}_{n}") for n in ("sqa", "sqd", "var", "root", "inv", "ya", "yd", "turn", "eva", "evd", "pass"))
    row, row_in = b.scr[:, 0:D], b.sem(f"{name}_rowin")
    passes = 0 if made is not None else 2 if residual_row is not None else 1
    if made is not None:
        y = made
    if rows_out is not None:
        b.rows_saved, b.wr_in = b.sem("rows_saved"), b.sem("wr_in")
        b.wr = b.scr[:, 0:KD * (EGROUPS + EXPERTS)].rearrange("p (k n) -> p k n", k=KD)
        y = b.s_ab[:, 8 * U:16 * U].rearrange("p (t d) -> p t d", t=NT)
    with ExitStack() as ps_ctx:
        ps = [ps_ctx.enter_context(nc.psum_tensor(f"{name}_ps{i}", [P, CH], F32)) for i in range(KD)]
        block = ps_ctx.enter_context(nc.Block())

        @block.sync
        def _(sp):
            if residual_row is not None:
                sp.dma_start(row, b.a[residual_row].partition_broadcast(P)).then_inc(row_in, 16)
            if rows_out is not None:
                sp.dma_start(b.wr[:, :, 0:EGROUPS], feature_tiles(b.a["w_grp_2"][0], 0, EGROUPS)).then_inc(b.wr_in, 16)
                sp.dma_start(b.wr[:, :, EGROUPS:], feature_tiles(b.a["w_exp_2"][0], 0, EXPERTS)).then_inc(b.wr_in, 16)
                sp.wait_ge(y_a, NT // 2)
                sp.wait_ge(y_d, NT // 2)
                sp.dma_start(rows_out.rearrange("(t p) d -> p t d", p=P), y).then_inc(b.rows_saved, 16)
            if save is not None:
                sp.wait_ge(ev_a, KD // 2)
                sp.wait_ge(ev_d, KD // 2)
                sp.dma_start(save, b.hTflat[:]).then_inc(b.h_saved, 16)

        @block.scalar
        def _(act):
            for r in range(passes):
                if r:
                    act.wait_ge(passd, 1)
                for t in range(0, NT, 2):
                    act_ = nc.scalar.activation(y[:, t, :], b.x[:, t, :], ACT.Square, accum_out=ss[:, 4 * r + t:4 * r + t + 1])
                act_.then_inc(sq_a, 1)
                act.wait_ge(var, r + 1)
                nc.scalar.activation(ss[:, 4 * r:4 * r + 4], ss[:, 4 * r:4 * r + 4], ACT.Sqrt).then_inc(root, 1)
            if passes:
                act.wait_ge(inv, passes)
            for t in range(0, NT, 2) if passes else []:
                nc.scalar.activation(y[:, t, :], b.x[:, t, :], ACT.Copy, scale=ss[:, 4 * passes - 4 + t:4 * passes - 3 + t]).then_inc(y_a, 1)
            for k in range(1, KD, 2):
                act.wait_ge(turned, k + 1)
                nc.scalar.activation(b.hT[:, k, :], ps[k][:], ACT.Identity, scale=mul[:, k:k + 1],
                                     bias=add[:, k:k + 1] if add is not None else 0.0).then_inc(ev_a, 1)

        @block.vector
        def _(dve):
            for r in range(passes):
                s = ss[:, 4 * r:4 * r + 4]
                for t in range(1, NT, 2):
                    nc.vector.tensor_tensor_reduce(out=y[:, t, :], in0=b.x[:, t, :], in1=b.x[:, t, :], scale=1.0, scalar=0.0,
                                                   op0=ALU.mult, op1=ALU.add, accum_out=ss[:, 4 * r + t:4 * r + t + 1]).then_inc(sq_d, 1)
                dve.wait_ge(sq_a, r + 1)
                dve.wait_ge(sq_d, NT // 2 * (r + 1))
                nc.vector.tensor_scalar(s, s, 1.0 / D, EPS, ALU.mult, ALU.add).then_inc(var, 1)
                dve.wait_ge(root, r + 1)
                nc.vector.reciprocal(s, s).then_inc(inv, 1)
                dve.wait_ge(inv, r + 1)
                if r < passes - 1:
                    dve.wait_ge(row_in, 16)
                for t in range(NT) if r < passes - 1 else range(1, NT, 2):
                    rs = ss[:, 4 * r + t:4 * r + t + 1]
                    if r < passes - 1:
                        last = nc.vector.scalar_tensor_tensor(out=b.x[:, t, :], in0=b.x[:, t, :], scalar=rs,
                                                              in1=row, op0=ALU.mult, op1=ALU.mult)
                    else:
                        nc.vector.tensor_scalar(y[:, t, :], b.x[:, t, :], rs, None, ALU.mult).then_inc(y_d, 1)
                if r < passes - 1:
                    last.then_inc(passd, 1)
                    dve.wait_ge(passd, 1)
            for k in range(0, KD, 2):
                dve.wait_ge(turned, k + 1)
                if add is not None:
                    nc.vector.tensor_scalar(b.hT[:, k, :], ps[k][:], mul[:, k:k + 1], add[:, k:k + 1],
                                            ALU.mult, ALU.add).then_inc(ev_d, 1)
                else:
                    nc.vector.tensor_scalar(b.hT[:, k, :], ps[k][:], mul[:, k:k + 1], None,
                                            ALU.mult).then_inc(ev_d, 1)

        @block.tensor
        def _(pe):
            for t in range(NT):
                if passes:
                    pe.wait_ge((y_a, y_d)[t % 2], t // 2 + 1)
                for k in range(KD):
                    mm = nc.tensor.transpose(ps[k][:, t * P:t * P + P], y[:, t, k * P:k * P + P], b.ident[:])
                    if t == NT - 1:
                        mm.then_inc(turned, 1)


def product_T(nc, ps, w, n0, hT, kt):
    for k in range(kt):
        mm = nc.tensor.matmul(ps, w[:, k, n0:n0 + P], hT[:, k, :], start=(k == 0), stop=(k == kt - 1))
    return mm


def product_rows(nc, ps, hT, t, w, kt, start=True, stop=True):
    for k in range(kt):
        mm = nc.tensor.matmul(ps, hT[:, k, t * P:t * P + P], w[:, k, :],
                              start=start and k == 0, stop=stop and k == kt - 1)
    return mm



def lower(nc, lo, v, hi):
    return nc.vector.tensor_tensor(lo, v, hi.bitcast(F32), ALU.subtract)


def product_parts(nc, ps, x, y, start, stop):
    nc.tensor.matmul(ps, x[0], y[0], start=start, stop=False)
    nc.tensor.matmul(ps, x[0], y[1], start=False, stop=False)
    return nc.tensor.matmul(ps, x[1], y[0], start=False, stop=stop)


class Parts:

    def __init__(self, b, name, units, release=True, wait=None):
        self.wait_in = wait or b.wait_chunk
        self.b, self.nc, self.units, self.release = b, b.nc, units, release
        self.h = [b.parts(f"{name}_h{i}", [P, KD, T]) for i in range(2)]
        self.w = [[b.parts(f"{name}_w{i}{j}", [P, D]) for j in range(2)] for i in range(2)]
        self.h_hi, self.h_lo, self.hi, self.lo, self.used = (
            b.sem(f"{name}_{n}") for n in ("h_hi", "h_lo", "w_hi", "w_lo", "w_used"))

    def unit(self, u, part):
        v = self.units[u][1]
        return self.w[u % 2][part][:].rearrange("p (k n) -> p k n", k=v.shape[1])

    def act_h(self, act):
        for k in range(KD):
            self.nc.scalar.copy(self.h[0][:, k, :], self.b.hT[:, k, :]).then_inc(self.h_hi, 1)

    def dve_h(self, dve):
        for k in range(KD):
            dve.wait_ge(self.h_hi, k + 1)
            lower(self.nc, self.h[1][:, k, :], self.b.hT[:, k, :], self.h[0][:, k, :]).then_inc(self.h_lo, 1)

    def act_w(self, act, u):
        if u >= len(self.units):
            return
        c, v, _ = self.units[u]
        self.wait_in(act, c)
        if u >= 2:
            act.wait_ge(self.used, u - 1)
        self.nc.scalar.copy(self.unit(u, 0), v).then_inc(self.hi, 1)

    def dve_w(self, dve, u):
        if u >= len(self.units):
            return
        c, v, last = self.units[u]
        self.wait_in(dve, c)
        dve.wait_ge(self.hi, u + 1)
        lower(self.nc, self.unit(u, 1), v, self.unit(u, 0)).then_inc(self.lo, 1)
        if last and self.release:
            dve.wait_ge(self.lo, u + 1)
            self.nc.vector.sem_inc(self.b.ring_used, 1)

    def pe_T(self, pe, u, bank, done=None):
        pe.wait_ge(self.lo, u + 1)
        for k in range(KD):
            if u == 0:
                pe.wait_ge(self.h_lo, k + 1)
            mm = product_parts(self.nc, bank, [self.unit(u, j)[:, k, :] for j in range(2)],
                               [self.h[j][:, k, :] for j in range(2)], k == 0, k == KD - 1)
        mm.then_inc(self.used, 1)

    def pe_rows(self, pe, u, banks, k0):
        pe.wait_ge(self.lo, u + 1)
        for t in range(NT):
            for k in range(2):
                if u < 4 and t == 0:
                    pe.wait_ge(self.h_lo, k0 + k + 1)
                mm = product_parts(self.nc, banks[t][:], [self.h[j][:, k0 + k, t * P:t * P + P] for j in range(2)],
                                   [self.unit(u, j)[:, k, :] for j in range(2)], k0 + k == 0, k0 + k == KD - 1)
        mm.then_inc(self.used, 1)


def units_T(b, c, part=0, n=CH):
    return [(c, b.chunk(c, part)[:, :, n0:n0 + P], n0 + P == n) for n0 in range(0, n, P)]


def units_rows(b, c):
    return [(c, b.chunk(c)[:, k0:k0 + 2, :], k0 + 2 == KD) for k0 in range(0, KD, 2)]


def compression_weights(b):
    posr = b.scr[0:32, 640:896]
    w1 = [r[:, 0:4 * U].rearrange("p (m n) -> p m n", m=CMP_BLOCK // 2) for r in (b.reg_a, b.w1flat)]
    w2 = b.scr[:, 960:1216]
    return posr, w1, w2


def compression_first(b, sp, i):
    w = b.a[("cmp_w1_k", "cmp_w1_v")[i]][0].rearrange("(m o d) n -> o d m n", d=HD, o=2)
    for odd in range(2):
        sp.dma_start(compression_weights(b)[1][i][64 * odd:64 * odd + 64], w[odd]).then_inc(b.cmp_in, 16)


def stage_project1(b):
    nc, a = b.nc, b.a
    b.cmp_in = b.sem("cmp_in")
    b.qT = b.s_a[:, 0:4 * T].rearrange("p (n t) -> p n t", n=4)
    b.sqT = b.s_a[:, 4 * T:8 * T].rearrange("p (n t) -> p n t", n=4)
    b.skT = b.s_a[:, 8 * T:12 * T].rearrange("p (n t) -> p n t", n=4)
    b.sv = b.s_a[:, 12 * T:16 * T].rearrange("p (t n) -> p t n", t=NT)
    b.kk = [b.s_b[:, i * 2 * T:(i + 1) * 2 * T].rearrange("p (g t) -> p g t", g=2) for i in range(2)]
    b.kvc = [b.reg_a[:, (4 + 2 * i) * T:(6 + 2 * i) * T].rearrange("p (g t) -> p g t", g=2) for i in range(2)]
    b.vv = [b.s_b[:, (6 + i) * T:(7 + i) * T].rearrange("p (t n) -> p t n", t=NT) for i in range(2)]
    b.gate = b.sb("gate", [P, NT, 24])

    tiles = [(0, n * P, "q", b.qT[:, n, :]) for n in range(4)]
    tiles += [(1, 0, "dup", b.kvc[0]), (1, P, "dup", b.kvc[1]), (1, 2 * P, "dup", b.kk[0]), (1, 3 * P, "rows", b.vv[0])]
    tiles += [(2, 0, "dup", b.kk[1]), (2, P, "rows", b.vv[1]), (2, 2 * P, "gate", b.gate)]
    tiles += [(3, n * P, "q", b.sqT[:, n, :]) for n in range(4)]
    tiles += [(4, n * P, "T", b.skT[:, n, :]) for n in range(4)]
    tiles += [(5, t, "wide", b.sv[:, t, :]) for t in range(4)]
    NB = 6
    def directs(i):
        return sum(t[2] in ("rows", "gate") for t in tiles[:i + 1])

    direct, ev_a, ev_d = (b.sem(f"p1_{n}") for n in ("direct", "eva", "evd"))
    units, unit_of = [], []
    for i, (c, n0, kind, _) in enumerate(tiles):
        unit_of.append(len(units))
        if kind == "wide":
            if n0 == 0:
                units += units_rows(b, b.c_in[c])
        elif kind in ("q", "T", "dup"):
            units.append((b.c_in[c], b.chunk(b.c_in[c])[:, :, n0:n0 + P], False))
    with b.parts_area(), ExitStack() as ps_ctx:
        parts = Parts(b, "p1", units, release=False)
        ps = [ps_ctx.enter_context(nc.psum_tensor(f"p1_ps{i}", [P, CH], F32)) for i in range(NB)]
        block = ps_ctx.enter_context(nc.Block())

        @block.sync
        def _(sp):
            sp.wait_ge(b.h_saved, 16)
            compression_first(b, sp, 0)
            b.load_until(sp, b.c_in[-1] + 1 + RING)

        @block.tensor
        def _(pe):
            for i, (c, n0, kind, _) in enumerate(tiles):
                if i >= NB and not (kind == "wide" and n0):
                    pe.wait_ge((ev_d, ev_a)[i % 2], (i - NB) // 2 + 1)
                bank = ps[i % NB]
                if kind in ("q", "T", "dup"):
                    parts.pe_T(pe, unit_of[i], bank[:])
                elif kind != "wide":
                    w = b.chunk(b.c_in[c])
                    b.wait_chunk(pe, b.c_in[c])
                    n = P if kind == "rows" else 24
                    for t in range(NT):
                        mm = product_rows(nc, bank[:, t * n:t * n + n], b.hT, t, w[:, :, n0:n0 + n], KD)
                elif n0 == 0:
                    for j in range(1, NT):
                        pe.wait_ge((ev_d, ev_a)[(i + j) % 2], (i + j - NB) // 2 + 1)
                    for j in range(4):
                        parts.pe_rows(pe, unit_of[i] + j, [ps[(i + t) % NB] for t in range(NT)], 2 * j)
                if kind in ("rows", "gate"):
                    mm.then_inc(direct, 1)
                    if i + 1 < len(tiles) and tiles[i + 1][0] != c:
                        pe.wait_ge(direct, directs(i))
                        nc.tensor.sem_inc(b.ring_used, 1)
                elif i + 1 == len(tiles) or tiles[i + 1][0] != c:
                    nc.tensor.sem_inc(b.ring_used, 1)

        def split_ahead(eng, split, i):
            first = 1 if i == 0 else until(i - 1)
            for u in range(first, until(i)):
                split(eng, u)

        def until(i):
            return len(units) if tiles[i][2] == "wide" else min(unit_of[i] + 2, len(units))

        def move(eng, copy, scaled, i, done):
            _, _, kind, dst = tiles[i]
            bank = ps[i % NB]
            if kind in ("rows", "gate"):
                eng.wait_ge(direct, directs(i))
            else:
                eng.wait_ge(parts.used, len(units) if kind == "wide" else unit_of[i] + 1)
            if kind == "q":
                last = scaled(dst, bank[:])
            elif kind in ("T", "wide"):
                last = copy(dst, bank[:])
            elif kind == "dup":
                for half in range(2):
                    for g in range(2):
                        last = copy(dst[64 * half:64 * half + 64, g, :], bank[64 * g:64 * g + 64, :])
            elif kind == "rows":
                last = copy(dst, bank[:].rearrange("p (t n) -> p t n", t=NT))
            else:
                last = copy(dst[:], bank[:, 0:NT * 24].rearrange("p (t n) -> p t n", t=NT))
            last.then_inc(done, 1)

        @block.vector
        def _(dve):
            parts.dve_w(dve, 0)
            parts.dve_h(dve)
            for i in range(len(tiles)):
                split_ahead(dve, parts.dve_w, i)
                if i % 2 == 0:
                    move(dve, nc.vector.tensor_copy, lambda o, s: nc.vector.tensor_scalar(o, s, SCALE, None, ALU.mult), i, ev_d)

        @block.scalar
        def _(act):
            parts.act_w(act, 0)
            parts.act_h(act)
            for i in range(len(tiles)):
                split_ahead(act, parts.act_w, i)
                if i % 2:
                    move(act, nc.scalar.copy, lambda o, s: nc.scalar.mul(o, s, SCALE), i, ev_a)


def stage_compress(b):
    nc, a = b.nc, b.a
    b.bias = b.u_big[:, 0:HEADS * T].rearrange("p (h k) -> p h k", h=HEADS)
    b.sbmask = b.u_big[:, 8 * T:9 * T]
    b.oa = b.u_big[:, 9 * T:13 * T].rearrange("p (t n) -> p t n", t=NT)
    nd = b.scr[:, 0:T]
    ndc = b.scr[:, T:T + NT * NC].rearrange("p (t n) -> p t n", t=NT)
    posT = b.scr[:, 896:960].rearrange("p (b l) -> p b l", b=2)
    posr, w1, w2 = compression_weights(b)
    kp = b.hTflat[:, 0:2 * 1024].rearrange("p (b g m n) -> p b g m n", b=2, g=GROUPS, m=CMP_BLOCK // 2)
    hid = b.hTflat[:, 2048:2048 + 4 * NC].rearrange("p (b g n) -> p b g n", b=2, g=2)
    kc = b.hTflat[:, 2304:2304 + 4 * NC].rearrange("p (o g n) -> p o g n", o=2, g=2)
    vbd = b.hTflat[:, 2560:2560 + 2 * REP * HD].rearrange("p (g n) -> p g n", g=2)
    cs = b.hTflat[:, 3072:4096].rearrange("p (t h n) -> p t h n", t=NT, h=HEADS)
    csum, cfac = (b.hTflat[:, i:i + NT * HEADS].rearrange("p (t h) -> p t h", t=NT) for i in (2432, 2464))
    pTc = b.hTflat[:, 0:2 * NT * P].rearrange("p (t g q) -> p t g q", t=NT, g=2)
    st = b.small
    pool, sel, win, hsum, hact, kcp, kco, dchain, sc, scm, expd, pt, pte, o, gsig, vz = (
        b.sem(f"cmp_{n}") for n in ("pool", "sel", "win", "hsum", "hact", "kcp", "kco", "chain", "sc", "scm",
                                    "exp", "pt", "pte", "o", "gsig", "vz"))
    slopes = [2.0 ** -(h + 1) for h in range(HEADS)]
    with ExitStack() as ps_ctx:
        def bank(n):
            return ps_ctx.enter_context(nc.psum_tensor(f"cmp_{n}", [P, CH], F32))
        ps_k, ps_h, ps_t, ps_s = bank("k"), bank("h"), [bank("t0"), bank("t1")], [bank("s0"), bank("s1")]
        ps_pos, ps_o = ps_t[0], [bank("o0"), bank("o1"), ps_k, ps_h]
        block = ps_ctx.enter_context(nc.Block())

        @block.sync
        def _(sp):
            for i, n in enumerate("kv"):
                for half in range(2):
                    cols = slice((2 * i + half) * HD, (2 * i + half + 1) * HD)
                    sp.dma_start(posr[:, cols], a[f"cmp_pos_{n}"][0]).then_inc(b.cmp_in, 16)
                    sp.dma_start(w2[:, cols], a[f"cmp_w2_{n}"][0]).then_inc(b.cmp_in, 16)
            compression_first(b, sp, 1)

        @block.gpsimd
        def _(pool_):
            nc.gpsimd.iota(nd, pattern=[[1, T]], base=-(T - P), channel_multiplier=-1,
                           allow_small_or_imprecise_dtypes=True).then_inc(pool, 1)
            nc.gpsimd.iota(ndc, pattern=[[-P, NT], [CMP_STRIDE, NC]], base=CMP_BLOCK - 1, channel_multiplier=-1,
                           allow_small_or_imprecise_dtypes=True).then_inc(pool, 1)
            nc.gpsimd.memset(b.sbmask, 0.0).then_inc(pool, 1)
            nc.gpsimd.memset(st[:, 40:41], 1.0).then_inc(pool, 1)
            pool_.wait_ge(pool, 4)
            nc.gpsimd.affine_select(out=nd, in_=nd, compare_op=ALU.is_ge, fill=MASKED, base=T - P,
                                    pattern=[[-1, T]], channel_multiplier=1).then_inc(sel, 1)
            nc.gpsimd.affine_select(out=ndc, in_=ndc, compare_op=ALU.is_ge, fill=MASKED, base=-(CMP_BLOCK - 1),
                                    pattern=[[P, NT], [-CMP_STRIDE, NC]], channel_multiplier=1).then_inc(sel, 1)
            nc.gpsimd.affine_select(out=b.sbmask, in_=b.sbmask, compare_op=ALU.is_gt, fill=NEG, base=T - P,
                                    pattern=[[-1, T]], channel_multiplier=1).then_inc(sel, 1)
            nc.gpsimd.affine_select(out=st[:, 40:41], in_=st[:, 40:41], compare_op=ALU.is_ge, fill=0.0,
                                    base=-(CMP_BLOCK - 1), pattern=[[0, 1]], channel_multiplier=1).then_inc(sel, 1)

        @block.tensor
        def _(pe):
            pe.wait_ge(b.cmp_in, 16 * 12)
            for i in range(2):
                mm = nc.tensor.transpose(ps_pos[:, 32 * i:32 * i + 32], posr[:, 2 * i * HD:2 * (i + 1) * HD], b.ident[0:32, 0:32])
            mm.then_inc(kcp, 1)
            for i in range(2):
                pe.wait_ge(win, i + 1)
                for m in range(CMP_BLOCK // 2):
                    mm = nc.tensor.matmul(ps_h[:, i * 2 * NC:(i + 1) * 2 * NC], w1[i][:, m, :], kp[:, i, :, m, :],
                                          start=(m == 0), stop=(m == CMP_BLOCK // 2 - 1))
                mm.then_inc(hsum, 1)
            pe.wait_ge(hact, 1)
            for g in range(2):
                nc.tensor.matmul(ps_k[:, g * NC:(g + 1) * NC], w2[:, 0:2 * HD], hid[:, 0, g, :], start=True, stop=True)
            for g in range(2):
                mm = nc.tensor.matmul(ps_k[0:NC, P + g * HD:P + (g + 1) * HD], hid[:, 1, g, :], w2[:, 2 * HD:3 * HD],
                                      start=True, stop=True)
            mm.then_inc(kco, 1)
            pe.wait_ge(dchain, 1)
            for t in range(NT):
                for h in range(HEADS):
                    at = (t * HEADS + h) // 2 * NC
                    mm = nc.tensor.matmul(ps_s[h % 2][:, at:at + NC], b.qT[:, h // 2, t * P:t * P + P],
                                          kc[:, h % 2, h // REP, :], start=True, stop=True)
            mm.then_inc(sc, 1)
            pe.wait_ge(expd, 1)
            for t in range(NT):
                for g in range(2):
                    at = (t % 2 * 2 + g) * P
                    mm = nc.tensor.transpose(ps_t[t // 2][:, at:at + P], cs[:, t, g * REP:(g + 1) * REP, :].rearrange("p h n -> p (h n)"), b.ident[:])
                if t % 2:
                    mm.then_inc(pt, 1)
            for t in range(NT):
                pe.wait_ge(pte, t // 2 + 1)
                for g in range(2):
                    mm = nc.tensor.matmul(ps_o[t][:, g * REP * HD:(g + 1) * REP * HD], pTc[:, t, g, :], vbd[:, g, :],
                                          start=True, stop=True)
                mm.then_inc(o, 1)

        @block.vector
        def _(dve):
            n = [0]

            def link(ins):
                n[0] += 1
                ins.then_inc(vz, 1)
                dve.wait_ge(vz, n[0])

            nc.vector.memset(kp[:, :, :, :, NCMP:NC], 0.0)
            nc.vector.memset(kc, 0.0)
            link(nc.vector.memset(vbd, 0.0))
            dve.wait_ge(kcp, 1)
            link(nc.vector.tensor_copy(posT, ps_pos[:, 0:64].rearrange("p (b l) -> p b l", b=2)))
            for i in range(2):
                s = b.kvc[i].rearrange("p g (n m o) -> p o g m n", o=2, m=CMP_STRIDE // 2)
                pos = posT[:, i].rearrange("p (m o) -> p o m", o=2)
                for odd in range(2):
                    rows = slice(64 * odd, 64 * odd + 64)
                    for half in range(2):
                        m = slice(half * CMP_STRIDE // 2, (half + 1) * CMP_STRIDE // 2)
                        for g in range(GROUPS):
                            last = nc.vector.tensor_tensor(
                                kp[rows, i, g, m, 0:NCMP], s[rows, odd, g, :, half:half + NCMP],
                                pos[rows, odd, m].unsqueeze(2).to_broadcast([64, CMP_STRIDE // 2, NCMP]), ALU.add)
                last.then_inc(win, 1)
            dve.wait_ge(sel, 4)
            for h in range(HEADS):
                nc.vector.tensor_scalar(b.bias[:, h, :], nd, slopes[h], None, ALU.mult)
                nc.vector.tensor_scalar(cs[:, :, h, :], ndc, slopes[h], None, ALU.mult).then_inc(scm, 1)
            dve.wait_ge(kco, 1)
            for odd in range(2):
                rows = slice(64 * odd, 64 * odd + 64)
                nc.vector.tensor_copy(kc[rows, odd], ps_k[rows, 0:2 * NC].rearrange("p (g n) -> p g n", g=2))
            for g in range(2):
                for r in range(REP):
                    last = nc.vector.tensor_copy(vbd[NC * r:NC * r + NC, g, r * HD:(r + 1) * HD], ps_k[0:NC, P + g * HD:P + (g + 1) * HD])
            last.then_inc(dchain, 1)
            dve.wait_ge(gsig, 1)
            dve.wait_ge(scm, HEADS)
            dve.wait_ge(sc, 1)
            for odd in range(2):
                c = cs[:, :, odd::2, :]
                last = nc.vector.tensor_tensor(c, c, ps_s[odd][:].rearrange("p (t h n) -> p t h n", t=NT, h=HEADS // 2), ALU.add)
            link(last)
            wide = csum.unsqueeze(3).to_broadcast([P, NT, HEADS, NC])
            link(nc.vector.tensor_reduce(csum, cs, AX.X, ALU.max))
            link(nc.vector.tensor_tensor(cs, cs, wide, ALU.subtract))
            nc.vector.sem_inc(dchain, 1)
            dve.wait_ge(expd, 1)
            link(nc.vector.tensor_reduce(csum, cs, AX.X, ALU.add))
            link(nc.vector.reciprocal(cfac, csum))
            link(nc.vector.tensor_tensor(cfac, cfac, b.gate[:].rearrange("p t (h b) -> p t h b", b=3)[:, :, :, 0], ALU.mult))
            link(nc.vector.tensor_scalar(cfac[:, 0, :], cfac[:, 0, :], st[:, 40:41], None, ALU.mult))
            for i in range(2):
                dve.wait_ge(pt, i + 1)
                nc.vector.tensor_copy(pTc[:, 2 * i:2 * i + 2], ps_t[i][:].rearrange("p (t g q) -> p t g q", t=2, g=2)).then_inc(pte, 1)
            for t in range(NT):
                dve.wait_ge(o, t + 1)
                nc.vector.tensor_tensor(b.oa[:, t, :].rearrange("p (h n) -> p h n", h=HEADS), ps_o[t][:].rearrange("p (h n) -> p h n", h=HEADS),
                                        cfac[:, t, :].unsqueeze(2).to_broadcast([P, HEADS, HD]), ALU.mult)

        @block.scalar
        def _(act):
            nc.scalar.activation(b.gate[:], b.gate[:], ACT.Sigmoid).then_inc(gsig, 1)
            act.wait_ge(hsum, 2)
            nc.scalar.activation(hid, ps_h[:, 0:4 * NC].rearrange("p (b g n) -> p b g n", b=2, g=2), ACT.Gelu_apprx_tanh).then_inc(hact, 1)
            act.wait_ge(dchain, 2)
            nc.scalar.activation(cs, cs, ACT.Exp).then_inc(expd, 1)


def stage_attention(b):
    nc = b.nc
    b.ob = b.hTflat[:, 0:4 * T].rearrange("p (t n) -> p t n", t=NT)
    PER = 3 * HEADS
    units = [(t, i // 3, i % 3) for t in range(NT) for i in range(PER)]
    N = len(units)
    STEPS = N + 8

    def bufs(reg, u0, n):
        return reg[:, u0 * U:(u0 + n) * U].rearrange("p (i k) -> p i k", i=n)
    prob, ssb = bufs(b.w1flat, 0, 6), bufs(b.w1flat, 6, 2)
    qz = b.reg_a[:].rearrange("p (i k o h q) -> p i k o h q", i=2, k=2, o=2, h=HEADS // 2)
    q_in, q_zero = b.sem("at_q"), b.sem("at_qzero")
    zbuf, zc, ex = bufs(b.hTflat, 4, 2), bufs(b.hTflat, 6, 2), bufs(b.s_b, 4, 2)
    ptsb = b.scr[:, 0:3 * T].rearrange("p (i k) -> p i k", i=3)
    tmp = b.scr[:, 3 * T:4 * T]
    negm = b.small[:, 0:4]
    fac = b.small[:, 24:40].rearrange("p (h b) -> p h b", b=2)
    (sc_ready, s_taken, p_soft, z_ready, e_done, l_ready, chain, w_ready, p_stick, pt_ready, pt_a, pt_d, pv,
     o_moved) = (b.sem(f"at_{n}") for n in (
         "scores", "taken", "psoft", "z", "e", "l", "chain", "w", "pstick", "pt", "pta", "ptd", "pv", "omoved"))

    def keys(i):
        return (units[i][0] + 1) * P

    def at(s, lag):
        return s - lag if 0 <= s - lag < N else None

    def soft_count(i):
        return (i // 3) * 2 + min(i % 3 + 1, 2)

    def wait_moved(eng, i):
        if i % 3 == 2:
            eng.wait_ge(pt_d, i // 3 + 1)
        else:
            eng.wait_ge(pt_a, soft_count(i))

    with ExitStack() as ps_ctx:
        def bank(n):
            return ps_ctx.enter_context(nc.psum_tensor(f"at_{n}", [P, CH], F32))
        ps_s = [bank(f"s{i}") for i in range(3)]
        ps_t = [bank(f"t{i}") for i in range(2)]
        ps_o = [bank(f"o{i}") for i in range(3)]
        block = ps_ctx.enter_context(nc.Block())

        @block.tensor
        def _(pe):
            for s in range(STEPS):
                i = at(s, 0)
                if i is not None:
                    t, h, kind = units[i]
                    if i >= 3:
                        pe.wait_ge(s_taken, i - 2)
                    if i % PER == 0:
                        pe.wait_ge(q_in, 4 * (t + 1))
                    q = qz[:, t % 2, kind // 2, h % 2, h // 2, :]
                    k = b.skT[:, h // 2, 0:keys(i)] if kind == 2 else b.kk[kind][:, h // REP, 0:keys(i)]
                    nc.tensor.matmul(ps_s[i % 3][:, 0:keys(i)], q, k, start=True, stop=True).then_inc(sc_ready, 1)
                i = at(s, 5)
                if i is not None:
                    if i % 3 == 2:
                        pe.wait_ge(p_stick, i // 3 + 1)
                    else:
                        pe.wait_ge(p_soft, soft_count(i))
                    if i >= 2:
                        wait_moved(pe, i - 2)
                    for c in range(0, keys(i), P):
                        mm = nc.tensor.transpose(ps_t[i % 2][:, c:c + P], prob[:, i % 6, c:c + P], b.ident[:])
                    mm.then_inc(pt_ready, 1)
                i = at(s, 7)
                if i is not None:
                    t, h, kind = units[i]
                    if i % PER == 0 and i:
                        pe.wait_ge(o_moved, t)
                    wait_moved(pe, i)
                    for c in range(t + 1):
                        v = b.sv[:, c, h * HD:(h + 1) * HD] if kind == 2 else b.vv[kind][:, c, h // REP * HD:(h // REP + 1) * HD]
                        mm = nc.tensor.matmul(ps_o[kind][:, h * HD:(h + 1) * HD], ptsb[:, i % 3, c * P:c * P + P], v,
                                              start=(c == 0), stop=(c == t))
                    mm.then_inc(pv, 1)

        @block.vector
        def _(dve):
            n = [0]

            def link(ins):
                n[0] += 1
                ins.then_inc(chain, 1)
                return n[0]

            def linked(ins):
                dve.wait_ge(chain, link(ins))

            def spread(t):
                if t >= 2:
                    dve.wait_ge(sc_ready, PER * (t - 1))
                for kind, q in enumerate((b.qT, b.sqT)):
                    for odd in range(2):
                        r = slice(64 * odd, 64 * odd + 64)
                        nc.vector.tensor_copy(qz[r, t % 2, kind, odd], q[r, :, t * P:t * P + P]).then_inc(q_in, 1)

            linked(nc.vector.memset(qz[:, 0], 0.0))
            spread(0)
            dve.wait_ge(q_zero, 1)
            spread(1)
            ex_made = {}
            for s in range(STEPS + 1):
                i = at(s, 1)
                if i is not None:
                    t, h, kind = units[i]
                    k, j = keys(i), i // 3
                    if i % PER == PER // 2 and 1 <= t < NT - 1:
                        spread(t + 1)
                    off = T - k
                    dve.wait_ge(sc_ready, i + 1)
                    if kind < 2:
                        m = soft_count(i) - 1
                        if m >= 2:
                            dve.wait_ge(p_soft, m - 1)
                        nc.vector.tensor_tensor_reduce(out=ssb[:, m % 2, 0:k], in0=ps_s[i % 3][:, 0:k], in1=b.bias[:, h, off:T],
                                                       scale=-1.0, scalar=3e38, op0=ALU.add, op1=ALU.min,
                                                       accum_out=negm[:, m % 2:m % 2 + 1]).then_inc(s_taken, 1)
                    else:
                        if j >= 2:
                            dve.wait_ge(p_stick, j - 1)
                        nc.vector.tensor_tensor(zbuf[:, j % 2, 0:k], ps_s[i % 3][:, 0:k], b.sbmask[:, off:T], ALU.add).then_inc(s_taken, 1)
                        dve.wait_ge(s_taken, i + 1)
                        nc.vector.tensor_scalar(zc[:, j % 2, 0:k], zbuf[:, j % 2, 0:k], SP_CAP, None, ALU.min).then_inc(z_ready, 1)
                        ex_made[j] = link(nc.vector.tensor_scalar(ex[:, j % 2, 0:k], zbuf[:, j % 2, 0:k], SP_CAP, 0.0, ALU.subtract, ALU.max))
                i = at(s, 6)
                if i is not None and i % 3 == 2:
                    dve.wait_ge(pt_ready, i + 1)
                    if i >= 3:
                        dve.wait_ge(pv, i - 2)
                    nc.vector.tensor_copy(ptsb[:, i % 3, 0:keys(i)], ps_t[i % 2][:, 0:keys(i)]).then_inc(pt_d, 1)
                i = at(s, 3)
                if i is not None and i % 3 == 2:
                    k, j = keys(i), i // 3
                    dve.wait_ge(l_ready, j + 1)
                    dve.wait_ge(chain, ex_made[j])
                    linked(nc.vector.tensor_tensor_scan(out=ex[:, j % 2, 0:k][:, ::-1], data0=zc[:, j % 2, 0:k][:, ::-1],
                                                        data1=ex[:, j % 2, 0:k][:, ::-1], initial=0.0, op0=ALU.add, op1=ALU.add))
                    nc.vector.tensor_tensor(zc[:, j % 2, 0:k], zbuf[:, j % 2, 0:k], ex[:, j % 2, 0:k], ALU.subtract).then_inc(w_ready, 1)
                i = s - 8
                if i >= 0 and i % PER == PER - 1:
                    t = units[i][0]
                    dve.wait_ge(pv, i + 1)
                    gates = b.gate[:, t, :].rearrange("p (h b) -> p h b", b=3)
                    linked(nc.vector.reciprocal(fac, b.rows2[:, t % 2]))
                    linked(nc.vector.tensor_tensor(fac, fac, gates[:, :, 1:3], ALU.mult))
                    oa = b.oa[:, t, :].rearrange("p (h n) -> p h n", h=HEADS)
                    tm = tmp.rearrange("p (h n) -> p h n", h=HEADS)
                    for kind in range(2):
                        linked(nc.vector.tensor_tensor(tm, ps_o[kind][:].rearrange("p (h n) -> p h n", h=HEADS),
                                                       fac[:, :, kind].unsqueeze(2).to_broadcast([P, HEADS, HD]), ALU.mult))
                        linked(nc.vector.tensor_tensor(oa, oa, tm, ALU.add))
                    nc.vector.tensor_copy(b.ob[:, t, :], ps_o[2][:]).then_inc(o_moved, 1)

        @block.scalar
        def _(act):
            nc.scalar.preload_act_table_set("natural_log_exp_and_others")
            for s in range(STEPS):
                i = at(s, 6)
                if i is not None and i % 3 != 2:
                    act.wait_ge(pt_ready, i + 1)
                    if i >= 3:
                        act.wait_ge(pv, i - 2)
                    nc.scalar.copy(ptsb[:, i % 3, 0:keys(i)], ps_t[i % 2][:, 0:keys(i)]).then_inc(pt_a, 1)
                i = at(s, 4)
                if i is not None and i % 3 == 2:
                    j = i // 3
                    act.wait_ge(w_ready, j + 1)
                    if i >= 6:
                        act.wait_ge(pt_ready, i - 5)
                    nc.scalar.activation(prob[:, i % 6, 0:keys(i)], zc[:, j % 2, 0:keys(i)], ACT.Exp).then_inc(p_stick, 1)
                i = at(s, 2)
                if i is not None:
                    t, h, kind = units[i]
                    k, j = keys(i), i // 3
                    if kind < 2:
                        m = soft_count(i) - 1
                        act.wait_ge(s_taken, i + 1)
                        if i >= 6:
                            act.wait_ge(pt_ready, i - 5)
                        if t >= 2 and i % PER == 0:
                            act.wait_ge(o_moved, t - 1)
                        nc.scalar.activation(prob[:, i % 6, 0:k], ssb[:, m % 2, 0:k], ACT.Exp, scale=-1.0,
                                             bias=negm[:, m % 2:m % 2 + 1],
                                             accum_out=b.rows2[:, t % 2, h, kind:kind + 1]).then_inc(p_soft, 1)
                    else:
                        act.wait_ge(z_ready, j + 1)
                        nc.scalar.activation(zc[:, j % 2, 0:k], zc[:, j % 2, 0:k], ACT.Exp).then_inc(e_done, 1)
                        act.wait_ge(e_done, j + 1)
                        nc.scalar.activation(zc[:, j % 2, 0:k], zc[:, j % 2, 0:k], ACT.Ln, bias=1.0).then_inc(l_ready, 1)

        @block.gpsimd
        def _(pool):
            nc.gpsimd.memset(qz[:, 1], 0.0).then_inc(q_zero, 1)


def stage_turn(b, name, jobs, move=None, reload=False):
    nc = b.nc
    turned, ev_a, ev_d = (b.sem(f"{name}_{n}") for n in ("turn", "eva", "evd"))
    tiles = [(rows, dst, col, k) for rows, dst, col in jobs for k in range(4)]
    with ExitStack() as ps_ctx:
        ps = [ps_ctx.enter_context(nc.psum_tensor(f"{name}_ps{i}", [P, CH], F32)) for i in range(4)]
        block = ps_ctx.enter_context(nc.Block())

        @block.sync
        def _(sp):
            if reload:
                sp.dma_start(b.reg_a[:], b.h_dram).then_inc(b.h_back, 16)

        @block.tensor
        def _(pe):
            for i, (rows, _, _, k) in enumerate(tiles):
                if i >= 4:
                    pe.wait_ge((ev_d, ev_a)[i % 2], (i - 4) // 2 + 1)
                for t in range(NT):
                    mm = nc.tensor.transpose(ps[i % 4][:, t * P:t * P + P], rows[:, t, k * P:k * P + P], b.ident[:])
                mm.then_inc(turned, 1)

        @block.vector
        def _(dve):
            if move is not None:
                nc.vector.tensor_copy(*move)
            for i in range(0, len(tiles), 2):
                _, dst, col, k = tiles[i]
                dve.wait_ge(turned, i + 1)
                if col is None:
                    nc.vector.tensor_copy(dst[:, k, :], ps[i % 4][:]).then_inc(ev_d, 1)
                else:
                    nc.vector.tensor_scalar(dst[:, k, :], ps[i % 4][:], col[:, k:k + 1], None, ALU.mult).then_inc(ev_d, 1)

        @block.scalar
        def _(act):
            for i in range(1, len(tiles), 2):
                _, dst, col, k = tiles[i]
                act.wait_ge(turned, i + 1)
                nc.scalar.activation(dst[:, k, :], ps[i % 4][:], ACT.Copy, scale=1.0 if col is None else col[:, k:k + 1]).then_inc(ev_a, 1)


def stage_merge(b, name, chunks, yaT, ybT, mT, x_load=None, h_wait=None):
    nc = b.nc
    ready, ev, gates, prod, add_ = (b.sem(f"{name}_{n}") for n in ("ready", "ev", "gates", "prod", "add"))
    sg = b.s_ab[:, 16 * U:20 * U].rearrange("p (i g n) -> p i g n", i=2, g=2)
    N = 2 * len(chunks)
    units = [(chunks[i // 2][0], b.chunk(chunks[i // 2][0], j)[:, :, i % 2 * P:i % 2 * P + P], False)
             for i in range(N) for j in range(2)]
    with b.parts_area(), ExitStack() as ps_ctx:
        parts = Parts(b, name, units)
        ps = [[ps_ctx.enter_context(nc.psum_tensor(f"{name}_ps{i}{j}", [P, CH], F32)) for j in range(4)] for i in range(2)]
        block = ps_ctx.enter_context(nc.Block())

        @block.sync
        def _(sp):
            if x_load is not None:
                sp.dma_start(b.x, x_load).then_inc(b.x_in, 16)
            b.load_until(sp, chunks[-1][-1] + 1 + RING)

        @block.tensor
        def _(pe):
            for i in range(N):
                cg, cy = chunks[i // 2]
                n0 = i % 2 * P
                if i % 2 == 0:
                    b.wait_chunk(pe, cy)
                if i >= 2:
                    pe.wait_ge(ev, i - 1)
                bank = ps[i % 2]
                product_T(nc, bank[1][:], b.chunk(cy, 0), n0, yaT, 4)
                parts.pe_T(pe, 2 * i, bank[0][:])
                parts.pe_T(pe, 2 * i + 1, bank[2][:])
                product_T(nc, bank[3][:], b.chunk(cy, 1), n0, ybT, 4).then_inc(ready, 1)
                if i % 2:
                    pe.wait_ge(ready, i + 1)
                    nc.tensor.sem_inc(b.ring_used, 2)

        @block.scalar
        def _(act):
            if h_wait is not None:
                act.wait_ge(h_wait, 16)
            parts.act_w(act, 0)
            parts.act_h(act)
            parts.act_w(act, 1)
            for i in range(N):
                parts.act_w(act, 2 * i + 2)
                parts.act_w(act, 2 * i + 3)
                act.wait_ge(ready, i + 1)
                if i >= 2:
                    act.wait_ge(ev, i - 1)
                nc.scalar.activation(sg[:, i % 2, 0], ps[i % 2][0][:], ACT.Sigmoid)
                nc.scalar.activation(sg[:, i % 2, 1], ps[i % 2][2][:], ACT.Sigmoid).then_inc(gates, 1)

        @block.vector
        def _(dve):
            if h_wait is not None:
                dve.wait_ge(h_wait, 16)
            parts.dve_w(dve, 0)
            parts.dve_h(dve)
            parts.dve_w(dve, 1)
            for i in range(N):
                parts.dve_w(dve, 2 * i + 2)
                parts.dve_w(dve, 2 * i + 3)
                dve.wait_ge(gates, i + 1)
                nc.vector.tensor_tensor(sg[:, i % 2, 0], sg[:, i % 2, 0], ps[i % 2][1][:], ALU.mult)
                nc.vector.tensor_tensor(sg[:, i % 2, 1], sg[:, i % 2, 1], ps[i % 2][3][:], ALU.mult).then_inc(prod, 1)
                dve.wait_ge(prod, i + 1)
                nc.vector.tensor_tensor(mT[:, i, :], sg[:, i % 2, 0], sg[:, i % 2, 1], ALU.add).then_inc(ev, 1)


def stage_rows_out(b, name, srcT, chunks, gate_row=None):
    nc = b.nc
    STEPS = 3
    s_hi, hi, lo, used, ready, ev, prod = (b.sem(f"{name}_{n}") for n in ("s_hi", "w_hi", "lo", "used", "ready", "ev", "prod"))
    steps = [(k, c, k - k0, k == k1 - 1) for k0, k1, c in chunks for k in range(k0, k1)]
    with b.parts_area() as area, ExitStack() as ps_ctx:
        s2 = [b.parts(f"{name}_s{j}", [P, STEPS, T]) for j in range(2)]
        w2 = [b.parts(f"{name}_w{j}", [P, STEPS, D]) for j in range(2)]
        tmp = area.enter_context(nc.sbuf_tensor(f"{name}_tmp", [P, 4, CH], F32, side="right"))
        ps = [ps_ctx.enter_context(nc.psum_tensor(f"{name}_ps{i}", [P, CH], F32)) for i in range(8)]
        block = ps_ctx.enter_context(nc.Block())

        @block.sync
        def _(sp):
            b.load_until(sp, chunks[-1][-1] + 1 + RING)

        @block.scalar
        def _(act):
            for k, c, kc, _ in steps:
                b.wait_chunk(act, c)
                if k >= STEPS:
                    act.wait_ge(used, k - STEPS + 1)
                nc.scalar.copy(s2[0][:, k % STEPS], srcT[:, k, :]).then_inc(s_hi, 1)
                nc.scalar.copy(w2[0][:, k % STEPS], b.chunk(c)[:, kc, :]).then_inc(hi, 1)

        @block.tensor
        def _(pe):
            K = len(steps)
            for ks in [[k] for k in range(K - 2)] + [[K - 2, K - 1]]:
                pe.wait_ge(lo, 2 * (ks[-1] + 1))
                for t in range(NT):
                    for h in range(2):
                        for k in ks:
                            i = k % STEPS
                            mm = product_parts(nc, ps[h * NT + t][:], [s2[j][:, i, t * P:t * P + P] for j in range(2)],
                                               [w2[j][:, i, h * CH:h * CH + CH] for j in range(2)], k == 0, k == K - 1)
                        if len(ks) == 2:
                            mm.then_inc(ready, 1)
                if len(ks) == 1:
                    mm.then_inc(used, 1)

        @block.vector
        def _(dve):
            for k, c, kc, chunk_done in steps:
                b.wait_chunk(dve, c)
                i = k % STEPS
                dve.wait_ge(s_hi, k + 1)
                lower(nc, s2[1][:, i], srcT[:, k, :], s2[0][:, i]).then_inc(lo, 1)
                dve.wait_ge(hi, k + 1)
                lower(nc, w2[1][:, i], b.chunk(c)[:, kc, :], w2[0][:, i]).then_inc(lo, 1)
                if chunk_done:
                    dve.wait_ge(lo, 2 * (k + 1))
                    nc.vector.sem_inc(b.ring_used, 1)
            n = 0
            for t in range(NT):
                for h in range(2):
                    cols = slice(h * CH, h * CH + CH)
                    dve.wait_ge(ready, n + 1)
                    src = ps[h * NT + t][:]
                    if gate_row is not None:
                        if n >= 4:
                            dve.wait_ge(ev, n - 3)
                        nc.vector.tensor_tensor(tmp[:, n % 4], src, gate_row[:, cols], ALU.mult).then_inc(prod, 1)
                        dve.wait_ge(prod, n + 1)
                        src = tmp[:, n % 4]
                    nc.vector.tensor_tensor(b.x[:, t, cols], b.x[:, t, cols], src, ALU.add).then_inc(ev, 1)
                    n += 1


def stage_ffn_up(b):
    nc = b.nc
    guT = b.s_ab[:, 0:KF * T].rearrange("p (k t) -> p k t", k=KF)
    silu, ev = (b.sem(f"up_{n}") for n in ("silu", "ev"))
    units = [(b.c_ffn[i // 2], b.chunk(b.c_ffn[i // 2], j)[:, :, i % 2 * P:i % 2 * P + P], i % 2 == 1 and j == 1)
             for i in range(KF) for j in range(2)]
    with b.parts_area(), ExitStack() as ps_ctx:
        parts = Parts(b, "up", units)
        ps = [[ps_ctx.enter_context(nc.psum_tensor(f"up_ps{i}{j}", [P, CH], F32)) for j in range(2)] for i in range(4)]
        block = ps_ctx.enter_context(nc.Block())

        @block.sync
        def _(sp):
            b.load_until(sp, b.c_ffn[-1] + 1 + RING)

        @block.tensor
        def _(pe):
            for i in range(KF):
                if i >= 4:
                    pe.wait_ge(ev, i - 3)
                for j in range(2):
                    parts.pe_T(pe, 2 * i + j, ps[i % 4][j][:])

        @block.scalar
        def _(act):
            parts.act_w(act, 0)
            parts.act_h(act)
            for u in range(len(units)):
                parts.act_w(act, u + 1)
                if u % 2:
                    act.wait_ge(parts.used, u + 1)
                    nc.scalar.activation(guT[:, u // 2, :], ps[u // 2 % 4][0][:], ACT.Silu).then_inc(silu, 1)

        @block.vector
        def _(dve):
            parts.dve_w(dve, 0)
            parts.dve_h(dve)
            for u in range(len(units)):
                parts.dve_w(dve, u + 1)
                if u % 2:
                    i = u // 2
                    dve.wait_ge(silu, i + 1)
                    nc.vector.tensor_tensor(guT[:, i, :], guT[:, i, :], ps[i % 4][1][:], ALU.mult).then_inc(ev, 1)
    return guT


def stage_project2(b):
    nc = b.nc

    def four(u0, inner):
        return b.s_ab[:, u0 * U:(u0 + 4) * U].rearrange("p (a n) -> p a n", a=4)
    b.gu, b.gv, b.hqT, b.hfT, b.hi, b.hog = (four(4 * i, 4) for i in range(6))
    kinds = [(b.gu, ACT.Gelu_apprx_tanh, False), (b.gv, ACT.Gelu_apprx_tanh, False), (b.hqT, ACT.Silu, True),
             (b.hfT, ACT.Sigmoid, True), (b.hog, ACT.Sigmoid, False), (b.hi, ACT.Copy, False)]
    order = [0, 1, 2, 3, 5, 4]
    ev, zero, filled = (b.sem(f"p2_{n}") for n in ("ev", "zero", "filled"))
    b.y_dram = nc.dram_tensor("slot_rows", (SLOTS, D), F32).ap()
    units = [u for j, c in enumerate(b.c_in2) for u in (units_T if kinds[order[j]][2] else units_rows)(b, c)]
    with b.parts_area() as area, ExitStack() as ps_ctx:
        parts = Parts(b, "p2", units)
        zeros = area.enter_context(nc.sbuf_tensor("p2_zeros", [P, CH], F32, side="right"))
        ps = [ps_ctx.enter_context(nc.psum_tensor(f"p2_ps{i}", [P, CH], F32)) for i in range(8)]
        block = ps_ctx.enter_context(nc.Block())

        @block.sync
        def _(sp):
            sp.wait_ge(zero, 1)
            for h in range(2):
                sp.dma_start(b.y_dram[PAIRS * P:, h * CH:(h + 1) * CH].rearrange("(i p) d -> p i d", p=P),
                             zeros[:].unsqueeze(1).to_broadcast([P, SPILL, CH])).then_inc(filled, 16)
            b.load_until(sp, b.c_in2[-1] + 1 + RING)
            sp.wait_ge(filled, 32)

        @block.gpsimd
        def _(pool):
            nc.gpsimd.memset(zeros[:], 0.0).then_inc(zero, 1)

        @block.tensor
        def _(pe):
            for u in range(len(units)):
                bank = ps[u // 4 % 2 * 4:u // 4 % 2 * 4 + 4]
                if kinds[order[u // 4]][2]:
                    if u >= 8:
                        pe.wait_ge(ev, u - 7)
                    parts.pe_T(pe, u, bank[u % 4][:])
                else:
                    if u >= 8 and u % 4 == 0:
                        pe.wait_ge(ev, u - 4)
                    parts.pe_rows(pe, u, bank, u % 4 * 2)

        @block.vector
        def _(dve):
            parts.dve_w(dve, 0)
            parts.dve_h(dve)
            for u in range(1, len(units)):
                parts.dve_w(dve, u)

        @block.scalar
        def _(act):
            parts.act_w(act, 0)
            parts.act_h(act)
            for u in range(len(units)):
                parts.act_w(act, u + 1)
                dst, func, tiled = kinds[order[u // 4]]
                for i in [u] if tiled else range(u - 3, u + 1) if u % 4 == 3 else []:
                    act.wait_ge(parts.used, u + 1)
                    nc.scalar.activation(dst[:, i % 4, :], ps[i % 8][:], func).then_inc(ev, 1)


def stage_gmlp(b):
    nc, a = b.nc, b.a
    DG = CH // GM_GROUPS
    u, v = b.gu, b.gv
    lnrow = b.scr[:, 0:2 * U].rearrange("p (i n) -> p i n", i=2)
    wT = b.scr[:, 2 * U:4 * U].rearrange("p (g t) -> p g t", g=GM_GROUPS)
    w = b.w1flat[:, 0:2 * U].rearrange("p (g s) -> p g s", g=GM_GROUPS)
    sq = b.u_big[:, 0:4 * U].rearrange("p (t n) -> p t n", t=NT)
    st = b.small
    b.tri = b.sb("tri", [P, P])
    loads, pool, chain, squared, root, turned, wmask, normed, ready = (
        b.sem(f"gm_{n}") for n in ("loads", "pool", "chain", "sq", "root", "turn", "wmask", "normed", "ready"))
    with ExitStack() as ps_ctx:
        pw = [ps_ctx.enter_context(nc.psum_tensor(f"gm_w{i}", [P, CH], F32)) for i in range(2)]
        ps = [ps_ctx.enter_context(nc.psum_tensor(f"gm_ps{i}", [P, CH], F32)) for i in range(4)]
        block = ps_ctx.enter_context(nc.Block())

        @block.sync
        def _(sp):
            sp.dma_start(w, a["gm_w_sp_2"][0].rearrange("g t s -> t g s")).then_inc(loads, 16)
            for i, n in enumerate(("gm_ln_g_2", "gm_ln_b_2")):
                sp.dma_start(lnrow[:, i], a[n].partition_broadcast(P).rearrange("p o n -> p (o n)")).then_inc(loads, 16)

        @block.gpsimd
        def _(g):
            nc.gpsimd.memset(b.tri[:], 1.0).then_inc(pool, 1)
            g.wait_ge(pool, 1)
            nc.gpsimd.affine_select(out=b.tri[:], in_=b.tri[:], compare_op=ALU.is_ge, fill=0.0, base=0,
                                    pattern=[[1, P]], channel_multiplier=-1).then_inc(pool, 1)

        @block.tensor
        def _(pe):
            pe.wait_ge(loads, 48)
            for g in range(GM_GROUPS):
                mm = nc.tensor.transpose(pw[g // 4][:, g % 4 * P:g % 4 * P + P], w[:, g, :], b.ident[:])
            mm.then_inc(turned, 1)
            pe.wait_ge(wmask, 1)
            pe.wait_ge(normed, 1)
            for g in range(GM_GROUPS):
                o = ps[g // 2][:, g % 2 * 4 * DG:(g % 2 + 1) * 4 * DG].rearrange("p (c n) -> p c n", c=NT)
                mm = nc.tensor.matmul(o, wT[:, g, :], v[:, :, g * DG:(g + 1) * DG], start=True, stop=True)
                mm.then_inc(ready, 1)

        @block.scalar
        def _(act):
            act.wait_ge(chain, 6)
            for t in range(NT):
                last = nc.scalar.activation(sq[:, t, :], v[:, t, :], ACT.Square, accum_out=st[:, 8 + t:9 + t])
            last.then_inc(squared, 1)
            act.wait_ge(chain, 7)
            nc.scalar.activation(st[:, 8:12], st[:, 8:12], ACT.Sqrt).then_inc(root, 1)

        @block.vector
        def _(dve):
            n = [0]

            def link(ins):
                n[0] += 1
                ins.then_inc(chain, 1)
                dve.wait_ge(chain, n[0])

            link(nc.vector.tensor_reduce(st[:, 0:4], v, AX.X, ALU.add))
            link(nc.vector.tensor_scalar(st[:, 4:8], st[:, 0:4], 1.0 / CH, None, ALU.mult))
            for t in range(NT):
                link(nc.vector.tensor_scalar(v[:, t, :], v[:, t, :], st[:, 4 + t:5 + t], None, ALU.subtract))
            dve.wait_ge(squared, 1)
            link(nc.vector.tensor_scalar(st[:, 8:12], st[:, 8:12], 1.0 / CH, EPS, ALU.mult, ALU.add))
            dve.wait_ge(root, 1)
            link(nc.vector.reciprocal(st[:, 12:16], st[:, 8:12]))
            dve.wait_ge(loads, 48)
            for t in range(NT):
                last = nc.vector.scalar_tensor_tensor(out=v[:, t, :], in0=v[:, t, :], scalar=st[:, 12 + t:13 + t],
                                                      in1=lnrow[:, 0], op0=ALU.mult, op1=ALU.mult)
            link(last)
            nc.vector.tensor_tensor(v, v, lnrow[:, 1:2, :].to_broadcast([P, NT, CH]), ALU.add).then_inc(normed, 1)
            dve.wait_ge(turned, 1)
            dve.wait_ge(pool, 2)
            for i in range(2):
                last = nc.vector.tensor_tensor(wT[:, 4 * i:4 * i + 4, :], pw[i][:].rearrange("p (g t) -> p g t", g=4),
                                               b.tri[:].unsqueeze(1).to_broadcast([P, 4, P]), ALU.mult)
            last.then_inc(wmask, 1)
            for g in range(GM_GROUPS):
                dve.wait_ge(ready, g // 2 * 2 + 2)
                o = ps[g // 2][:, g % 2 * 4 * DG:(g % 2 + 1) * 4 * DG].rearrange("p (c n) -> p c n", c=NT)
                us = u[:, :, g * DG:(g + 1) * DG]
                bias = b.vcol[:, VAT["gm_b_sp_2"] + g:VAT["gm_b_sp_2"] + g + 1]
                nc.vector.scalar_tensor_tensor(out=us, in0=o, scalar=bias, in1=us, op0=ALU.add, op1=ALU.mult)


def stage_hgrn(b):
    nc = b.nc
    NCH = T // HG_CHUNK
    qT, fT, vrows, og = b.hqT, b.hfT, b.hi, b.hog

    def four(reg, u0):
        return reg[:, u0 * U:(u0 + 4) * U].rearrange("p (h t) -> p h t", h=4)
    kT, bT, eb = four(b.u_big, 0), four(b.u_big, 4), four(b.u_big, 8)
    kend, kinv = four(b.s_ab, 0), four(b.s_ab, 4)
    kerows = four(b.u_big, 0)
    attm = four(b.u_big, 4)
    state = [b.u_big[:, (8 + i) * U:(9 + i) * U] for i in range(4)] + [b.s_ab[:, (12 + i) * U:(13 + i) * U] for i in range(4)]
    reset = b.u_big[:, 12 * U:13 * U]
    st = b.small
    lb, omlb, e0, e1, dec = st[:, 0:4], st[:, 4:8], st[:, 8:12], st[:, 12:16], st[:, 16:48].rearrange("p (h c) -> p h c", h=4)
    ss = b.rows2[:].rearrange("p a h b -> p (a h b)")[:, 0:16]
    bmask = b.sb("hg_mask", [P, P], I32)
    bmf = b.scr[:, 0:P]
    sqj = b.scr[:, U:2 * U]
    sem = {n: b.sem(f"hg_{n}") for n in ("pool", "lb", "chain", "f", "ln", "b", "eb", "enb", "kd", "kde", "turn", "ev",
                                         "att", "attm", "ds", "s", "o", "sq", "var", "root", "act", "zero", "y", "bm")}
    l0 = b.vcol[:, VAT["hg_lb_param_2"]:VAT["hg_lb_param_2"] + 4]
    l1 = b.vcol[:, VAT["hg_lb_param_2"] + 4:VAT["hg_lb_param_2"] + 8]

    def per_chunk(x, h=None):
        return x.rearrange("p h (c t) -> p h c t", c=NCH) if h is None else x[:, h, :].rearrange("p (c t) -> p c t", c=NCH)

    with ExitStack() as ps_ctx:
        ps = [ps_ctx.enter_context(nc.psum_tensor(f"hg_ps{i}", [P, CH], F32)) for i in range(8)]
        block = ps_ctx.enter_context(nc.Block())

        @block.gpsimd
        def _(g):
            nc.gpsimd.memset(bmf, 1.0).then_inc(sem["pool"], 1)
            g.wait_ge(sem["pool"], 1)
            nc.gpsimd.affine_select(out=bmf, in_=bmf, compare_op=ALU.is_ge, fill=0.0, base=0,
                                    pattern=[[1, P]], channel_multiplier=-1).then_inc(sem["pool"], 1)
            g.wait_ge(sem["pool"], 2)
            nc.gpsimd.memset(bmf[0:64, 64:128], 0.0).then_inc(sem["pool"], 1)
            g.wait_ge(sem["pool"], 3)
            nc.gpsimd.tensor_copy(bmask[:], bmf).then_inc(sem["bm"], 1)

        @block.vector
        def _(dve):
            n = [0]

            def link(ins, by="chain"):
                n[0] += 1
                ins.then_inc(sem["chain"], 1)
                dve.wait_ge(sem["chain"], n[0])

            nc.vector.memset(reset, 1.0).then_inc(sem["zero"], 1)
            dve.wait_ge(sem["zero"], 1)
            link(nc.vector.memset(reset.rearrange("p (c t) -> p c t", c=NCH)[:, :, 0:1], 0.0))
            link(nc.vector.tensor_tensor(lb, l0, l1, ALU.max))
            link(nc.vector.tensor_tensor(e0, l0, lb, ALU.subtract))
            nc.vector.tensor_tensor(e1, l1, lb, ALU.subtract).then_inc(sem["lb"], 1)
            dve.wait_ge(sem["act"], 1)
            link(nc.vector.tensor_tensor(e1, e0, e1, ALU.add))
            link(nc.vector.reciprocal(e1, e1))
            link(nc.vector.tensor_tensor(lb, e0, e1, ALU.mult))
            link(nc.vector.tensor_scalar(omlb, lb, -1.0, 1.0, ALU.mult, ALU.add))
            for h in range(HG_HEADS):
                nc.vector.tensor_scalar(fT[:, h, :], fT[:, h, :], omlb[:, h:h + 1], lb[:, h:h + 1], ALU.mult, ALU.add).then_inc(sem["f"], 1)
            dve.wait_ge(sem["f"], 4)
            nc.vector.tensor_scalar(kT, fT, -1.0, 1.0, ALU.mult, ALU.add).then_inc(sem["kd"], 1)
            for h in range(HG_HEADS):
                dve.wait_ge(sem["ln"], h + 1)
                nc.vector.tensor_tensor_scan(out=bT[:, h, :], data0=reset, data1=fT[:, h, :], initial=0.0,
                                             op0=ALU.mult, op1=ALU.add).then_inc(sem["b"], 1)
            dve.wait_ge(sem["b"], 4)
            for h in range(HG_HEADS):
                bc = per_chunk(bT, h)
                nc.vector.tensor_tensor(per_chunk(fT, h), bc[:, :, HG_CHUNK - 1:HG_CHUNK].to_broadcast([P, NCH, HG_CHUNK]), bc,
                                        ALU.subtract).then_inc(sem["kde"], 1)
            dve.wait_ge(sem["eb"], 1)
            nc.vector.tensor_tensor(qT, qT, eb, ALU.mult)
            nc.vector.tensor_copy(dec, eb.rearrange("p h (c t) -> p h c t", c=NCH)[:, :, :, HG_CHUNK - 1]).then_inc(sem["kd"], 1)
            dve.wait_ge(sem["enb"], 1)
            nc.vector.tensor_tensor(kinv, kinv, kT, ALU.mult).then_inc(sem["kd"], 1)
            dve.wait_ge(sem["enb"], 2)
            nc.vector.tensor_tensor(kend, fT, kT, ALU.mult).then_inc(sem["kd"], 1)
            link(nc.vector.memset(attm, 0.0))
            for t in range(NT):
                dve.wait_ge(sem["turn"], t + 1)
                nc.vector.tensor_copy(kerows[:, t, :], ps[t][:]).then_inc(sem["ev"], 1)
            dve.wait_ge(sem["bm"], 1)
            for t in range(NT):
                dve.wait_ge(sem["att"], t + 1)
                for h in range(HG_HEADS):
                    last = nc.vector.copy_predicated(attm[:, t, h * P:h * P + P], bmask[:], ps[4 + t][:, h * P:h * P + P])
                last.then_inc(sem["attm"], 1)
            for c in range(NCH - 1):
                dve.wait_ge(sem["ds"], c + 1)
                if c == 0:
                    last = nc.vector.tensor_copy(state[0], ps[0][:])
                else:
                    dve.wait_ge(sem["s"], c)
                    for h in range(HG_HEADS):
                        r = slice(h * P, h * P + P)
                        last = nc.vector.scalar_tensor_tensor(out=state[c][:, r], in0=state[c - 1][:, r], scalar=dec[:, h, c:c + 1],
                                                              in1=ps[c % 2][:, r], op0=ALU.mult, op1=ALU.add)
                last.then_inc(sem["s"], 1)
            dve.wait_ge(sem["sq"], 4)
            link(nc.vector.tensor_scalar(ss, ss, 1.0 / P, EPS, ALU.mult, ALU.add))
            nc.vector.sem_inc(sem["var"], 1)
            dve.wait_ge(sem["root"], 1)
            link(nc.vector.reciprocal(ss, ss))
            for t in range(NT):
                for h in range(HG_HEADS):
                    r = slice(h * P, h * P + P)
                    nc.vector.scalar_tensor_tensor(out=og[:, t, r], in0=ps[(2, 3, 4, 5)[t]][:, r], scalar=ss[:, 4 * t + h:4 * t + h + 1],
                                                   in1=og[:, t, r], op0=ALU.mult, op1=ALU.mult)

        @block.scalar
        def _(act):
            act.wait_ge(sem["lb"], 1)
            nc.scalar.preload_act_table_set("natural_log_exp_and_others")
            nc.scalar.activation(st[:, 8:16], st[:, 8:16], ACT.Exp).then_inc(sem["act"], 1)
            act.wait_ge(sem["kd"], 1)
            for h in range(HG_HEADS):
                nc.scalar.activation(fT[:, h, :], fT[:, h, :], ACT.Ln).then_inc(sem["ln"], 1)
            act.wait_ge(sem["b"], 4)
            nc.scalar.activation(eb, bT, ACT.Exp).then_inc(sem["eb"], 1)
            nc.scalar.activation(kinv, bT, ACT.Exp, scale=-1.0).then_inc(sem["enb"], 1)
            act.wait_ge(sem["kde"], 4)
            nc.scalar.activation(fT, fT, ACT.Exp).then_inc(sem["enb"], 1)
            for t in range(NT):
                act.wait_ge(sem["o"], t + 1)
                if t:
                    act.wait_ge(sem["sq"], t)
                for h in range(HG_HEADS):
                    r = slice(h * P, h * P + P)
                    last = nc.scalar.activation(sqj[:, r], ps[(2, 3, 4, 5)[t]][:, r], ACT.Square, accum_out=ss[:, 4 * t + h:4 * t + h + 1])
                last.then_inc(sem["sq"], 1)
            act.wait_ge(sem["var"], 1)
            nc.scalar.activation(ss, ss, ACT.Sqrt).then_inc(sem["root"], 1)

        @block.tensor
        def _(pe):
            pe.wait_ge(sem["kd"], 4)
            for t in range(NT):
                for h in range(HG_HEADS):
                    mm = nc.tensor.transpose(ps[t][:, h * P:h * P + P], kend[:, h, t * P:t * P + P], b.ident[:])
                mm.then_inc(sem["turn"], 1)
            for t in range(NT):
                for h in range(HG_HEADS):
                    r = slice(t * P, t * P + P)
                    mm = nc.tensor.matmul(ps[4 + t][:, h * P:h * P + P], kinv[:, h, r], qT[:, h, r], start=True, stop=True)
                mm.then_inc(sem["att"], 1)
            pe.wait_ge(sem["ev"], 4)
            for c in range(NCH - 1):
                r = slice(64 * (c % 2), 64 * (c % 2) + 64)
                if c >= 2:
                    pe.wait_ge(sem["s"], c - 1)
                for h in range(HG_HEADS):
                    k = slice(h * P, h * P + P)
                    mm = nc.tensor.matmul(ps[c % 2][:, k], kerows[r, c // 2, k], vrows[r, c // 2, k], start=True, stop=True)
                mm.then_inc(sem["ds"], 1)
            pe.wait_ge(sem["attm"], 4)
            pe.wait_ge(sem["s"], NCH - 1)
            for t in range(NT):
                bank = ps[(2, 3, 4, 5)[t]]
                for h in range(HG_HEADS):
                    k = slice(h * P, h * P + P)
                    for j in range(2):
                        c, o = 2 * t + j, bank[64 * j:64 * j + 64, k]
                        if c:
                            nc.tensor.matmul(o, qT[:, h, c * HG_CHUNK:(c + 1) * HG_CHUNK], state[c - 1][:, k], start=True, stop=False)
                        mm = nc.tensor.matmul(o, attm[:, t, h * P + 64 * j:h * P + 64 * j + 64], vrows[:, t, k],
                                              start=(c == 0), stop=True)
                mm.then_inc(sem["o"], 1)


def stage_router(b):
    nc, a = b.nc, b.a
    at = [0]

    def take(*shape):
        n = int(np.prod(shape))
        v = b.u_big[:, at[0]:at[0] + n]
        at[0] += n
        if len(shape) == 2:
            v = v.rearrange("p (a b) -> p a b", a=shape[0])
        return v
    b.slot = b.sb("slot", [P, 2 * NT], U32)
    b.weight = b.sb("weight", [P, 2 * NT])
    b.tok = b.sb("tok", [P, SLOTS // P], U32)
    b.spill = b.sb("spill", [P, SPILL + 1], I32)
    b.tok_dram = nc.dram_tensor("tok_list", (SLOTS, 1), F32).ap()
    b.wfull = [b.sem(f"ex_w{i}") for i in range(6)]
    expert_buffers(b)
    NE = EGROUPS + EXPERTS
    io32, lg, tg, ohg = take(EXPERTS), take(NT, NE), take(NT, EGROUPS), take(NT, EGROUPS)
    eg, sel, oh1, oh2, m, tt = take(NT, EGROUPS), *(take(NT, EXPERTS) for _ in range(5))
    rank, over, cnt, X, Xi, A, B, tokid = take(NT, EXPERTS), take(NT, EXPERTS), *(take(EXPERTS) for _ in range(5)), take(NT)
    (mg, pg, m1, m2, e2, r2, s1), slotf = (take(NT) for _ in range(7)), take(2 * NT)
    before = take(P)
    spf, cmp_ = take(SPILL), take(SPILL, EXPERTS)
    io16 = take(SPILL)
    zeros = take(P)
    toks = take(P)
    pool = b.sem("ro_pool")
    logits, chain, expin, expd, ranks, masks, slots_, scat, back, zero, turned = (
        b.sem(f"ro_{n}") for n in ("logits", "chain", "expin", "expd", "ranks", "masks", "slots", "scat", "back",
                                   "zero", "turned"))
    with ExitStack() as ps_ctx:
        ps_l, ps_r, ps_t = (ps_ctx.enter_context(nc.psum_tensor(f"ro_{n}", [P, CH], F32)) for n in "lrt")
        block = ps_ctx.enter_context(nc.Block())

        @block.sync
        def _(sp):
            sp.wait_ge(pool, 7)
            sp.dma_start(b.tok_dram.rearrange("(b s) o -> b (s o)", s=P), zeros[0:SLOTS // P, :]).then_inc(zero, 16)
            for j in range(2):
                if j == 1:
                    sp.wait_ge(logits, 1)
                for i, dram in enumerate(expert_weights(b, j)):
                    sp.dma_start(weight_views(b, j)[i], dram).then_inc(b.wfull[3 * j + i], 16)
            sp.wait_ge(b.rows_saved, 16)
            sp.wait_ge(scat, 16 * 2 * NT)
            sp.dma_start(toks[0:SLOTS // P, :], b.tok_dram.rearrange("(b s) o -> b (s o)", s=P)).then_inc(back, 16)

        @block.gpsimd
        def _(g):
            def iota(out, pattern, cm=0, base=0):
                nc.gpsimd.iota(out, pattern=pattern, base=base, channel_multiplier=cm,
                               allow_small_or_imprecise_dtypes=True).then_inc(pool, 1)
            iota(io32, [[1, EXPERTS]])
            iota(A, [[CAP, EXPERTS]])
            iota(tokid, [[P, NT]], cm=1)
            iota(io16, [[1, SPILL]])
            nc.gpsimd.memset(before, 1.0).then_inc(pool, 1)
            g.wait_ge(pool, 5)
            nc.gpsimd.affine_select(out=before, in_=before, compare_op=ALU.is_gt, fill=0.0, base=0,
                                    pattern=[[1, P]], channel_multiplier=-1).then_inc(pool, 1)
            nc.gpsimd.memset(zeros, 0.0).then_inc(pool, 1)
            g.wait_ge(slots_, 1)
            g.wait_ge(zero, 16)
            for i in range(2 * NT):
                nc.gpsimd.indirect_dma_start(b.tok_dram, bass.IndirectOffsetOnAxis(b.slot[:, i:i + 1], 0),
                                             tokid[:, i % NT:i % NT + 1], None).then_inc(scat, 16)

        @block.tensor
        def _(pe):
            pe.wait_ge(b.wr_in, 32)
            for t in range(NT):
                mm = product_rows(nc, ps_l[:, t * NE:(t + 1) * NE], b.hT, t, b.wr, KD)
            mm.then_inc(logits, 1)
            pe.wait_ge(pool, 7)
            pe.wait_ge(masks, 1)
            for t in range(NT):
                for u in range(t + 1):
                    mm = nc.tensor.matmul(ps_r[:, t * EXPERTS:(t + 1) * EXPERTS], before if u == t else b.ones[:], m[:, u, :],
                                          start=(u == 0), stop=(u == t))
            for u in range(NT):
                mm = nc.tensor.matmul(ps_r[:, NT * EXPERTS:(NT + 1) * EXPERTS], b.ones[:], m[:, u, :], start=(u == 0), stop=(u == NT - 1))
            mm.then_inc(ranks, 1)
            pe.wait_ge(back, 16)
            nc.tensor.transpose(ps_t[:, 0:SLOTS // P], toks[0:SLOTS // P, :], b.ident[0:SLOTS // P, 0:SLOTS // P]).then_inc(turned, 1)

        @block.scalar
        def _(act):
            act.wait_ge(expin, 1)
            nc.scalar.activation(eg, eg, ACT.Exp).then_inc(expd, 1)
            act.wait_ge(expin, 2)
            nc.scalar.activation(e2, e2, ACT.Exp).then_inc(expd, 1)

        @block.vector
        def _(dve):
            n = [0]

            def link(ins):
                n[0] += 1
                ins.then_inc(chain, 1)
                dve.wait_ge(chain, n[0])

            def wide(v, k):
                return v.unsqueeze(2).to_broadcast([P, NT, k])

            def first_max(values, k, best, onehot):
                link(nc.vector.tensor_reduce(best, values, AX.X, ALU.max))
                link(nc.vector.tensor_tensor(onehot, values, wide(best, k), ALU.is_ge))
                link(nc.vector.scalar_tensor_tensor(out=onehot, in0=onehot, scalar=-64.0, in1=io32[:, 0:k].unsqueeze(1).to_broadcast([P, NT, k]),
                                                    op0=ALU.mult, op1=ALU.add))
                link(nc.vector.tensor_reduce(s1, onehot, AX.X, ALU.min))
                link(nc.vector.tensor_tensor(onehot, onehot, wide(s1, k), ALU.is_equal))

            dve.wait_ge(pool, 7)
            dve.wait_ge(logits, 1)
            link(nc.vector.tensor_copy(lg, ps_l[:, 0:NT * NE].rearrange("p (t n) -> p t n", t=NT)))
            gl, el = lg[:, :, 0:EGROUPS], lg[:, :, EGROUPS:NE]
            first_max(gl, EGROUPS, mg, ohg)
            nc.vector.tensor_tensor(eg, gl, wide(mg, EGROUPS), ALU.subtract).then_inc(expin, 1)
            link(nc.vector.tensor_scalar(tg, ohg, 1.0, 1e30, ALU.subtract, ALU.mult))
            for t in range(NT):
                last = nc.vector.tensor_tensor(sel[:, t, :].rearrange("p (g e) -> p g e", g=EGROUPS), el[:, t, :].rearrange("p (g e) -> p g e", g=EGROUPS),
                                               tg[:, t, :].unsqueeze(2).to_broadcast([P, EGROUPS, EPG]), ALU.add)
            link(last)
            first_max(sel, EXPERTS, m1, oh1)
            link(nc.vector.scalar_tensor_tensor(out=sel, in0=oh1, scalar=-3e30, in1=sel, op0=ALU.mult, op1=ALU.add))
            first_max(sel, EXPERTS, m2, oh2)
            nc.vector.tensor_tensor(m, oh1, oh2, ALU.add).then_inc(masks, 1)
            nc.vector.tensor_tensor(e2, m2, m1, ALU.subtract).then_inc(expin, 1)
            dve.wait_ge(expd, 2)
            link(nc.vector.tensor_reduce(pg, eg, AX.X, ALU.add))
            link(nc.vector.tensor_scalar(r2, e2, 1.0, None, ALU.add))
            link(nc.vector.tensor_tensor(r2, r2, pg, ALU.mult))
            link(nc.vector.reciprocal(b.weight[:, 0:NT], r2))
            nc.vector.tensor_tensor(b.weight[:, NT:2 * NT], b.weight[:, 0:NT], e2, ALU.mult)
            dve.wait_ge(ranks, 1)
            nc.vector.tensor_copy(rank, ps_r[:, 0:NT * EXPERTS].rearrange("p (t n) -> p t n", t=NT))
            link(nc.vector.tensor_copy(cnt, ps_r[:, NT * EXPERTS:(NT + 1) * EXPERTS]))
            link(nc.vector.tensor_scalar(X, cnt, float(CAP), None, ALU.is_gt))
            for more in range(CAP + P, T, P):
                link(nc.vector.scalar_tensor_tensor(out=X, in0=cnt, scalar=float(more), in1=X, op0=ALU.is_gt, op1=ALU.add))
            link(nc.vector.tensor_tensor_scan(out=Xi, data0=X, data1=X, initial=0.0, op0=ALU.add, op1=ALU.bypass))
            link(nc.vector.tensor_tensor(B, Xi, X, ALU.subtract))
            link(nc.vector.tensor_scalar(B, B, float(P), float(PAIRS * P - CAP), ALU.mult, ALU.add))
            link(nc.vector.tensor_tensor(B, B, A, ALU.subtract))
            link(nc.vector.tensor_scalar(over, rank, float(CAP), None, ALU.is_ge))
            wideA, wideB = (v.unsqueeze(1).to_broadcast([P, NT, EXPERTS]) for v in (A, B))
            link(nc.vector.tensor_tensor(over, over, wideB, ALU.mult))
            link(nc.vector.tensor_tensor(over, over, rank, ALU.add))
            link(nc.vector.tensor_tensor(over, over, wideA, ALU.add))
            for k, oh in enumerate((oh1, oh2)):
                link(nc.vector.tensor_tensor(tt, oh, over, ALU.mult))
                link(nc.vector.tensor_reduce(slotf[:, k * NT:(k + 1) * NT], tt, AX.X, ALU.add))
            nc.vector.tensor_copy(b.slot[:], slotf).then_inc(slots_, 1)
            link(nc.vector.tensor_tensor(cmp_, Xi.unsqueeze(1).to_broadcast([P, SPILL, EXPERTS]),
                                         io16.unsqueeze(2).to_broadcast([P, SPILL, EXPERTS]), ALU.is_le))
            link(nc.vector.tensor_reduce(spf, cmp_, AX.X, ALU.add))
            link(nc.vector.tensor_scalar(spf, spf, float(EXPERTS - 1), None, ALU.min))
            nc.vector.tensor_copy(b.spill[:, 0:SPILL], spf)
            nc.vector.tensor_copy(b.spill[:, SPILL:SPILL + 1], Xi[:, EXPERTS - 1:EXPERTS])
            dve.wait_ge(turned, 1)
            nc.vector.tensor_copy(b.tok[:], ps_t[:, 0:SLOTS // P])


def expert_buffers(b):
    b.wslot = [b.ring[:, i] for i in range(RING)] + [b.reg_a[:], b.s_ab[:, 0:8 * U]]
    b.xg = b.s_ab[:, 8 * U:10 * U]
    b.xT = b.s_ab[:, 10 * U:12 * U].rearrange("p (k s) -> p k s", k=KD)
    b.hs, b.hm = b.s_ab[:, 12 * U:13 * U], b.s_ab[:, 13 * U:14 * U]
    b.ys = b.s_ab[:, 14 * U:18 * U].rearrange("p (j n) -> p j n", j=2)
    b.gcol = b.vcol[:, VAT["g_ffn_2"]:VAT["g_ffn_2"] + KD].unsqueeze(2).to_broadcast([P, KD, P])


def weight_views(b, j):
    w1, w3, w2 = b.wslot[3 * j:3 * j + 3]
    return (w1.rearrange("p (k n) -> p k n", k=KD), w3.rearrange("p (k n) -> p k n", k=KD), w2.rearrange("p (k n) -> p k n", k=KE))


def expert_weights(b, e):
    w1, w3, w2 = (b.a[n][0][bass.ds(e, 1)] for n in ("w1_2", "w3_2", "w2_2"))
    return (w1.rearrange("o (k p) n -> p (o k) n", p=P), w3.rearrange("o (k p) n -> p (o k) n", p=P),
            w2.rearrange("o (k p) n -> p (o k) n", p=P))


def turn_rows(nc, ps, xg, ident):
    for k in range(KD):
        mm = nc.tensor.transpose(ps[k // 4][:, k % 4 * P:k % 4 * P + P], xg[:, k * P:(k + 1) * P], ident)
    return mm


def rows_in(nc, b, ps):
    for i in range(2):
        last = nc.vector.tensor_tensor(b.xT[:, 4 * i:4 * i + 4, :], ps[i][:].rearrange("p (k s) -> p k s", k=4),
                                       b.gcol[:, 4 * i:4 * i + 4, :], ALU.mult)
    return last


def expert_in(nc, ps, w, xT, n):
    for i in range(2):
        for f in range(KE):
            for k in range(KD):
                mm = nc.tensor.matmul(ps[i][:, f * n:(f + 1) * n], w[i][:, k, f * P:f * P + P], xT[:, k, :],
                                      start=(k == 0), stop=(k == KD - 1))
    return mm


def expert_out(nc, ps, w2, hm, n):
    for h in range(2):
        for f in range(KE):
            mm = nc.tensor.matmul(ps[h][0:n, :], hm[:, f * n:(f + 1) * n], w2[:, f, h * CH:(h + 1) * CH],
                                  start=(f == 0), stop=(f == KE - 1))
    return mm


def stage_experts(b):
    nc = b.nc
    wfull = b.wfull
    yout = [b.sem(f"ex_out{i}") for i in range(2)]
    xfull, turned, xt, h_done, silu, hm_full, hm_hi, hm, w_hi, w_lo, w_used, y0, y1 = (
        b.sem(f"ex_{n}") for n in ("x", "turn", "xt", "h", "silu", "hmfull", "hmhi", "hm", "whi", "wlo", "wused", "y0", "y1"))
    half = [slice(j * KE * CAP, (j + 1) * KE * CAP) for j in range(2)]
    last = PAIRS - 1
    with b.parts_area(), ExitStack() as ps_ctx:
        w2p = [b.parts(f"ex_w2{i}", [P, KE, D]) for i in range(2)]
        hmp = [b.parts(f"ex_hm{i}", [P, 2 * KE * CAP]) for i in range(2)]
        ps_x, ps_h1, ps_h3, ps_y = ([ps_ctx.enter_context(nc.psum_tensor(f"ex_{n}{i}", [P, CH], F32)) for i in range(2)]
                                    for n in ("x", "h1", "h3", "y"))
        block = ps_ctx.enter_context(nc.Block())

        @block.sync
        def _(sp):
            def load(s, j):
                for i, dram in enumerate(expert_weights(b, 2 * s + j)):
                    if i == 0:
                        sp.wait_ge(h_done, 2 * s + j - 1)
                    if i == 2:
                        sp.wait_ge(w_lo, KE * (2 * s + j - 1))
                    sp.dma_start(weight_views(b, j)[i], dram).then_inc(wfull[3 * j + i], 16)
            with sp.Fori(1, PAIRS) as s:
                load(s, 0)
                load(s, 1)

        @block.gpsimd
        def _(pool):
            for s in range(PAIRS):
                if s:
                    pool.wait_ge(turned, s)
                nc.gpsimd.indirect_dma_start(b.xg, None, b.rows_dram, bass.IndirectOffsetOnAxis(b.tok[:, s:s + 1], 0)).then_inc(xfull, 16)

        @block.tensor
        def _(pe):
            def turn(s):
                pe.wait_ge(xfull, 16 * (s + 1))
                turn_rows(nc, ps_x, b.xg, b.ident[:]).then_inc(turned, 1)

            def inputs(s, j):
                if j == 0:
                    pe.wait_ge(xt, s + 1)
                for i in range(2):
                    pe.wait_ge(wfull[3 * j + i], 16 * (s + 1))
                expert_in(nc, (ps_h1[j], ps_h3[j]), weight_views(b, j), b.xT[:, :, j * CAP:(j + 1) * CAP], CAP).then_inc(h_done, 1)

            def outputs(s, j):
                pe.wait_ge(hm, 2 * s + j + 1)
                pe.wait_ge(y0, 2 * s + j)
                pe.wait_ge(y1, 2 * s + j)
                for f in range(KE):
                    pe.wait_ge(w_lo, KE * (2 * s + j) + f + 1)
                    hcols = slice(half[j].start + f * CAP, half[j].start + (f + 1) * CAP)
                    for h in range(2):
                        mm = product_parts(nc, ps_y[h][0:CAP, :], [x[:, hcols] for x in hmp],
                                           [w[:, f, h * CH:(h + 1) * CH] for w in w2p], f == 0, f == KE - 1)
                    mm.then_inc(w_used, 1)

            turn(0)
            inputs(0, 0)
            inputs(0, 1)
            turn(1)
            outputs(0, 0)
            with pe.Fori(1, last) as s:
                inputs(s, 0)
                outputs(s - 1, 1)
                inputs(s, 1)
                turn(s + 1)
                outputs(s, 0)
            inputs(last, 0)
            outputs(last - 1, 1)
            inputs(last, 1)
            outputs(last, 0)
            outputs(last, 1)

        @block.vector
        def _(dve):
            def x_in(s, again=True):
                dve.wait_ge(turned, s + 1)
                if again:
                    dve.wait_ge(h_done, 2 * s)
                rows_in(nc, b, ps_x).then_inc(xt, 1)

            def product(s, j, again=True):
                dve.wait_ge(silu, 2 * s + j + 1)
                if again:
                    dve.wait_ge(w_used, KE * (2 * s + j - 1))
                hi, lo = (x[:, half[j]] for x in hmp)
                nc.vector.tensor_tensor(b.hm[:, half[j]], b.hs[:, half[j]], ps_h3[j][:, 0:KE * CAP], ALU.mult).then_inc(hm_full, 1)
                dve.wait_ge(hm_full, 2 * s + j + 1)
                nc.vector.tensor_copy(hi, b.hm[:, half[j]]).then_inc(hm_hi, 1)
                dve.wait_ge(hm_hi, 2 * s + j + 1)
                lower(nc, lo, b.hm[:, half[j]], hi).then_inc(hm, 1)

            def split(s, j):
                for f in range(KE):
                    dve.wait_ge(w_hi, KE * (2 * s + j) + f + 1)
                    lower(nc, w2p[1][:, f, :], weight_views(b, j)[2][:, f, :], w2p[0][:, f, :]).then_inc(w_lo, 1)

            def y_half(s, j):
                dve.wait_ge(w_used, KE * (2 * s + j + 1))
                dve.wait_ge(yout[j], 16 * (s + 1))
                nc.vector.tensor_copy(b.ys[0:CAP, j, 0:CH], ps_y[0][0:CAP, :]).then_inc(y0, 1)

            x_in(0, False)
            split(0, 0)
            product(0, 0, False)
            product(0, 1, False)
            x_in(1)
            y_half(0, 0)
            split(0, 1)
            with dve.Fori(1, last) as s:
                product(s, 0)
                y_half(s - 1, 1)
                split(s, 0)
                product(s, 1)
                x_in(s + 1)
                y_half(s, 0)
                split(s, 1)
            product(last, 0)
            y_half(last - 1, 1)
            split(last, 0)
            product(last, 1)
            y_half(last, 0)
            split(last, 1)
            y_half(last, 1)

        @block.scalar
        def _(act):
            def gate(s, j, again=True):
                act.wait_ge(h_done, 2 * s + j + 1)
                if again:
                    act.wait_ge(hm, 2 * s + j - 1)
                nc.scalar.activation(b.hs[:, half[j]], ps_h1[j][:, 0:KE * CAP], ACT.Silu).then_inc(silu, 1)

            def split(s, j, again=True):
                act.wait_ge(wfull[3 * j + 2], 16 * (s + 1))
                for f in range(KE):
                    if again:
                        act.wait_ge(w_used, KE * (2 * s + j - 1) + f + 1)
                    nc.scalar.copy(w2p[0][:, f, :], weight_views(b, j)[2][:, f, :]).then_inc(w_hi, 1)

            def y_half(s, j):
                act.wait_ge(w_used, KE * (2 * s + j + 1))
                act.wait_ge(yout[j], 16 * (s + 1))
                nc.scalar.copy(b.ys[0:CAP, j, CH:2 * CH], ps_y[1][0:CAP, :]).then_inc(y1, 1)
                act.wait_ge(y0, 2 * s + j + 1)
                act.wait_ge(y1, 2 * s + j + 1)
                act.dma_start(b.y_dram[bass.ds((2 * s + j) * CAP, CAP), :], b.ys[0:CAP, j, :]).then_inc(yout[j], 16)

            for j in range(2):
                nc.scalar.sem_inc(yout[j], 16)
            split(0, 0, False)
            gate(0, 0, False)
            gate(0, 1, False)
            y_half(0, 0)
            split(0, 1)
            with act.Fori(1, last) as s:
                gate(s, 0)
                y_half(s - 1, 1)
                split(s, 0)
                gate(s, 1)
                y_half(s, 0)
                split(s, 1)
            gate(last, 0)
            y_half(last - 1, 1)
            split(last, 0)
            gate(last, 1)
            y_half(last, 0)
            split(last, 1)
            y_half(last, 1)
            for j in range(2):
                act.wait_ge(yout[j], 16 * (PAIRS + 1))


def stage_spill(b):
    nc = b.nc
    wfull, idx, go, xfull, turned, xt, h_done, silu, hm, y_done, ysb, yout = (
        b.sem(f"sp_{n}") for n in ("w", "idx", "go", "x", "turn", "xt", "h", "silu", "hm", "y", "ysb", "out"))
    stage = b.sb("spill_idx", [P, 1], U32)
    with ExitStack() as ps_ctx:
        ps_x, ps_h, ps_y = ([ps_ctx.enter_context(nc.psum_tensor(f"sp_{n}{i}", [P, CH], F32)) for i in range(2)] for n in "xhy")
        block = ps_ctx.enter_context(nc.Block())

        def each(eng, body):
            n = eng.value_load(b.spill[0:1, SPILL:SPILL + 1], min_val=0, max_val=SPILL)
            with eng.If(n > 0):
                with eng.Fori(0, n) as j:
                    body(j)

        @block.sync
        def _(sp):
            def body(j):
                sp.wait_ge(yout, 16 * (j + 1))
                e = sp.value_load(b.spill[0:1, bass.ds(j, 1)], min_val=0, max_val=EXPERTS - 1)
                for w, dram in zip(weight_views(b, 0), expert_weights(b, e)):
                    sp.dma_start(w, dram).then_inc(wfull, 16)
            each(sp, body)

        @block.gpsimd
        def _(pool):
            def body(j):
                pool.wait_ge(yout, 16 * (j + 1))
                nc.gpsimd.tensor_copy(stage[:], b.tok[:, bass.ds(j + PAIRS, 1)]).then_inc(idx, 1)
                pool.wait_ge(idx, j + 1)
                nc.gpsimd.sem_inc(go, 1)
                nc.gpsimd.indirect_dma_start(b.xg, None, b.rows_dram, bass.IndirectOffsetOnAxis(stage[:], 0)).then_inc(xfull, 16)
            each(pool, body)

        @block.tensor
        def _(pe):
            def body(j):
                pe.wait_ge(xfull, 16 * (j + 1))
                turn_rows(nc, ps_x, b.xg, b.ident[:]).then_inc(turned, 1)
                pe.wait_ge(xt, j + 1)
                pe.wait_ge(wfull, 48 * (j + 1))
                expert_in(nc, ps_h, weight_views(b, 0), b.xT, P).then_inc(h_done, 1)
                pe.wait_ge(hm, j + 1)
                expert_out(nc, ps_y, weight_views(b, 0)[2], b.hm, P).then_inc(y_done, 1)
            each(pe, body)

        @block.vector
        def _(dve):
            def body(j):
                dve.wait_ge(turned, j + 1)
                rows_in(nc, b, ps_x).then_inc(xt, 1)
                dve.wait_ge(silu, j + 1)
                nc.vector.tensor_tensor(b.hm, b.hs, ps_h[1][:], ALU.mult).then_inc(hm, 1)
                dve.wait_ge(y_done, j + 1)
                for h in range(2):
                    last = nc.vector.tensor_copy(b.ys[:, 0, h * CH:(h + 1) * CH], ps_y[h][:])
                last.then_inc(ysb, 1)
                dve.wait_ge(yout, 16 * (j + 2))
            each(dve, body)

        @block.scalar
        def _(act):
            def body(j):
                act.wait_ge(h_done, j + 1)
                nc.scalar.activation(b.hs, ps_h[0][:], ACT.Silu).then_inc(silu, 1)
                act.wait_ge(ysb, j + 1)
                act.dma_start(b.y_dram[bass.ds((j + PAIRS) * P, P), :], b.ys[:, 0, :]).then_inc(yout, 16)
                act.wait_ge(yout, 16 * (j + 2))
            nc.scalar.sem_inc(yout, 16)
            each(act, body)


def stage_combine(b):
    nc, a = b.nc, b.a
    b.pg = b.ring[:, 0:2].rearrange("p i n -> p (i n)").rearrange("p (k n) -> p k n", k=KD)
    b.ple = b.ring[:, 2, 0:2 * D].rearrange("p (k n) -> p k n", k=2)
    b.prow = b.ring[:, 2, 2 * D:2 * D + 4 * 256].rearrange("p (t n) -> p t n", t=NT)
    b.frow = b.ring[:, 3, 0:D]
    b.last_in = b.sem("last_in")
    rows, done = [b.sem(f"co_rows{i}") for i in range(2 * NT)], b.sem("co_done")
    ybuf = b.s_ab[:, 8 * U:24 * U].rearrange("p (i n) -> p i n", i=2 * NT)
    with nc.Block() as block:
        @block.sync
        def _(sp):
            for rows_in_ in rows:
                sp.wait_ge(rows_in_, 16)
            sp.dma_start(b.pg, feature_tiles(a["w_pg_2"][0], 0, D)).then_inc(b.last_in, 16)
            sp.dma_start(b.ple, feature_tiles(a["w_ple_2"][0], 0, D)).then_inc(b.last_in, 16)
            sp.dma_start(b.prow, a["p_2"][0, 0].rearrange("(t p) n -> p t n", p=P)).then_inc(b.last_in, 16)
            sp.dma_start(b.frow, a["g_final_2"].partition_broadcast(P)).then_inc(b.last_in, 16)

        @block.gpsimd
        def _(pool):
            for i in range(2 * NT):
                nc.gpsimd.indirect_dma_start(ybuf[:, i, :], None, b.y_dram, bass.IndirectOffsetOnAxis(b.slot[:, i:i + 1], 0)).then_inc(rows[i], 16)

        @block.vector
        def _(dve):
            for i in range(2 * NT):
                t = i % NT
                dve.wait_ge(rows[i], 16)
                if i >= NT:
                    dve.wait_ge(done, i - NT + 1)
                nc.vector.scalar_tensor_tensor(out=b.x[:, t, :], in0=ybuf[:, i, :], scalar=b.weight[:, i:i + 1], in1=b.x[:, t, :],
                                               op0=ALU.mult, op1=ALU.add).then_inc(done, 1)


def stage_embedding(b):
    nc = b.nc
    pT = b.s_ab[:, 0:2 * U].rearrange("p (k t) -> p k t", k=2)
    sg = b.s_ab[:, 4 * U:8 * U].rearrange("p (i n) -> p i n", i=4)
    turned, pt, ready, gate, prod, ev = (b.sem(f"em_{n}") for n in ("turn", "pt", "ready", "gate", "prod", "ev"))
    units = [(h, b.pg[:, k0:k0 + 2, h * CH:(h + 1) * CH], False) for h in range(2) for k0 in range(0, KD, 2)]
    with b.parts_area(), ExitStack() as ps_ctx:
        parts = Parts(b, "em", units, release=False, wait=lambda eng, _: eng.wait_ge(b.last_in, 64))
        ps_g, ps_p = ([ps_ctx.enter_context(nc.psum_tensor(f"em_{n}{i}", [P, CH], F32)) for i in range(4)] for n in "gp")
        block = ps_ctx.enter_context(nc.Block())

        @block.tensor
        def _(pe):
            pe.wait_ge(b.last_in, 64)
            for k in range(2):
                for t in range(NT):
                    mm = nc.tensor.transpose(ps_p[k][:, t * P:t * P + P], b.prow[:, t, k * P:k * P + P], b.ident[:])
            mm.then_inc(turned, 1)
            for h in range(2):
                if h:
                    pe.wait_ge(gate, NT)
                for i in range(4):
                    parts.pe_rows(pe, 4 * h + i, ps_g, 2 * i)
                if h == 0:
                    pe.wait_ge(pt, 1)
                for t in range(NT):
                    if h:
                        pe.wait_ge(ev, t + 1)
                    product_rows(nc, ps_p[t][:], pT, t, b.ple[:, :, h * CH:(h + 1) * CH], 2).then_inc(ready, 1)

        @block.scalar
        def _(act):
            parts.act_w(act, 0)
            parts.act_h(act)
            for u in range(len(units)):
                parts.act_w(act, u + 1)
                if u % 4 == 3:
                    act.wait_ge(parts.used, u + 1)
                    for t in range(NT):
                        if u > 4:
                            act.wait_ge(ev, t + 1)
                        nc.scalar.activation(sg[:, t], ps_g[t][:], ACT.Sigmoid).then_inc(gate, 1)

        @block.vector
        def _(dve):
            parts.dve_w(dve, 0)
            parts.dve_h(dve)
            dve.wait_ge(turned, 1)
            for k in range(2):
                last = nc.vector.tensor_copy(pT[:, k, :], ps_p[k][:])
            last.then_inc(pt, 1)
            for u in range(len(units)):
                parts.dve_w(dve, u + 1)
                for t in range(NT if u % 4 == 3 else 0):
                    i, h = u // 4 * NT + t, u // 4
                    xs = b.x[:, t, h * CH:(h + 1) * CH]
                    dve.wait_ge(gate, i + 1)
                    dve.wait_ge(ready, i + 1)
                    nc.vector.tensor_tensor(sg[:, t], sg[:, t], ps_p[t][:], ALU.mult).then_inc(prod, 1)
                    dve.wait_ge(prod, i + 1)
                    nc.vector.tensor_tensor(xs, xs, sg[:, t], ALU.add).then_inc(ev, 1)


def stage_final(b):
    nc = b.nc
    y = b.u_big[:, 0:NT * D].rearrange("p (t d) -> p t d", t=NT)
    ss = b.small[:, 0:4]
    sq, var, root, inv, done, stored = (b.sem(f"fi_{n}") for n in ("sq", "var", "root", "inv", "done", "stored"))
    with nc.Block() as block:
        @block.scalar
        def _(act):
            for t in range(NT):
                last = nc.scalar.activation(y[:, t, :], b.x[:, t, :], ACT.Square, accum_out=ss[:, t:t + 1])
            last.then_inc(sq, 1)
            act.wait_ge(var, 1)
            nc.scalar.activation(ss, ss, ACT.Sqrt).then_inc(root, 1)

        @block.vector
        def _(dve):
            dve.wait_ge(sq, 1)
            nc.vector.tensor_scalar(ss, ss, 1.0 / D, EPS, ALU.mult, ALU.add).then_inc(var, 1)
            dve.wait_ge(root, 1)
            nc.vector.reciprocal(ss, ss).then_inc(inv, 1)
            dve.wait_ge(inv, 1)
            for t in range(NT):
                nc.vector.scalar_tensor_tensor(out=y[:, t, :], in0=b.x[:, t, :], scalar=ss[:, t:t + 1], in1=b.frow,
                                               op0=ALU.mult, op1=ALU.mult).then_inc(done, 1)

        @block.sync
        def _(sp):
            for t in range(NT):
                sp.wait_ge(done, t + 1)
                sp.dma_start(b.out[0, t * P:(t + 1) * P, :], y[:, t, :]).then_inc(stored, 16)
            sp.wait_ge(stored, 16 * NT)


_INS = ["x", "c", "w_ada", "b_ada", "norm_mix_g", "w_in", "cmp_pos_k", "cmp_w1_k", "cmp_w2_k", "cmp_pos_v",
        "cmp_w1_v", "cmp_w2_v", "w_proj_a", "w_proj_b", "w_out", "norm_ffn_g", "w_ffn_gate", "w_ffn_up",
        "w_ffn_down", "norm_final_g", "p_2", "g_mix_2", "w_in_2", "gm_ln_g_2", "gm_ln_b_2", "gm_w_sp_2",
        "gm_b_sp_2", "w_up_a_2", "hg_lb_param_2", "hg_norm_g_2", "w_up_b_2", "w_out_2", "g_ffn_2", "w_grp_2",
        "w_exp_2", "w1_2", "w3_2", "w2_2", "g_ple_2", "w_pg_2", "w_ple_2", "g_final_2"]


def build(nc, a, out, stop=99):
    with ExitStack() as ctx:
        ctx.enter_context(nc.allow_non_contiguous_dma(reason="small vectors"))
        b = Build(nc, ctx, a, out)
        plan_weights(b)
        b.rows_dram = nc.dram_tensor("normed_rows", (T, D), F32).ap()
        b.h_back, b.h_saved = b.sem("h_back"), b.sem("h_saved")
        yT = [b.s_ab[:, i * 4 * U:(i + 1) * 4 * U].rearrange("p (k t) -> p k t", k=4) for i in range(2)]

        def work_u():
            return b.w1flat[:, 0:4 * U].rearrange("p (k t) -> p k t", k=4)
        mT = b.s_ab[:, 8 * U:16 * U].rearrange("p (k t) -> p k t", k=KD)
        guT = b.s_ab[:, 0:KF * T].rearrange("p (k t) -> p k t", k=KF)

        def vec(name, n=KD):
            return b.vcol[:, VAT[name]:VAT[name] + n]

        def block1_merge(b):
            b.take_x(b.reg_b)
            b.take_h(b.reg_a)
            stage_merge(b, "merge1", b.c_merge1, yT[0], yT[1], mT,
                        x_load=a["x"][0].rearrange("(t p) d -> p t d", p=P), h_wait=b.h_back)

        stages = [
            lambda: stage_constants(b),
            lambda: stage_modulation(b),
            lambda: stage_norm(b, "n1", b.mulcol[:, 0:KD], b.modcol[:, 0:KD], made=b.n1_rows, save=b.h_dram),
            lambda: stage_project1(b),
            lambda: stage_compress(b),
            lambda: stage_attention(b),
            lambda: stage_turn(b, "turn1", [(b.oa, yT[0], None), (b.ob, yT[1], None)], reload=True),
            lambda: block1_merge(b),
            lambda: stage_rows_out(b, "out1", mT, b.c_out1, b.g1row),
            b.fresh_sems,
            lambda: stage_norm(b, "n2", b.mulcol[:, KD:2 * KD], b.modcol[:, 2 * KD:3 * KD]),
            lambda: stage_ffn_up(b),
            lambda: stage_rows_out(b, "down", guT, b.c_down, b.g2row),
            b.fresh_sems,
            lambda: stage_norm(b, "n3", vec("g_mix_2"), None, residual_row="norm_final_g"),
            lambda: stage_project2(b),
            lambda: stage_gmlp(b),
            lambda: stage_turn(b, "turn2", [(b.gu, work_u(), None)]),
            lambda: stage_hgrn(b),
            lambda: stage_turn(b, "turn3", [(b.hog, yT[0], vec("hg_norm_g_2", 4))], move=(yT[1], work_u())),
            lambda: stage_merge(b, "merge2", b.c_merge2, yT[1], yT[0], mT),
            lambda: stage_rows_out(b, "out2", mT, b.c_out2),
            b.fresh_sems,
            lambda: stage_norm(b, "n4", vec("g_ffn_2"), None, rows_out=b.rows_dram),
            lambda: stage_router(b),
            lambda: stage_experts(b),
            lambda: stage_spill(b),
            lambda: stage_combine(b),
            lambda: stage_norm(b, "n5", vec("g_ple_2"), None),
            lambda: stage_embedding(b),
            lambda: stage_final(b),
        ]
        for s in stages[:stop]:
            s()
    return b


def kernel(**inputs):
    import concourse.bacc as bacc
    from concourse.bass_utils import run_bass_kernel_spmd

    nc = bacc.Bacc("TRN2", target_bir_lowering=False, num_devices=1)
    arrays, a = {}, {}
    for name in _INS:
        v = np.ascontiguousarray(inputs[name])
        arrays[f"in_{name}"] = v
        a[name] = nc.dram_tensor(f"in_{name}", v.shape, mybir.dt.from_np(v.dtype), kind="ExternalInput").ap()
    out = nc.dram_tensor("out", (1, T, D), F32, kind="ExternalOutput").ap()
    build(nc, a, out)
    r = run_bass_kernel_spmd(nc, [arrays], core_ids=[0])
    return r.results[0]["out"]
```
